# Optimizing a Trainium2 kernel written in Bass

```python
import math
import jax, jax.numpy as jnp
from jax import lax
import numpy as np

D_MODEL = 1024
BATCH = 1
SEQ = 128
DEPTH = 1
DEC_BATCH = 1
DEC_SEQ = 1024
PAST_LEN = 128

GRID_W = 64
GLA_HEADS = 4
GLA_DK = 64
GLA_DV = 128
GLA_CHUNK = 64
GATE_TAU = 16.0
LR_RANK = 16
FNO_GROUPS = 4
FNO_GROUP_W = 128
D_FF = 4 * D_MODEL
EPS = 1e-6
QK_W = GLA_HEADS * GLA_DK
V_W = GLA_HEADS * GLA_DV
FNO_W = FNO_GROUPS * FNO_GROUP_W
MIX_W = V_W + FNO_W
D_IN = 2 * QK_W + 2 * V_W + 2 * LR_RANK + FNO_W
SPLITS = [QK_W, 2 * QK_W, 2 * QK_W + V_W, 2 * QK_W + 2 * V_W,
          2 * QK_W + 2 * V_W + LR_RANK, 2 * QK_W + 2 * V_W + 2 * LR_RANK]

kernel_name = "hybrid_gla_fnet_diffusion_step"

def _rmsnorm(x, g):
    x32 = x.astype(jnp.float32)
    y = x32 * lax.rsqrt(jnp.mean(x32 * x32, axis=-1, keepdims=True) + EPS)
    return (y * g.astype(jnp.float32)).astype(x.dtype)

def _pos_emb_2d(n_tokens, dtype):
    rows = n_tokens // GRID_W
    t = jnp.arange(rows * GRID_W)
    r = (t // GRID_W).astype(jnp.float32)[:, None]
    col = (t % GRID_W).astype(jnp.float32)[:, None]
    nf = D_MODEL // 4
    omega = 1.0 / (10000.0 ** (jnp.arange(nf, dtype=jnp.float32) / nf))
    emb = jnp.concatenate([jnp.sin(r * omega), jnp.cos(r * omega),
                           jnp.sin(col * omega), jnp.cos(col * omega)], axis=-1)
    return emb.astype(dtype)

def _gla_chunked(q, k, v, log_a, s0):
    B, N, H, DK = q.shape
    DV = v.shape[-1]
    nc = N // GLA_CHUNK

    def to_chunks(a):
        d = a.shape[-1]
        return a.astype(jnp.float32).reshape(B, nc, GLA_CHUNK, H, d).transpose(1, 0, 3, 2, 4)

    qc, kc, vc, lac = to_chunks(q), to_chunks(k), to_chunks(v), to_chunks(log_a)
    causal = jnp.tril(jnp.ones((GLA_CHUNK, GLA_CHUNK), dtype=bool))[:, :, None]

    def step(S, inp):
        qi, ki, vi, lai = inp
        b = jnp.cumsum(lai, axis=2)
        inter = jnp.einsum('bhtd,bhde->bhte', qi * jnp.exp(b), S)
        diff = b[:, :, :, None, :] - b[:, :, None, :, :]
        decay = jnp.exp(jnp.where(causal, diff, -jnp.inf))
        A = jnp.einsum('bhtd,bhsd,bhtsd->bhts', qi, ki, decay)
        intra = jnp.einsum('bhts,bhse->bhte', A, vi)
        b_last = b[:, :, -1:, :]
        S_new = jnp.exp(b_last[:, :, 0, :])[..., None] * S + jnp.einsum(
            'bhsd,bhse->bhde', ki * jnp.exp(b_last - b), vi)
        return S_new, inter + intra

    S_fin, out = lax.scan(step, s0.astype(jnp.float32), (qc, kc, vc, lac))
    out = out.transpose(1, 0, 3, 2, 4).reshape(B, N, H, DV)
    return out.astype(q.dtype), S_fin

def _log_decay(lr, w_a2, b_a2):
    logits = jnp.einsum('bnr,rk->bnk', lr.astype(jnp.float32), w_a2.astype(jnp.float32)) + b_a2.astype(jnp.float32)
    return jax.nn.log_sigmoid(logits) / GATE_TAU

def _fourier_mix(u):
    B, N, _ = u.shape
    ug = u.astype(jnp.float32).reshape(B, N, FNO_GROUPS, FNO_GROUP_W)
    y = jnp.real(jnp.fft.fftn(ug, axes=(1, 3), norm="ortho"))
    return y.reshape(B, N, FNO_W).astype(u.dtype)

def _layer(x, mod, s0_fwd, s0_bwd, w_in, w_out, w_a2, b_a2, g_head,
           g_pre_mix, g_post_mix, g_pre_mlp, g_post_mlp, w_fc1, w_fc2):
    B, N, _ = x.shape
    sh_m, sc_m, gt_m, sh_f, sc_f, gt_f = jnp.split(mod.astype(x.dtype), 6, axis=-1)
    h = _rmsnorm(x, g_pre_mix) * (1 + sc_m) + sh_m
    z = h @ w_in
    q, k, v, g, lr_f, lr_b, u = jnp.split(z, SPLITS, axis=-1)
    q = q.reshape(B, N, GLA_HEADS, GLA_DK) * (GLA_DK ** -0.5)
    k = k.reshape(B, N, GLA_HEADS, GLA_DK)
    v = v.reshape(B, N, GLA_HEADS, GLA_DV)
    la_f = _log_decay(lr_f, w_a2[0], b_a2[0]).reshape(B, N, GLA_HEADS, GLA_DK)
    la_b = _log_decay(lr_b, w_a2[1], b_a2[1]).reshape(B, N, GLA_HEADS, GLA_DK)
    o_f, s_f = _gla_chunked(q, k, v, la_f, s0_fwd)
    flip = lambda a: jnp.flip(a, axis=1)
    o_b, s_b = _gla_chunked(flip(q), flip(k), flip(v), flip(la_b), s0_bwd)
    o = _rmsnorm(o_f + flip(o_b), g_head).reshape(B, N, V_W) * jax.nn.silu(g)
    y_fno = _fourier_mix(u)
    y = jnp.concatenate([o, y_fno], axis=-1) @ w_out
    x = x + gt_m * _rmsnorm(y, g_post_mix)
    h = _rmsnorm(x, g_pre_mlp) * (1 + sc_f) + sh_f
    f = jnp.square(jax.nn.relu(h @ w_fc1)) @ w_fc2
    x = x + gt_f * _rmsnorm(f, g_post_mlp)
    return x, s_f, s_b

def setup_inputs(seed: int = 0) -> dict:
    key = jax.random.key(seed)
    ks = jax.random.split(key, 20)
    f32 = jnp.float32
    nrm = lambda k, shape, s: (jax.random.normal(k, shape, f32) * s)
    st_shape = (DEC_BATCH, DEPTH, GLA_HEADS, GLA_DK, GLA_DV)
    return {
        "x_prompt": nrm(ks[0], (BATCH, SEQ, D_MODEL), 1.0),
        "x_sample": nrm(ks[1], (DEC_BATCH, DEC_SEQ, D_MODEL), 1.0),
        "state_gla_fwd": nrm(ks[2], st_shape, 1.0),
        "state_gla_bwd": nrm(ks[3], st_shape, 1.0),
        "c": nrm(ks[4], (DEC_BATCH, D_MODEL), 1.0),
        "c_ctx": nrm(ks[5], (D_MODEL,), 1.0),
        "w_in": nrm(ks[6], (DEPTH, D_MODEL, D_IN), D_MODEL ** -0.5),
        "w_out": nrm(ks[7], (DEPTH, MIX_W, D_MODEL), MIX_W ** -0.5),
        "w_a2": nrm(ks[8], (DEPTH, 2, LR_RANK, QK_W), LR_RANK ** -0.5),
        "b_a2": 1.0 + nrm(ks[9], (DEPTH, 2, QK_W), 0.5),
        "g_head": 1.0 + nrm(ks[10], (DEPTH, GLA_HEADS, GLA_DV), 0.02),
        "w_ada": nrm(ks[11], (DEPTH, D_MODEL, 6 * D_MODEL), 0.5 * D_MODEL ** -0.5),
        "b_ada": nrm(ks[12], (DEPTH, 6 * D_MODEL), 0.02),
        "g_pre_mix": 1.0 + nrm(ks[13], (DEPTH, D_MODEL), 0.02),
        "g_post_mix": 1.0 + nrm(ks[14], (DEPTH, D_MODEL), 0.02),
        "g_pre_mlp": 1.0 + nrm(ks[15], (DEPTH, D_MODEL), 0.02),
        "g_post_mlp": 1.0 + nrm(ks[16], (DEPTH, D_MODEL), 0.02),
        "w_fc1": nrm(ks[17], (DEPTH, D_MODEL, D_FF), D_MODEL ** -0.5),
        "w_fc2": nrm(ks[18], (DEPTH, D_FF, D_MODEL), D_FF ** -0.5),
    }

def reference(x_prompt, x_sample, state_gla_fwd, state_gla_bwd, c, c_ctx,
              w_in, w_out, w_a2, b_a2, g_head, w_ada, b_ada,
              g_pre_mix, g_post_mix, g_pre_mlp, g_post_mlp, w_fc1, w_fc2):
    ctx_mod = jnp.einsum('d,ldk->lk', jax.nn.silu(c_ctx), w_ada) + b_ada
    lat_mod = jnp.einsum('bd,ldk->lbk', jax.nn.silu(c), w_ada) + b_ada[:, None, :]

    bp = x_prompt.shape[0]
    zero_state = jnp.zeros((bp, GLA_HEADS, GLA_DK, GLA_DV), jnp.float32)
    xp = x_prompt
    fwd_states, bwd_states = [], []
    for l in range(DEPTH):
        xp, s_f, s_b = _layer(xp, ctx_mod[l][None, None, :], zero_state, zero_state,
                              w_in[l], w_out[l], w_a2[l], b_a2[l], g_head[l],
                              g_pre_mix[l], g_post_mix[l], g_pre_mlp[l], g_post_mlp[l],
                              w_fc1[l], w_fc2[l])
        fwd_states.append(s_f)
        bwd_states.append(s_b)
    new_state_fwd = jnp.stack(fwd_states, axis=1).astype(x_prompt.dtype)
    new_state_bwd = jnp.stack(bwd_states, axis=1).astype(x_prompt.dtype)

    xs = x_sample + _pos_emb_2d(x_sample.shape[1], x_sample.dtype)[None]
    for l in range(DEPTH):
        xs, _, _ = _layer(xs, lat_mod[l][:, None, :], state_gla_fwd[:, l], state_gla_bwd[:, l],
                          w_in[l], w_out[l], w_a2[l], b_a2[l], g_head[l],
                          g_pre_mix[l], g_post_mix[l], g_pre_mlp[l], g_post_mlp[l],
                          w_fc1[l], w_fc2[l])

    return (xp, xs, new_state_fwd, new_state_bwd)


_drawn_inputs = setup_inputs


def setup_inputs(seed=0):
    import zlib

    import numpy as np

    out = dict(_drawn_inputs(seed))
    spreads = {}
    factors = {'state_gla_fwd': 8.0,
     'state_gla_bwd': 8.0,
     'g_head': 8.0,
     'g_post_mix': 22.014,
     'g_pre_mlp': 90.578,
     'g_post_mlp': 114.994}
    for name, (base, spread) in spreads.items():
        noise = np.random.default_rng([zlib.crc32(name.encode()), seed]).standard_normal(out[name].shape)
        drawn = base * np.exp(spread * noise) if base else spread * noise
        out[name] = __import__('jax').numpy.asarray(drawn.astype(out[name].dtype))
    for name, factor in factors.items():
        out[name] = (out[name] * factor).astype(out[name].dtype)
    return out
```

```python
from contextlib import ExitStack

import concourse.bass as bass
from concourse import mybir

ALU = mybir.AluOpType
ACT = mybir.ActivationFunctionType
AX_X = mybir.AxisListType.X
F32 = mybir.dt.float32
F16 = mybir.dt.float16
RMAX = bass.bass_isa.ReduceOp.max

P = 128
D = 1024
KT = D // P
CTX = 128
LAT = 1024
TOK = CTX + LAT
NT = TOK // P
TB = 3
TBW = TOK // TB
HEADS, DK, DV = 4, 64, 128
HK = HEADS * DK // P
VW = HEADS * DV
RANK = 16
GROUPS = 4
FF = 4 * D
GFF = 512
NG = FF // GFF
FT = GFF // P
CW = 256
EPS = 1e-6
TAU = 16.0
CLAMP = 80.0 * TAU
NCOS, NSIN = 65, 63
FOLD = LAT // 2
TOP = 2.0 ** 15
TINY = 1e-30
F_ALPHA = 2.0 ** -28

Q0, K0, V0, G0 = 0, 256, 512, 1024
LR0 = 1536
U0 = LR0 + 2 * RANK
SH_M, SC_M, GT_M, SH_F, SC_F, GT_F = range(6)

C_ID, C_MASK, C_SEL2, C_SELB, C_CH, C_CTX, C_ALT = 0, 128, 384, 386, 642, 770, 1026
C_ALL = 1027
SMALL = 704
R_C, R_CTX, R_GPM, R_GPF, R_SHM, R_SCM, R_SHF, R_SCF, R_BA = 0, 8, 16, 24, 32, 40, 48, 56, 64
R_ALL = 68


class Ring:

    def __init__(self, banks, full, free, keys):
        self.banks, self.full, self.free, self.keys = banks, full, free, keys
        self.at = {k: i for i, k in enumerate(keys)}
        self.next = 0

    def spot(self, key, turns=0):
        i = self.at[key] if not isinstance(key, int) else key
        return i % len(self.banks), i // len(self.banks) + 1, turns

    def open(self, eng, key, turns=0):
        if not isinstance(key, int):
            assert self.at[key] == self.next, (key, self.keys[self.next])
            self.next += 1
        b, n, t = self.spot(key, turns)
        if n > 1:
            eng.wait_ge(self.free[b], n - 1 + t)
        return self.banks[b]

    def filled(self, key):
        return self.full[self.spot(key)[0]]

    def read(self, key):
        return self.free[self.spot(key)[0]]

    def take(self, eng, key, turns=0):
        b, n, t = self.spot(key, turns)
        eng.wait_ge(self.full[b], n + t)
        return self.banks[b]

    def wait_read(self, eng, key, turns=0):
        b, n, t = self.spot(key, turns)
        eng.wait_ge(self.free[b], n + t)


class Steps:

    def __init__(self, eng, sem):
        self.eng, self.sem, self.n = eng, sem, 0

    def did(self, ins):
        ins.then_inc(self.sem, 1)
        self.n += 1

    def settle(self):
        self.eng.wait_ge(self.sem, self.n)


def hybrid_step(nc, a):
    x_prompt, x_sample, w_in, w_out, w_ada, w_fc1, w_fc2 = (
        a[n] for n in ("x_prompt", "x_sample", "w_in", "w_out", "w_ada", "w_fc1", "w_fc2"))
    out_p, out_s, out_sf, out_sb = a["out_0"], a["out_1"], a["out_2"], a["out_3"]

    ada1 = [("ada", s, n) for s in (SH_M, SC_M) for n in range(D // CW)]
    zin = [("win", Q0, CW), ("win", K0, CW), ("win", LR0, 2 * RANK), ("win", U0, CW), ("win", U0 + CW, CW),
           ("win", V0, CW), ("win", V0 + CW, CW), ("win", G0, CW), ("win", G0 + CW, CW)]
    ada2 = [("ada", s, n) for s in (GT_M, SH_F, SC_F, GT_F) for n in range(D // CW)]
    wout = [("wout", part, n) for n in range(2) for part in (1, 0)]
    chunks = ada1 + zin + ada2 + wout
    splits = zin + wout
    ff_chunk = len(chunks)
    ff_split = len(splits)
    chunk_of = {c: i for i, c in enumerate(chunks)}
    split_of = {c: i for i, c in enumerate(splits)}

    def w1_split(g, x):
        return ff_split + x if g == 0 else ff_split + 4 * g - 2 + x

    TFORM = {0: "q", 1: "k", 2: "lr", 3: "u0", 4: "u1"}
    a_keys, b_keys = [], []
    a_keys.append("vec")
    for c in ada1:
        a_keys.append(c)
        b_keys.append(("mod", c))
    for j in range(NT):
        b_keys += [("xT", j, h) for h in range(2)]

    def z_uses(i):
        if i == 2:
            return [("z", i, 0, t) for t in range(TB)]
        if i in TFORM:
            return [("z", i, m, t) for t in range(TB) for m in range(2)]
        return [("z", i, 0, j) for j in range(NT)]

    for i in range(len(zin)):
        a_keys += z_uses(i)
    logit_keys = [("la", d, k, t) for k in range(HK) for d in range(2) for t in range(TB)]
    b_keys += logit_keys
    f_order = [0] + list(range(1, NT))
    b_order = [0] + list(range(NT - 1, 0, -1))
    for j in f_order[:-1]:
        for k in range(HK):
            b_keys.append(("kn", 0, j, k))
            a_keys.append(("U", 0, j, k))
    for i in range(4):
        a_keys.append(("dA", i))
    a_keys += [("dA", 4), ("dA", 5)]
    for i in range(-1, 4):
        a_keys += [("P", i), ("Q", i)]
        b_keys += [("Y1", i)] + ([("Y2", i)] if i >= 0 else [])
    a_keys.append(("P", 4))
    b_keys.append(("Y1", 4))

    def gla_scores(j):
        for h in range(HEADS):
            a_keys.append(("At", j, h))
        if j != 1:
            for k in range(HK):
                b_keys.append(("kn", 1, j, k))
                a_keys.append(("U", 1, j, k))

    gla_scores(b_order[0])
    for s, j in enumerate(b_order):
        if s + 1 < NT:
            gla_scores(b_order[s + 1])
        b_keys.append(("o", j))
        if s >= 1:
            b_keys.append(("oT", b_order[s - 1]))
    b_keys.append(("oT", b_order[-1]))
    for c in ada2:
        a_keys.append(c)
        b_keys.append(("mod", c))
    LAG2 = 6
    for i in range(4):
        for j in range(NT):
            a_keys.append(("wo", i, j))
            if i == 3 and j >= LAG2:
                b_keys += [("x2", j - LAG2, h) for h in range(2)]
    for j in range(NT - LAG2, NT):
        b_keys += [("x2", j, h) for h in range(2)]
    A0, B0 = len(a_keys), len(b_keys)
    UA, UB = 2 * TB * 2, 2 * NT
    w2_rel = {4 * g + 4 + n for g in range(NG - 1) for n in range(2)} | {4 * NG - 2, 4 * NG - 1}

    with ExitStack() as ctx:
        def sb(name, shape, dt=F32):
            return ctx.enter_context(nc.sbuf_tensor(name, shape, dt))

        def sem(name):
            return ctx.enter_context(nc.semaphore(name))

        banks = [ctx.enter_context(nc.psum_tensor(f"bank{i}", [P, 512], F32)) for i in range(8)]
        A = Ring(banks[0:4], [sem(f"a_full{i}") for i in range(4)], [sem(f"a_free{i}") for i in range(4)], a_keys)
        B = Ring(banks[4:7], [sem(f"b_full{i}") for i in range(3)], [sem(f"b_free{i}") for i in range(3)], b_keys)
        junk = banks[7]

        R1 = sb("region1", [P, 9216])
        R2 = sb("region2", [P, 9216])
        R34 = sb("region34", [P, 9216])
        R5 = sb("region5", [P, 4608])
        R7 = sb("region7", [P, 9216])
        stage = [sb(f"stage{i}", [P, 2048]) for i in range(2)]
        whi = [sb(f"whi{i}", [P, 2048], F16) for i in range(2)]
        wlo = [sb(f"wlo{i}", [P, 2048], F16) for i in range(2)]

        consts = sb("consts", [P, C_ALL])
        small = sb("small", [P, SMALL])
        vrow = sb("vrow", [P, P])
        ones = vrow[:]
        part = [sb(f"part{i}", [P, CW]) for i in range(2)]
        slq = sb("slq", [P, KT, 32])
        ghb = sb("ghb", [P, VW])

        ident = consts[:, C_ID:C_ID + P]
        masks = consts[:, C_MASK:C_MASK + 2 * P]
        sel2 = consts[:, C_SEL2:C_SEL2 + 2]
        selb = [consts[:, C_SELB + P * v:C_SELB + P * v + P] for v in range(2)]
        dft_ch = consts[:, C_CH:C_CH + P]
        dft_ctx = consts[:, C_CTX:C_CTX + 2 * P]
        alt_col = consts[:, C_ALT:C_ALT + 1]

        used = [0]

        def cols(n):
            used[0] += n
            assert used[0] <= SMALL
            return small[:, used[0] - n:used[0]]

        vT = cols(R_ALL)
        sil, sil2 = cols(16), cols(16)
        shf = [cols(16) for _ in range(2)]
        amul = [cols(16) for _ in range(2)]
        hmx = [cols(3) for _ in range(2)]
        hinv, hscl = ([cols(1) for _ in range(2)] for _ in range(2))
        neg = cols(5)
        ssq, sqs, rst = cols(2 * NT), cols(NT), cols(NT)
        wmax, wall, winv, wscl, wcof = (cols(8) for _ in range(5))
        fmx, frg, ftm, finv = (cols(2) for _ in range(4))
        beta = cols(4)
        ymx, yall, yinv, yscl = (cols(2) for _ in range(4))
        wexp = [cols(3 * NT) for _ in range(4)]
        oss, ors = cols(4 * NT), cols(4 * NT)
        pss, psm, prs = cols(2 * NT), cols(NT), cols(NT)
        qss, qsm, qrs = cols(2 * NT), cols(NT), cols(NT)
        fss, fsm, frs = cols(2 * NT), cols(NT), cols(NT)

        HTh = R1[:, 0:4608].bitcast(F16).rearrange("p (k t) -> p k t", k=KT)
        HTl = R1[:, 4608:9216].bitcast(F16).rearrange("p (k t) -> p k t", k=KT)
        YTh, YTl = HTh, HTl
        dftC = R1[:, 0:2048].rearrange("p (m n) -> p m n", m=4)
        dftS = R1[:, 2048:4096].rearrange("p (m n) -> p m n", m=4)
        AB = R1[:, 4096:6144].rearrange("p (m n) -> p m n", m=4)
        Y1b, Y2b, Qs = R1[:, 6144:6656], R1[:, 6656:7168], R1[:, 7168:7680]
        A512 = R1[0:1, 7680:7940]
        alt_row = R1[0:1, 7940:8452]
        kn = [R1[:, 8452:8580], R1[:, 8580:8708]]
        tU = [R1[:, 8708:8836], R1[:, 8836:8964]]
        ATb = R1[:, 0:1024].rearrange("p (b h t) -> p b h t", b=2, h=HEADS)
        Am = R1[:, 1024:2048].rearrange("p (h t) -> p h t", h=HEADS)
        Srb = R1[:, 4096:5632].rearrange("p (b k n) -> p b k n", b=3, k=HK)
        yo = R1[:, 3072:4096].rearrange("p (b n) -> p b n", b=2)

        qt = [[R2[:, 2304 * d + 1152 * k:2304 * d + 1152 * k + 1152] for k in range(HK)] for d in range(2)]
        kt_ = [[R2[:, 4608 + 2304 * d + 1152 * k:4608 + 2304 * d + 1152 * k + 1152] for k in range(HK)] for d in range(2)]
        x1 = R2[:].rearrange("p (j n) -> p j n", j=NT)

        qT = R34[:, 0:2304].rearrange("p (k t) -> p k t", k=HK)
        kT = R34[:, 2304:4608].rearrange("p (k t) -> p k t", k=HK)
        Srf = R34[:, 0:4096].rearrange("p (j k n) -> p j k n", j=NT - 1, k=HK)
        Sst = R34[:, 4096:4608].rearrange("p (d k n) -> p d k n", d=2, k=HK)
        gex = R34[:, 0:4608].rearrange("p (j n) -> p j n", j=NT)
        Sctx = [part[d][:].rearrange("p (k n) -> p k n", k=HK) for d in range(2)]
        vN = R34[:, 4608:9216].rearrange("p (j n) -> p j n", j=NT)
        xs = R34[:, 4608:6656].rearrange("p (b n) -> p b n", b=2)
        xh = R34[:, 6656:8704].rearrange("p (b n) -> p b n", b=2)
        bcast = R34[:, 0:4096].rearrange("p (b n) -> p b n", b=4)
        yN = R34[:].rearrange("p (j n) -> p j n", j=NT)
        FTh = [R34[:, 4608 * b:4608 * b + 2304].bitcast(F16).rearrange("p (f t) -> p f t", f=FT) for b in range(2)]
        FTl = [R34[:, 4608 * b + 2304:4608 * b + 4608].bitcast(F16).rearrange("p (f t) -> p f t", f=FT) for b in range(2)]

        gN = R5[:].rearrange("p (j n) -> p j n", j=NT)
        tmp = [R5[:, 1152 * i:1152 * i + 1152] for i in range(4)]
        posr = R5[:, 0:1024].rearrange("p (b n) -> p b n", b=2)
        posc = R5[:, 1024:1536]
        tb = [R5[:, 1536:2048], R5[:, 2048:2560]]
        gates = R5[:, 0:4096].rearrange("p (g v n) -> p g v n", g=2, v=2)
        tb2 = [R5[:, 4096:4608], ghb[:]]
        frel = R5[:, 0:768].rearrange("p (b n) -> p b n", b=2)
        fsq = R5[:, 768:1536].rearrange("p (b n) -> p b n", b=2)

        uT = R7[:, 0:4608].rearrange("p (g t) -> p g t", g=GROUPS)
        Ef = R7[:, 4608:4608 + 4 * (FOLD + 1)].rearrange("p (g t) -> p g t", g=GROUPS)
        Of = R7[:, 6660:6660 + 4 * FOLD].rearrange("p (g t) -> p g t", g=GROUPS)
        yT = R7[:].rearrange("p (k t) -> p k t", k=KT)
        HT2h = R7[:, 0:4608].bitcast(F16).rearrange("p (k t) -> p k t", k=KT)
        HT2l = R7[:, 4608:9216].bitcast(F16).rearrange("p (k t) -> p k t", k=KT)
        acc = R1[:].rearrange("p (j n) -> p j n", j=NT)

        lrS = R7[0:2 * RANK, 6660:6660 + TOK]
        wa2 = R7[0:2 * RANK, 4608:4608 + 512]

        s_2h = sem("h2_high")
        s_2l = sem("h2_low")
        s_2x = sem("x1_normed")
        s_accz = sem("ff_sums_zeroed")
        s_act = sem("act_steps")
        s_at = sem("scores_summed")
        s_bc = sem("gate_rows_loaded")
        s_beta = sem("ff_scale_set")
        s_const = sem("consts_loaded")
        s_de = sem("decay_exponents")
        s_dexp = sem("decay_exps")
        s_dft = sem("dft_loaded")
        s_dln = sem("decay_log1p")
        s_dve = sem("dve_steps")
        s_fh = sem("f_high")
        s_fl = sem("f_low")
        s_fold = sem("u_folded")
        s_fq = sem("f_squared")
        s_frs = sem("f_rstd")
        s_fss = sem("f_squares")
        s_ge = sem("gate_exp")
        s_gs = sem("gate_silu")
        s_hmx = sem("h_bound_parts")
        s_hsc = sem("h_scale_set")
        s_misc = sem("w_a2_g_head_loaded")
        s_ors = sem("o_rstd")
        s_oss = sem("o_squares")
        s_out = sem("outputs_stored")
        s_pool = sem("pool_steps")
        s_pos = [sem(f"pos{i}_loaded") for i in range(2)]
        s_posc = sem("pos_columns_loaded")
        s_posd = sem("pos_added")
        s_prs = sem("post_rstd")
        s_pss = sem("post_squares")
        s_qk = sem("decayed_q_k")
        s_qrs = sem("x1_rstd")
        s_qss = sem("x1_squares")
        s_rst = sem("x_rstd")
        s_sexp = sem("exp_c")
        s_slp = sem("silu_c_set")
        s_sout = sem("states_stored")
        s_srb = sem("bwd_state_blocks")
        s_srf = sem("fwd_state_blocks")
        s_ssq = sem("x_squares")
        s_stage = [sem(f"stage{i}_loaded") for i in range(2)]
        s_state = sem("states_loaded")
        s_th = sem("h_high")
        s_tl = sem("h_low")
        s_vec = sem("vectors_loaded")
        s_wa2 = sem("wa2_zeroed")
        s_whi = sem("chunk_high")
        s_wlo = sem("chunk_low")
        s_wmax = sem("chunk_max")
        s_wscl = sem("chunk_scale")
        s_x = [sem(f"x{i}_loaded") for i in range(2)]
        s_x1 = [sem(f"x1_{i}_loaded") for i in range(NT)]
        s_xh = sem("x_normed")
        s_xr = sem("x1_set")
        s_xst = [sem(f"x{i}_kept") for i in range(2)]
        s_y = sem("y_final")
        s_yh = sem("y_high")
        s_yl = sem("y_low")
        s_ymx = sem("y_max")
        s_ysc = sem("y_scale")
        s_zero = sem("silu_pad_zeroed")
        xkeep = nc.dram_tensor("x_with_position", [TOK, D], F32, kind="Internal").ap()

        def x_ready(eng, j):
            if j == 0:
                eng.wait_ge(s_x[0], 16)
            else:
                eng.wait_ge(s_posd, j)

        def x_src(j):
            return x_prompt[0] if j == 0 else x_sample[0, P * (j - 1):P * j, :]

        def stage_waits(eng, c):
            if c < 2:
                return
            old = chunks[c - 2] if c - 2 < ff_chunk else None
            if old is not None and old[0] == "ada":
                A.take(eng, old)
            else:
                n = split_of[old] + 1 if old is not None else c - 2 - ff_chunk + ff_split + 1
                eng.wait_ge(s_wlo, n)

        def chunk_src(ch):
            if ch[0] == "ada":
                c0 = D * ch[1] + CW * ch[2]
                return w_ada[0].rearrange("(k p) n -> p k n", p=P)[:, :, c0:c0 + CW], CW
            if ch[0] == "win":
                return w_in[0].rearrange("(k p) n -> p k n", p=P)[:, :, ch[1]:ch[1] + ch[2]], ch[2]
            rows = w_out[0, 512 * ch[1]:512 * ch[1] + 512, 512 * ch[2]:512 * ch[2] + 512]
            return rows.rearrange("(k p) n -> p k n", p=P), 512

        def staged(c, w):
            return stage[c % 2][:, 0:(2048 // (CW if w <= CW else 512)) * w].rearrange("p (k n) -> p k n", n=w)

        def load_chunk(eng, c):
            src, w = chunk_src(chunks[c])
            stage_waits(eng, c)
            eng.dma_start(staged(c, w), src).then_inc(s_stage[c % 2], 16)

        w1_v = w_fc1[0].rearrange("(k p) n -> p k n", p=P)
        w2_v = w_fc2[0].rearrange("(g k p) n -> g p k n", k=FT, p=P)

        def load_ff(eng, rel, src, t=0):
            c = ff_chunk + rel
            if rel < 2:
                stage_waits(eng, c)
            else:
                eng.wait_ge(s_wlo, ff_split + rel - 2 + 1 + 8 * t)
            w = src.shape[-1]
            eng.dma_start(stage[c % 2][:].rearrange("p (k n) -> p k n", n=w), src).then_inc(s_stage[c % 2], 16)

        def chunk_no(i):
            return chunk_of[splits[i]] if i < ff_split else ff_chunk + i - ff_split

        def wait_staged(eng, i, t=0):
            c = chunk_no(i)
            eng.wait_ge(s_stage[c % 2], 16 * (c // 2 + 1) + 64 * t)
            return stage[c % 2][:, 0:8 * splits[i][2]] if i < len(zin) else stage[c % 2][:]

        def pair(i):
            n = 8 * splits[i][2] if i < len(zin) else 2048
            w = splits[i][2] if i < len(zin) else (512 if i < ff_split or (i - ff_split) in w2_rel else CW)
            return [x[i % 2][:, 0:n].rearrange("p (k n) -> p k n", n=w) for x in (whi, wlo)]

        def last_use(i):
            if i < len(zin):
                return A, z_uses(i)[-1]
            if i < ff_split:
                return A, ("wo", i - len(zin), NT - 1)
            r = i - ff_split
            if r < 2:
                return A, A0 + 6 * r + 5
            if r >= 4 * NG - 2:
                return B, B0 + UB * (NG - 1) + NT * (r - 4 * NG + 2) + NT - 1
            g, x = (r - 2) // 4, (r - 2) % 4
            return (A, A0 + UA * (g + 1) + 6 * x + 5) if x < 2 else (B, B0 + UB * g + NT * (x - 2) + NT - 1)

        def wait_used(eng, i, t=0):
            ring, key = last_use(i)
            b, n, _ = ring.spot(key)
            eng.wait_ge(ring.full[b], n + (6 if ring is A else 12) * t)

        def chunk_max(dve, i, t=0):
            src = wait_staged(dve, i, t)
            nc.vector.tensor_reduce(wmax[:, i % 8:i % 8 + 1], src, AX_X, ALU.max, apply_absolute_value=True).then_inc(s_wmax, 1)

        def chunk_high(act, i, t=0):
            if i >= 2:
                wait_used(act, i - 2, 0 if i - ff_split == 3 else t)
            act.wait_ge(s_wscl, i + 1 + 8 * t)
            src = wait_staged(act, i, t)
            n = src.shape[-1]
            nc.scalar.activation(whi[i % 2][:, 0:n], src, ACT.Copy, scale=wscl[:, i % 8:i % 8 + 1]).then_inc(s_whi, 1)

        def chunk_low(dve, i, t=0):
            dve.wait_ge(s_whi, i + 1 + 8 * t)
            src = stage[chunk_no(i) % 2][:, 0:8 * splits[i][2] if i < len(zin) else 2048]
            n = src.shape[-1]
            nc.vector.scalar_tensor_tensor(out=wlo[i % 2][:, 0:n], in0=src, scalar=wscl[:, i % 8:i % 8 + 1],
                                           in1=whi[i % 2][:, 0:n], op0=ALU.mult, op1=ALU.subtract).then_inc(s_wlo, 1)

        block = ctx.enter_context(nc.Block())

        @block.sync
        def _(sp):
            sp.dma_start(consts[:], a["k_consts"]).then_inc(s_const, 16)
            for row, src in ((R_C, a["c"][0]), (R_CTX, a["c_ctx"]), (R_GPM, a["g_pre_mix"][0]), (R_GPF, a["g_pre_mlp"][0]),
                             (R_SHM, a["b_ada"][0, 0:D]), (R_SCM, a["b_ada"][0, D:2 * D]),
                             (R_SHF, a["b_ada"][0, SH_F * D:SH_F * D + D]), (R_SCF, a["b_ada"][0, SC_F * D:SC_F * D + D])):
                sp.dma_start(vrow[row:row + 8, :], src.rearrange("(k p) -> k p", p=P)).then_inc(s_vec, 16)
            sp.dma_start(vrow[R_BA:R_ALL, :], a["b_a2"][0].rearrange("d (k p) -> (d k) p", p=P)).then_inc(s_vec, 16)

            def load_x(j):
                sp.dma_start(xs[:, j % 2, :], x_src(j)).then_inc(s_x[j % 2], 16)

            def load_pos(j):
                rows = a["k_pos_row"][2 * (j - 1):2 * j, :]
                for r in range(2):
                    sp.dma_start(posr[64 * r:64 * r + 64, j % 2, :], rows[r, :].partition_broadcast(64)).then_inc(s_pos[j % 2], 16)

            load_chunk(sp, 0)
            load_x(0)
            load_x(1)
            sp.dma_start(posc, a["k_pos_col"]).then_inc(s_posc, 16)
            load_pos(1)
            load_pos(2)
            for c in range(1, len(ada1)):
                load_chunk(sp, c)
            sp.dma_start(ghb[:], a["g_head"][0].rearrange("h v -> (h v)").partition_broadcast(P)).then_inc(s_misc, 16)
            sp.wait_ge(s_wa2, 1)
            for d in range(2):
                sp.dma_start(wa2[RANK * d:RANK * d + RANK, 256 * d:256 * d + 256], a["w_a2"][0, d]).then_inc(s_misc, 16)
            for c in range(len(ada1), len(ada1) + 2):
                load_chunk(sp, c)
            for j in range(NT):
                x_ready(sp, j)
                sp.dma_start(xkeep[P * j:P * j + P, :], xs[:, j % 2, :]).then_inc(s_xst[j % 2], 16)
                if j + 2 < NT:
                    sp.wait_ge(s_xst[j % 2], 16 * (j // 2 + 1))
                    sp.wait_ge(s_xh, j + 1)
                    load_x(j + 2)
                if 1 <= j and j + 2 < NT:
                    load_pos(j + 2)
            for c in range(len(ada1) + 2, len(ada1) + len(zin)):
                load_chunk(sp, c)
            sp.wait_ge(s_gs, 6)
            for d, name in enumerate(("state_gla_fwd", "state_gla_bwd")):
                sp.dma_start(Sst[:, d], a[name][0, 0].rearrange("(k h) d v -> (h d) k v", k=HK)).then_inc(s_state, 16)
            A.take(sp, z_uses(len(zin) - 1)[-1])
            sp.dma_start(dftC, a["k_dft_cos"].rearrange("(m p) n -> p m n", p=P)).then_inc(s_dft, 16)
            sp.dma_start(dftS, a["k_dft_sin"].rearrange("(m p) n -> p m n", p=P)).then_inc(s_dft, 16)
            sp.dma_start(alt_row, a["k_alt"]).then_inc(s_dft, 16)
            for c in range(len(ada1) + len(zin), len(ada1) + len(zin) + 2):
                load_chunk(sp, c)
            for d, out in enumerate((out_sf, out_sb)):
                for k in range(HK):
                    A.wait_read(sp, ("U", d, 0, k))
                sp.dma_start(out[0, 0].rearrange("(k h) d v -> (h d) k v", k=HK), Sctx[d]).then_inc(s_sout, 16)
            B.take(sp, ("oT", b_order[-1]))
            for i, src in enumerate((a["b_ada"][0, GT_M * D:GT_M * D + D], a["g_post_mix"][0],
                                     a["b_ada"][0, GT_F * D:GT_F * D + D], a["g_post_mlp"][0])):
                sp.dma_start(bcast[:, i, :], src.partition_broadcast(P)).then_inc(s_bc, 16)
            for b in range(2):
                sp.wait_ge(s_xst[b], 16 * (5 - b))
            for j in range(NT):
                sp.dma_start(x1[:, j, :], xkeep[P * j:P * j + P, :]).then_inc(s_x1[j], 16)
            for c in range(len(ada1) + len(zin) + 2, ff_chunk):
                load_chunk(sp, c)
            load_ff(sp, 0, w1_v[:, :, 0:CW])
            load_ff(sp, 1, w1_v[:, :, CW:2 * CW])

            def group(g, t):
                for x in range(2):
                    load_ff(sp, 4 * g + 2 + x, w1_v[:, :, bass.ds(t * (2 * GFF) + GFF * (g + 1) + CW * x, CW)], t)
                for n in range(2):
                    down = w2_v[bass.ds(t * 2 + g, 1), :, :, 512 * n:512 * n + 512].rearrange("a p k n -> p (a k) n")
                    load_ff(sp, 4 * g + 4 + n, down, t)

            with sp.Fori(0, NG // 2 - 1) as t:
                group(0, t)
                group(1, t)
            group(NG - 2, 0)
            for n in range(2):
                load_ff(sp, 4 * NG - 2 + n, w2_v[NG - 1, :, :, 512 * n:512 * n + 512])
            for j in range(NT):
                sp.wait_ge(s_y, j + 1)
                sp.dma_start(out_p[0] if j == 0 else out_s[0, P * (j - 1):P * j, :], x1[:, j, :]).then_inc(s_out, 16)
            sp.wait_ge(s_sout, 32)
            sp.wait_ge(s_out, 16 * NT)

        @block.gpsimd
        def _(pool):
            own = Steps(pool, s_pool)
            nc.gpsimd.memset(slq[:], 0.0).then_inc(s_zero, 1)
            own.did(nc.gpsimd.memset(neg[:, 0:4], -0.5))
            own.did(nc.gpsimd.memset(neg[:, 4:5], -1.0))
            nc.gpsimd.memset(wa2, 0.0).then_inc(s_wa2, 1)
            own.settle()

            def power(out, src, exponent, done=None):
                ins = nc.gpsimd.tensor_tensor(out, src, exponent, ALU.pow)
                if done is not None:
                    ins.then_inc(done, 1)
                else:
                    own.did(ins)
                    own.settle()

            def step(ins):
                own.did(ins)
                own.settle()

            def h_scale(n):
                pool.wait_ge(s_hmx, 2 * (n + 1))
                step(nc.gpsimd.partition_all_reduce(hmx[n][:, 1:3], hmx[n][:, 1:3], P, RMAX))
                step(nc.gpsimd.tensor_tensor(hmx[n][:, 0:1], hmx[n][:, 1:2], hmx[n][:, 2:3], ALU.add))
                step(nc.gpsimd.tensor_scalar(hinv[n], hmx[n][:, 0:1], D ** 0.5 / TOP, TINY, ALU.mult, ALU.max))
                power(hscl[n], hinv[n], neg[:, 4:5], s_hsc)

            def chunk_inverse(i, t=0):
                c = slice(i % 8, i % 8 + 1)
                pool.wait_ge(s_wmax, i + 1 + 8 * t)
                step(nc.gpsimd.partition_all_reduce(wall[:, c], wmax[:, c], P, RMAX))
                step(nc.gpsimd.tensor_scalar(winv[:, c], wall[:, c], 1.0 / TOP, TINY, ALU.mult, ALU.max))

            def chunk_scale(i):
                c = slice(i % 8, i % 8 + 1)
                chunk_inverse(i)
                if i < len(zin):
                    other, factor = hinv[0], DK ** -0.5 if i == 0 else 1.0
                else:
                    half = wout[i - len(zin)][1]
                    other, factor = yinv[:, half:half + 1], 1.0
                step(nc.gpsimd.tensor_scalar(wcof[:, c], winv[:, c], other, factor, ALU.mult, ALU.mult))
                power(wscl[:, c], winv[:, c], neg[:, 4:5], s_wscl)

            def ff_up_scale(g, x, t=0):
                i = w1_split(g, x)
                c = slice(i % 8, i % 8 + 1)
                chunk_inverse(i, t)
                power(wscl[:, c], winv[:, c], neg[:, 4:5], s_wscl)
                if x == 1:
                    b = g % 2
                    first = w1_split(g, 0) % 8
                    p = slice(b, b + 1)
                    step(nc.gpsimd.tensor_scalar(fmx[:, p], winv[:, first:first + 1], winv[:, c], None, ALU.max))
                    power(frg[:, p], fmx[:, p], neg[:, 4:5])
                    step(nc.gpsimd.tensor_scalar(ftm[:, p], fmx[:, p], hinv[1], 1.0 / F_ALPHA, ALU.mult, ALU.mult))
                    step(nc.gpsimd.tensor_tensor(finv[:, p], ftm[:, p], ftm[:, p], ALU.mult))
                    step(nc.gpsimd.tensor_scalar(beta[:, 2 * b:2 * b + 1], winv[:, first:first + 1], frg[:, p], F_ALPHA,
                                                 ALU.mult, ALU.mult))
                    nc.gpsimd.tensor_scalar(beta[:, 2 * b + 1:2 * b + 2], winv[:, c], frg[:, p], F_ALPHA,
                                            ALU.mult, ALU.mult).then_inc(s_beta, 1)

            def ff_down_scale(i, g, t=0):
                c = slice(i % 8, i % 8 + 1)
                chunk_inverse(i, t)
                step(nc.gpsimd.tensor_tensor(wcof[:, c], winv[:, c], finv[:, g % 2:g % 2 + 1], ALU.mult))
                power(wscl[:, c], winv[:, c], neg[:, 4:5], s_wscl)

            def rstd(out, mean, sums, n, done):
                if sums.shape[-1] == 2 * out.shape[-1]:
                    step(nc.gpsimd.tensor_tensor(mean, sums[:, 0:1], sums[:, 1:2], ALU.add))
                    sums = mean
                step(nc.gpsimd.tensor_scalar(mean, sums, 1.0 / n, EPS, ALU.mult, ALU.add))
                power(out, mean, neg[:, 0:out.shape[-1]], done)

            def x_rstd(j):
                pool.wait_ge(s_ssq, 2 * (j + 1))
                rstd(rst[:, j:j + 1], sqs[:, j:j + 1], ssq[:, 2 * j:2 * j + 2], D, s_rst)

            x_rstd(0)
            x_rstd(1)
            h_scale(0)
            chunk_scale(0)
            chunk_scale(1)
            for j in range(2, NT):
                x_rstd(j)
            for i in range(2, len(zin)):
                chunk_scale(i)
            for s, j in enumerate(b_order):
                for h in range(HEADS):
                    A.wait_read(pool, ("At", j, h))
                    if s >= 2 and h == 0:
                        B.take(pool, ("o", b_order[s - 2]))
                    nc.gpsimd.tensor_tensor(ATb[:, s % 2, h, :], Am[:, h, 0:P], Am[:, h, P:2 * P], ALU.add).then_inc(s_at, 1)
                if s >= 1:
                    jj = b_order[s - 1]
                    pool.wait_ge(s_oss, HEADS * s)
                    rstd(ors[:, 4 * jj:4 * jj + 4], ors[:, 4 * jj:4 * jj + 4], oss[:, 4 * jj:4 * jj + 4], DV, s_ors)
            jj = b_order[-1]
            pool.wait_ge(s_oss, HEADS * NT)
            rstd(ors[:, 4 * jj:4 * jj + 4], ors[:, 4 * jj:4 * jj + 4], oss[:, 4 * jj:4 * jj + 4], DV, s_ors)
            for half in (1, 0):
                p = slice(half, half + 1)
                pool.wait_ge(s_ymx, 2 - half)
                step(nc.gpsimd.partition_all_reduce(yall[:, p], ymx[:, p], P, RMAX))
                step(nc.gpsimd.tensor_scalar(yinv[:, p], yall[:, p], 1.0 / TOP, TINY, ALU.mult, ALU.max))
                power(yscl[:, p], yinv[:, p], neg[:, 4:5], s_ysc)
            h_scale(1)
            for i in range(len(zin), ff_split):
                chunk_scale(i)
            ff_up_scale(0, 0)
            for s in range(NT + 2):
                if s < NT:
                    pool.wait_ge(s_pss, 2 * (s + 1))
                    rstd(prs[:, s:s + 1], psm[:, s:s + 1], pss[:, 2 * s:2 * s + 2], D, s_prs)
                if s >= 2:
                    j = s - 2
                    pool.wait_ge(s_qss, 2 * (j + 1))
                    rstd(qrs[:, j:j + 1], qsm[:, j:j + 1], qss[:, 2 * j:2 * j + 2], D, s_qrs)
            A.take(pool, ("wo", 3, NT - 1))
            nc.gpsimd.memset(acc, 0.0).then_inc(s_accz, 1)
            ff_up_scale(0, 1)
            ff_up_scale(1, 0)

            def group(g, t):
                ff_up_scale(g + 1, 1, t)
                for n in range(2):
                    ff_down_scale(ff_split + 4 * g + 4 + n, g, t)
                if g + 2 < NG:
                    ff_up_scale(g + 2, 0, t)

            for t in range(NG // 2 - 1):
                group(0, t)
                group(1, t)
            group(NG - 2, 0)
            for n in range(2):
                ff_down_scale(ff_split + 4 * NG - 2 + n, NG - 1)
            for j in range(NT):
                pool.wait_ge(s_fss, 2 * (j + 1))
                rstd(frs[:, j:j + 1], fsm[:, j:j + 1], fss[:, 2 * j:2 * j + 2], D, s_frs)

        @block.scalar
        def _(act):
            own = Steps(act, s_act)

            squared = {}
            last_squares = []

            def squares(src, out2, done, width=512):
                for h in range(src.shape[-1] // width):
                    if last_squares:
                        act.wait_ge(last_squares[-1], squared[last_squares[-1].name])
                    nc.scalar.activation(junk[:, 0:width], src[:, width * h:width * h + width], ACT.Square,
                                         accum_out=out2[:, h:h + 1]).then_inc(done, 1)
                    squared[done.name] = squared.get(done.name, 0) + 1
                    last_squares.append(done)

            A.wait_read(act, "vec")
            nc.scalar.activation(sil, vT[:, 0:16], ACT.Exp, scale=-1.0).then_inc(s_sexp, 1)

            def mod_part(n, c):
                bank = A.take(act, c)
                if n >= 2:
                    B.take(act, ("mod", mods[n - 2]))
                nc.scalar.activation(part[n % 2][:], bank[:, 0:CW], ACT.Copy).then_inc(A.read(c), 1)

            mods = ada1 + ada2

            def norm_x(j):
                act.wait_ge(s_rst, j + 1)
                if j >= 2:
                    B.take(act, ("xT", j - 2, 1))
                nc.scalar.activation(xh[:, j % 2, :], xs[:, j % 2, :], ACT.Copy, scale=rst[:, j:j + 1]).then_inc(s_xh, 1)

            def square_x(j):
                x_ready(act, j)
                squares(xs[:, j % 2, :], ssq[:, 2 * j:2 * j + 2], s_ssq)

            for j in range(2):
                square_x(j)
                norm_x(j)
            for n, c in enumerate(ada1):
                mod_part(n, c)
            chunk_high(act, 0)

            def high_x(j, h):
                key = ("xT", j, h)
                B.wait_read(act, key)
                nc.scalar.activation(HTh[:, 4 * h:4 * h + 4, P * j:P * j + P], tb[h].rearrange("p (k t) -> p k t", k=4),
                                     ACT.Copy).then_inc(s_th, 1)

            for j in range(NT):
                if j + 2 < NT:
                    square_x(j + 2)
                high_x(j, 0)
                high_x(j, 1)
                if j + 2 < NT:
                    norm_x(j + 2)

            def take_z(key):
                return A.take(act, key)

            def evac_t(i, dst):
                for key in z_uses(i):
                    _, _, m, t = key
                    bank = take_z(key)
                    nc.scalar.activation(dst[:, m, TBW * t:TBW * t + TBW], bank[:, 0:TBW], ACT.Copy,
                                         scale=wcof[:, i % 8:i % 8 + 1]).then_inc(A.read(key), 1)

            def decay_logs(k):
                for d in range(2):
                    for t in range(TB):
                        B.wait_read(act, ("la", d, k, t))
                    own.did(nc.scalar.activation(tmp[2 * d + 1], tmp[2 * d], ACT.Abs))
                own.settle()
                for d in range(2):
                    own.did(nc.scalar.activation(tmp[2 * d + 1], tmp[2 * d + 1], ACT.Exp, scale=-1.0))
                own.settle()
                for d in range(2):
                    nc.scalar.activation(tmp[2 * d + 1], tmp[2 * d + 1], ACT.Ln, bias=1.0).then_inc(s_dln, 1)

            def decay_exps(k):
                for d in range(2):
                    act.wait_ge(s_de, 2 * k + d + 1)
                    own.did(nc.scalar.activation(wexp[2 * d + k], wexp[2 * d + k], ACT.Exp, scale=1.0 / TAU))
                    nc.scalar.activation(tmp[2 * d + 1], tmp[2 * d], ACT.Exp, scale=1.0 / TAU).then_inc(s_dexp, 1)
                    act.wait_ge(s_dexp, 4 * k + 2 * d + 1)
                    nc.scalar.activation(tmp[2 * d], tmp[2 * d], ACT.Exp, scale=-1.0 / TAU).then_inc(s_dexp, 1)

            for i in range(len(zin)):
                if i + 1 < ff_split and i + 1 < len(zin):
                    chunk_high(act, i + 1)
                if i == 0:
                    evac_t(i, qT)
                elif i == 1:
                    evac_t(i, kT)
                elif i == 2:
                    for key in z_uses(i):
                        bank = take_z(key)
                        t = key[3]
                        nc.scalar.activation(lrS[:, TBW * t:TBW * t + TBW], bank[0:2 * RANK, 0:TBW], ACT.Copy,
                                             scale=wcof[0:2 * RANK, i % 8:i % 8 + 1]).then_inc(A.read(key), 1)
                elif i <= 4:
                    evac_t(i, uT[:, 2 * (i - 3):2 * (i - 3) + 2, :])
                    if i == 4:
                        decay_logs(0)
                        decay_exps(0)
                elif i <= 6:
                    for key in z_uses(i):
                        bank = take_z(key)
                        nc.scalar.activation(vN[:, key[3], CW * (i - 5):CW * (i - 5) + CW], bank[:, 0:CW], ACT.Copy,
                                             scale=wcof[:, i % 8:i % 8 + 1]).then_inc(A.read(key), 1)
                    if i == 6:
                        decay_logs(1)
                        decay_exps(1)
                else:
                    act.wait_ge(s_qk, 8)
                    x = i - 7
                    for key in z_uses(i):
                        bank = take_z(key)
                        j = key[3]
                        nc.scalar.activation(gN[:, j, CW * x:CW * x + CW], bank[:, 0:CW], ACT.Copy,
                                             scale=wcof[:, i % 8:i % 8 + 1]).then_inc(A.read(key), 1)
                        A.wait_read(act, key)
                        nc.scalar.activation(gex[:, j, CW * x:CW * x + CW], gN[:, j, CW * x:CW * x + CW], ACT.Exp,
                                             scale=-1.0).then_inc(s_ge, 1)

            def copy_kn(n, key, ukeys):
                bank = B.take(act, key)
                if n >= 2:
                    A.take(act, ukeys[n - 2])
                nc.scalar.activation(kn[n % 2], bank[:, 0:P], ACT.Copy).then_inc(B.read(key), 1)

            kn_keys = [k for k in b_keys if k[0] == "kn"]
            u_keys = [k for k in a_keys if k[0] == "U"]
            n_fwd = HK * (NT - 1)
            for n in range(n_fwd):
                copy_kn(n, kn_keys[n], u_keys)

            for i in range(4):
                bank = A.take(act, ("dA", i))
                nc.scalar.activation(AB[:, i, :], bank[:], ACT.Copy).then_inc(A.read(("dA", i)), 1)
            bank = A.take(act, ("dA", 4))
            nc.scalar.activation(A512, bank[0:1, 0:4 * NCOS], ACT.Copy).then_inc(A.read(("dA", 4)), 1)
            bank = A.take(act, ("dA", 5))
            nc.scalar.activation(Y2b, bank[:], ACT.Copy).then_inc(A.read(("dA", 5)), 1)

            def put_y(i):
                bank = B.take(act, ("Y1", i))
                c0 = 0 if i < 0 else CTX + P * i
                nc.scalar.activation(yT[:, 4:8, c0:c0 + P], bank[:].rearrange("p (g t) -> p g t", g=GROUPS),
                                     ACT.Copy).then_inc(B.read(("Y1", i)), 1)
                if i < 0:
                    return
                bank = B.take(act, ("Y2", i))
                first = 1 if i == 0 else 0
                c1 = CTX + LAT - P * i - first
                nc.scalar.activation(yT[:, 4:8, c1:c1 - (P - first):-1],
                                     bank[:].rearrange("p (g t) -> p g t", g=GROUPS)[:, :, first:P],
                                     ACT.Copy).then_inc(B.read(("Y2", i)), 1)

            for i in range(-1, 4):
                bank = A.take(act, ("Q", i))
                if i >= 0:
                    A.wait_read(act, ("P", i - 1))
                nc.scalar.activation(Qs[:, 0:4 * NSIN], bank[:, 0:4 * NSIN], ACT.Copy).then_inc(A.read(("Q", i)), 1)
                if i >= 0:
                    put_y(i - 1)
            put_y(3)
            bank = B.take(act, ("Y1", 4))
            nc.scalar.activation(yT[:, 4:8, CTX + FOLD:CTX + FOLD + 1], bank[:, 0:4].rearrange("p (g t) -> p g t", g=GROUPS),
                                 ACT.Copy).then_inc(B.read(("Y1", 4)), 1)

            n = [n_fwd]

            def scores(j):
                if j != 1:
                    for k in range(HK):
                        copy_kn(n[0], kn_keys[n[0]], u_keys)
                        n[0] += 1

            def put_o(j):
                bank = B.take(act, ("oT", j))
                nc.scalar.activation(yT[:, 0:4, P * j:P * j + P], bank[:].rearrange("p (g t) -> p g t", g=HEADS),
                                     ACT.Copy).then_inc(B.read(("oT", j)), 1)

            scores(b_order[0])
            for s, j in enumerate(b_order):
                if s + 1 < NT:
                    scores(b_order[s + 1])
                bank = B.take(act, ("o", j))
                squares(bank[:], oss[:, 4 * j:4 * j + 4], s_oss, DV)
                if s >= 1:
                    put_o(b_order[s - 1])
            put_o(b_order[-1])

            def high_y(half, j):
                act.wait_ge(s_ysc, 2 - half)
                nc.scalar.activation(YTh[:, 4 * half:4 * half + 4, P * j:P * j + P], yT[:, 4 * half:4 * half + 4, P * j:P * j + P],
                                     ACT.Copy, scale=yscl[:, half:half + 1]).then_inc(s_yh, 1)

            for nn, c in enumerate(ada2):
                if nn == 0:
                    act.wait_ge(s_sout, 32)
                mod_part(len(ada1) + nn, c)
                for r in range(2 * NT * nn // len(ada2), 2 * NT * (nn + 1) // len(ada2)):
                    high_y(1 - r // NT, r % NT)
            chunk_high(act, 9)
            chunk_high(act, 10)

            def post(j):
                A.wait_read(act, ("wo", 3, j))
                squares(yN[:, j, :], pss[:, 2 * j:2 * j + 2], s_pss)

            def post2(j):
                act.wait_ge(s_xr, j + 1)
                squares(x1[:, j, :], qss[:, 2 * j:2 * j + 2], s_qss)

            def post3(j):
                act.wait_ge(s_qrs, j + 1)
                nc.scalar.activation(yN[:, j, :], x1[:, j, :], ACT.Copy, scale=qrs[:, j:j + 1]).then_inc(s_2x, 1)

            def high_2(j):
                for h in range(2):
                    B.wait_read(act, ("x2", j, h))
                    nc.scalar.activation(HT2h[:, 4 * h:4 * h + 4, P * j:P * j + P],
                                         tb2[h].rearrange("p (k t) -> p k t", k=4), ACT.Copy).then_inc(s_2h, 1)

            chunk_high(act, 11)
            chunk_high(act, 12)
            chunk_high(act, ff_split)
            for s in range(NT + LAG2):
                for stage_of, lag in ((post, 0), (post2, 2), (post3, 3), (high_2, LAG2)):
                    if 0 <= s - lag < NT:
                        stage_of(s - lag)
            chunk_high(act, ff_split + 1)

            def up(g, x, t=0):
                for u in range(6):
                    r = 6 * x + u
                    tb_, m = u // 2, 2 * x + u % 2
                    n_ = 12 * g + r
                    key = A0 + UA * g + r
                    bank = A.take(act, key, 6 * t)
                    if r == 0:
                        act.wait_ge(s_beta, g + 1 + 2 * t)
                        if g >= 1:
                            B.take(act, B0 + UB * (g - 2) + UB - 1, 12 * t)
                    if n_ >= 2:
                        act.wait_ge(s_fq, n_ - 1 + 24 * t)
                        act.wait_ge(s_fh, n_ - 1 + 24 * t)
                    nc.scalar.activation(frel[:, n_ % 2, :], bank[:, 0:TBW], ACT.Relu,
                                         scale=beta[:, 2 * (g % 2) + x:2 * (g % 2) + x + 1]).then_inc(A.read(key), 1)
                    b, cnt, _ = A.spot(key)
                    act.wait_ge(A.free[b], cnt + 6 * t)
                    nc.scalar.activation(FTh[g % 2][:, m, TBW * tb_:TBW * tb_ + TBW], frel[:, n_ % 2, :],
                                         ACT.Square).then_inc(s_fh, 1)

            up(0, 0)
            chunk_high(act, ff_split + 2)
            up(0, 1)

            def group(g, t):
                for s in range(4):
                    if g == 0 and s == 0:
                        B.take(act, B0 - 1, 12 * t)
                    chunk_high(act, ff_split + 4 * g + 3 + s, t)
                    if s < 2:
                        up(g + 1, s, t)

            with act.Fori(0, NG // 2 - 1) as t:
                group(0, t)
                group(1, t)
            group(NG - 2, 0)
            chunk_high(act, ff_split + 4 * NG - 1)
            for j in range(NT):
                B.wait_read(act, B0 + UB * (NG - 1) + NT + j)
                squares(acc[:, j, :], fss[:, 2 * j:2 * j + 2], s_fss)

        @block.tensor
        def _(pe):
            def mm(out, lhsT, rhs, start, stop):
                return nc.tensor.matmul(out, lhsT, rhs, start=start, stop=stop, skip_group_check=True)

            def three(out, ks, lhs, rhs):
                (lh, ll), (rh, rl) = lhs, rhs
                terms = [(k, x) for k in ks for x in ((lh, rh), (lh, rl), (ll, rh))]
                for n, (k, (x, y)) in enumerate(terms):
                    ins = mm(out, x(k), y(k), n == 0, n == len(terms) - 1)
                return ins

            pe.wait_ge(s_const, 16)
            pe.wait_ge(s_vec, 16 * 9)
            bank = A.open(pe, "vec")
            nc.tensor.transpose(bank[:, 0:R_ALL], vrow[0:R_ALL, :], ident[0:R_ALL, 0:R_ALL]).then_inc(A.filled("vec"), 1)
            pe.wait_ge(s_slp, 1)
            mods = ada1 + ada2

            def mod_rows(c):
                g = chunk_of[c]
                pe.wait_ge(s_stage[g % 2], 16 * (g // 2 + 1))
                bank = A.open(pe, c)
                w = staged(g, CW)
                for k in range(KT):
                    r = 32 * (k % 4)
                    ins = nc.tensor.matmul(bank[r:r + 32, 0:CW], slq[:, k, :], w[:, k, :], start=k < 4, stop=k >= 4,
                                           tile_position=(0, r), skip_group_check=True)
                ins.then_inc(A.filled(c), 1)

            def mod_out(n, c):
                A.wait_read(pe, c)
                key = ("mod", c)
                bank = B.open(pe, key)
                if c[1] in (GT_M, GT_F):
                    for v in range(2):
                        ins = mm(bank[:, CW * v:CW * v + CW], selb[v], part[n % 2][:], True, True)
                else:
                    for m in range(2):
                        ins = mm(bank[:, 2 * m:2 * m + 2], part[n % 2][:, P * m:P * m + P], sel2, True, True)
                ins.then_inc(B.filled(key), 1)

            def modulation(first, cs):
                for n, c in enumerate(cs):
                    mod_rows(c)
                    if n >= 1:
                        mod_out(first + n - 1, cs[n - 1])
                mod_out(first + len(cs) - 1, cs[-1])

            modulation(0, ada1)

            def turn(key, src, ready):
                ready()
                bank = B.open(pe, key)
                for k in range(4):
                    ins = nc.tensor.transpose(bank[:, P * k:P * k + P], src[:, P * k:P * k + P], ident)
                ins.then_inc(B.filled(key), 1)

            for j in range(NT):
                for h in range(2):
                    turn(("xT", j, h), xh[:, j % 2, 512 * h:512 * h + 512], lambda: pe.wait_ge(s_xh, j + 1))

            def up_tile(ring_key, turns, i, m, t, Hh, Hl, mw=P):
                wh, wl = pair(i)
                bank = A.open(pe, ring_key, turns)
                toks = slice(TBW * t, TBW * t + TBW)
                return three(bank[0:mw, 0:TBW], range(KT),
                             (lambda k: wh[:, k, P * m:P * m + mw], lambda k: wl[:, k, P * m:P * m + mw]),
                             (lambda k: Hh[:, k, toks], lambda k: Hl[:, k, toks]))

            def row_tile(ring, ring_key, turns, i, j, ks, Hh, Hl, k0, w):
                wh, wl = pair(i)
                bank = ring.open(pe, ring_key, turns)
                toks = slice(P * j, P * j + P)
                return three(bank[:, 0:w], ks,
                             (lambda k: Hh[:, k0 + k, toks], lambda k: Hl[:, k0 + k, toks]),
                             (lambda k: wh[:, k, :], lambda k: wl[:, k, :]))

            def logits(k):
                pe.wait_ge(s_misc, 48)
                for t in range(TB):
                    A.wait_read(pe, ("z", 2, 0, t))
                for d in range(2):
                    for t in range(TB):
                        key = ("la", d, k, t)
                        bank = B.open(pe, key)
                        mm(bank[:, 0:TBW], wa2[:, 256 * d + P * k:256 * d + P * k + P], lrS[:, TBW * t:TBW * t + TBW],
                           True, True).then_inc(B.filled(key), 1)

            for i in range(len(zin)):
                pe.wait_ge(s_wlo, i + 1)
                for n, key in enumerate(z_uses(i)):
                    if i in TFORM:
                        _, _, m, t = key
                        if i == 0 and m == 0:
                            pe.wait_ge(s_tl, 6 * (t + 1))
                        ins = up_tile(key, 0, i, m, t, HTh, HTl, P if i != 2 else 2 * RANK)
                    else:
                        ins = row_tile(A, key, 0, i, key[3], range(KT), HTh, HTl, 0, CW)
                    ins.then_inc(A.filled(key), 1)
                if i == 3:
                    logits(0)
                if i == 5:
                    logits(1)

            def turn_k(d, j, k):
                key = ("kn", d, j, k)
                bank = B.open(pe, key)
                nc.tensor.transpose(bank[:, 0:P], kt_[d][k][:, P * j:P * j + P], ident).then_inc(B.filled(key), 1)

            def update(d, j, k):
                B.wait_read(pe, ("kn", d, j, k))
                key = ("U", d, j, k)
                n = u_keys.index(key)
                bank = A.open(pe, key)
                mm(bank[:, 0:2 * DV], kn[n % 2], vN[:, j, 2 * DV * k:2 * DV * k + 2 * DV], True, True).then_inc(A.filled(key), 1)

            u_keys = [k for k in a_keys if k[0] == "U"]
            A.wait_read(pe, z_uses(6)[-1])
            pe.wait_ge(s_qk, 8)
            for j in f_order[:-1]:
                for k in range(HK):
                    turn_k(0, j, k)
                for k in range(HK):
                    update(0, j, k)

            pe.wait_ge(s_fold, 1)
            cosw, sinw = dft_ch[:, 0:NCOS], dft_ch[:, NCOS:P]
            for i in range(6):
                key = ("dA", i)
                bank = A.open(pe, key)
                for g in range(GROUPS):
                    if i < 4:
                        e, o = Ef[:, g, P * i:P * i + P], Of[:, g, P * i:P * i + P]
                    elif i == 4:
                        e, o = Ef[:, g, FOLD:FOLD + 1], None
                    else:
                        e = o = uT[:, g, 0:CTX]
                    ins = mm(bank[0:e.shape[-1], NCOS * g:NCOS * g + NCOS], e, cosw, True, True)
                    if o is not None:
                        c0 = GROUPS * NCOS + NSIN * g
                        ins = mm(bank[:, c0:c0 + NSIN], o, sinw, True, True)
                ins.then_inc(A.filled(key), 1)
            NP_, NQ_ = GROUPS * NCOS, GROUPS * NSIN
            pe.wait_ge(s_dft, 48)
            for i in range(4):
                A.wait_read(pe, ("dA", i))
            A.wait_read(pe, ("dA", 4))
            A.wait_read(pe, ("dA", 5))

            def turn_y(i):
                for b, y in (("Y1", Y1b), ("Y2", Y2b)):
                    if b == "Y2" and i < 0:
                        continue
                    turn((b, i), y, lambda: A.wait_read(pe, ("P", i)))

            for i in range(-1, 4):
                P_, Q_ = ("P", i), ("Q", i)
                bank = A.open(pe, P_)
                if i < 0:
                    ins = mm(bank[:, 0:NP_], dft_ctx[:, 0:P], Y2b[:, 0:NP_], True, True)
                else:
                    for m in range(4):
                        mm(bank[:, 0:NP_], dftC[:, m, P * i:P * i + P], AB[:, m, 0:NP_], m == 0, False)
                    ins = mm(bank[:, 0:NP_], alt_row[:, P * i:P * i + P], A512, False, True)
                ins.then_inc(A.filled(P_), 1)
                bank = A.open(pe, Q_)
                if i < 0:
                    ins = mm(bank[:, 0:NQ_], dft_ctx[:, P:2 * P], Y2b[:, NP_:512], True, True)
                else:
                    for m in range(4):
                        ins = mm(bank[:, 0:NQ_], dftS[:, m, P * i:P * i + P], AB[:, m, NP_:512], m == 0, m == 3)
                ins.then_inc(A.filled(Q_), 1)
                if i >= 0:
                    turn_y(i - 1)
            P_ = ("P", 4)
            bank = A.open(pe, P_)
            for m in range(4):
                mm(bank[0:1, 0:NP_], consts[:, C_ALT:C_ALT + 1], AB[:, m, 0:NP_], m == 0, False)
            mm(bank[0:1, 0:NP_], alt_row[:, 0:1], A512, False, True).then_inc(A.filled(P_), 1)
            turn_y(3)
            A.wait_read(pe, P_)
            key = ("Y1", 4)
            bank = B.open(pe, key)
            for g in range(GROUPS):
                ins = mm(bank[:, g:g + 1], Y1b[0:1, P * g:P * g + P], ident[0:1, 0:1], True, True)
            ins.then_inc(B.filled(key), 1)

            def scores(j):
                if j != 1:
                    for k in range(HK):
                        turn_k(1, j, k)
                for h in range(HEADS):
                    key = ("At", j, h)
                    bank = A.open(pe, key)
                    rows = slice(DK * (h % 2), DK * (h % 2) + DK)
                    for d in range(2):
                        ins = mm(bank[:, P * d:P * d + P], kt_[d][h // 2][rows, P * j:P * j + P],
                                 qt[d][h // 2][rows, P * j:P * j + P], True, True)
                    ins.then_inc(A.filled(key), 1)
                if j != 1:
                    for k in range(HK):
                        update(1, j, k)

            def outputs(s, j):
                key = ("o", j)
                pe.wait_ge(s_at, HEADS * (s + 1))
                if j > 0:
                    pe.wait_ge(s_srf, HK * j)
                    pe.wait_ge(s_srb, HK * s)
                bank = B.open(pe, key)
                for k in range(HK):
                    both = slice(2 * DV * k, 2 * DV * k + 2 * DV)
                    if j > 0:
                        mm(bank[:, both], qt[0][k][:, P * j:P * j + P], Srf[:, j - 1, k, :], True, False)
                        mm(bank[:, both], qt[1][k][:, P * j:P * j + P], Srb[:, s % 3, k, :], False, False)
                    for h in (2 * k, 2 * k + 1):
                        ins = mm(bank[:, DV * h:DV * h + DV], ATb[:, s % 2, h, :], vN[:, j, DV * h:DV * h + DV],
                                 j == 0, True)
                ins.then_inc(B.filled(key), 1)

            def turn_o(s, j):
                turn(("oT", j), yo[:, s % 2, :], lambda: B.wait_read(pe, ("o", j)))

            scores(b_order[0])
            for s, j in enumerate(b_order):
                if s + 1 < NT:
                    scores(b_order[s + 1])
                outputs(s, j)
                if s >= 1:
                    turn_o(s - 1, b_order[s - 1])
            turn_o(NT - 1, b_order[-1])

            modulation(len(ada1), ada2)

            def turn_x(j):
                for h in range(2):
                    turn(("x2", j, h), yN[:, j, 512 * h:512 * h + 512], lambda: pe.wait_ge(s_2x, j + 1))

            for c in range(4):
                i = len(zin) + c
                half = wout[c][1]
                pe.wait_ge(s_wlo, i + 1)
                for j in range(NT):
                    if c < 2:
                        pe.wait_ge(s_yl, NT * (1 - half) + j + 1)
                    key = ("wo", c, j)
                    row_tile(A, key, 0, i, j, range(4), YTh, YTl, 4 * half, 512).then_inc(A.filled(key), 1)
                    if c == 3 and j >= LAG2:
                        turn_x(j - LAG2)
            for j in range(NT - LAG2, NT):
                turn_x(j)

            def up(g, x, t=0):
                i = w1_split(g, x)
                pe.wait_ge(s_wlo, i + 1 + 8 * t)
                for u in range(6):
                    key = A0 + UA * g + 6 * x + u
                    if g == 0 and x == 0 and u % 2 == 0:
                        pe.wait_ge(s_2l, 6 * (u // 2 + 1))
                    up_tile(key, 6 * t, i, u % 2, u // 2, HT2h, HT2l).then_inc(A.filled(key), 1)

            def down(i, g, n, t=0):
                pe.wait_ge(s_wlo, i + 1 + 8 * t)
                if n == 0:
                    pe.wait_ge(s_fl, 12 * (g + 1) + 24 * t)
                for j in range(NT):
                    key = B0 + UB * g + NT * n + j
                    row_tile(B, key, 12 * t, i, j, range(FT), FTh[g % 2], FTl[g % 2], 0, 512).then_inc(B.filled(key), 1)

            for x in range(2):
                up(0, x)

            def group(g, t):
                for x in range(2):
                    up(g + 1, x, t)
                for n in range(2):
                    down(ff_split + 4 * g + 4 + n, g, n, t)

            with pe.Fori(0, NG // 2 - 1) as t:
                group(0, t)
                group(1, t)
            group(NG - 2, 0)
            for n in range(2):
                down(ff_split + 4 * NG - 2 + n, NG - 1, n)

        @block.vector
        def _(dve):
            own = Steps(dve, s_dve)
            V = nc.vector

            def step(ins):
                own.did(ins)
                own.settle()

            bank = A.take(dve, "vec")
            V.tensor_copy(vT, bank[:, 0:R_ALL]).then_inc(A.read("vec"), 1)
            own.did(V.memset(ones, 1.0))
            A.wait_read(dve, "vec")
            dve.wait_ge(s_sexp, 1)
            step(V.tensor_scalar(sil, sil, 1.0, None, ALU.add))
            step(V.reciprocal(sil2, sil))
            dve.wait_ge(s_zero, 1)
            V.tensor_tensor(slq[:, :, 0:2], vT[:, 0:16].rearrange("p (v k) -> p k v", v=2),
                            sil2.rearrange("p (v k) -> p k v", v=2), ALU.mult).then_inc(s_slp, 1)

            def add_pos(j):
                dve.wait_ge(s_x[j % 2], 16 * (j // 2 + 1))
                dve.wait_ge(s_pos[j % 2], 32 * ((j + 1) // 2))
                dve.wait_ge(s_posc, 16)
                own.did(V.tensor_tensor(xs[:, j % 2, 0:512], xs[:, j % 2, 0:512], posr[:, j % 2, :], ALU.add))
                V.tensor_tensor(xs[:, j % 2, 512:D], xs[:, j % 2, 512:D], posc, ALU.add).then_inc(s_posd, 1)

            add_pos(1)

            def mod_cols(c, norm):
                bank = B.take(dve, ("mod", c))
                shift = c[1] in (SH_M, SH_F)
                dst = (shf if shift else amul)[norm].rearrange("p (k v) -> p k v", v=2)
                row = {SH_M: R_SHM, SC_M: R_SCM, SH_F: R_SHF, SC_F: R_SCF}[c[1]] + 2 * c[2]
                V.tensor_tensor(dst[:, 2 * c[2]:2 * c[2] + 2, :], bank[:, 0:4].rearrange("p (k v) -> p k v", v=2),
                                vT[:, row:row + 2].unsqueeze(2).to_broadcast([P, 2, 2]), ALU.add).then_inc(B.read(("mod", c)), 1)
                B.wait_read(dve, ("mod", c))

            def finish_gains(norm, row):
                view = amul[norm].rearrange("p (k v) -> p k v", v=2)
                step(V.scalar_tensor_tensor(out=view, in0=view, scalar=1.0,
                                            in1=vT[:, row:row + 8].unsqueeze(2).to_broadcast([P, 8, 2]),
                                            op0=ALU.add, op1=ALU.mult))
                V.tensor_reduce(hmx[norm][:, 1:2], amul[norm], AX_X, ALU.max, apply_absolute_value=True).then_inc(s_hmx, 1)
                V.tensor_reduce(hmx[norm][:, 2:3], shf[norm], AX_X, ALU.max, apply_absolute_value=True).then_inc(s_hmx, 1)

            def scale_gains(norm):
                dve.wait_ge(s_hsc, norm + 1)
                own.did(V.tensor_scalar(amul[norm], amul[norm], hscl[norm], None, ALU.mult))
                step(V.tensor_scalar(shf[norm], shf[norm], hscl[norm], None, ALU.mult))

            for c in ada1:
                mod_cols(c, 0)
            finish_gains(0, R_GPM)
            chunk_max(dve, 0)
            scale_gains(0)
            chunk_max(dve, 1)

            def modulate(key, norm, j, h, buf):
                bank = B.take(dve, key)
                v = 1 if j == 0 else 0
                for k in range(4):
                    c = 2 * (4 * h + k) + v
                    ins = V.tensor_scalar(buf[:, P * k:P * k + P], bank[:, P * k:P * k + P], amul[norm][:, c:c + 1],
                                          shf[norm][:, c:c + 1], ALU.mult, ALU.add)
                    if k < 3:
                        own.did(ins)
                ins.then_inc(B.read(key), 1)

            def low_h(high_done, low_done, hi, lo, j, h, buf):
                dve.wait_ge(high_done, 2 * j + h + 1)
                tile_ = (slice(None), slice(4 * h, 4 * h + 4), slice(P * j, P * j + P))
                V.tensor_tensor(lo[tile_], buf.rearrange("p (k t) -> p k t", k=4), hi[tile_], ALU.subtract).then_inc(low_done, 1)

            for j in range(NT):
                if j + 2 < NT:
                    add_pos(j + 2)
                for h in range(2):
                    if j >= 1:
                        dve.wait_ge(s_tl, 2 * (j - 1) + h + 1)
                    modulate(("xT", j, h), 0, j, h, tb[h])
                for h in range(2):
                    B.wait_read(dve, ("xT", j, h))
                    low_h(s_th, s_tl, HTh, HTl, j, h, tb[h])
                if j == 2:
                    chunk_low(dve, 0)

            def decays(k):
                for d in range(2):
                    for t in range(TB):
                        key = ("la", d, k, t)
                        bank = B.take(dve, key)
                        r = R_BA + HK * d + k
                        V.tensor_scalar(tmp[2 * d][:, TBW * t:TBW * t + TBW], bank[:, 0:TBW], vT[:, r:r + 1], None,
                                        ALU.add).then_inc(B.read(key), 1)
                for d in range(2):
                    x, c = tmp[2 * d], tmp[2 * d + 1]
                    dve.wait_ge(s_dln, 2 * k + d + 1)
                    step(V.scalar_tensor_tensor(out=x, in0=x, scalar=0.0, in1=c, op0=ALU.min, op1=ALU.subtract))
                    for j in range(NT):
                        part_ = slice(P * j, P * j + P) if d == 0 else slice(P * j + P - 1, P * j - 1 if j else None, -1)
                        own.did(V.tensor_tensor_scan(c[:, part_], ones, x[:, part_], 0.0, ALU.mult, ALU.add))
                    own.settle()
                    last, mid = (P - 1, P // 2 - 1) if d == 0 else (0, P // 2)
                    w = wexp[2 * d + k]
                    cv = c.rearrange("p (j t) -> p j t", t=P)
                    own.did(V.tensor_copy(w[:, 0:NT], cv[:, :, last]))
                    own.did(V.tensor_copy(w[:, 2 * NT:3 * NT], cv[:, :, mid]))
                    own.settle()
                    own.did(V.tensor_tensor(w[:, NT:2 * NT], w[:, 0:NT], w[:, 2 * NT:3 * NT], ALU.subtract))
                    step(V.tensor_tensor(x.rearrange("p (j t) -> p j t", t=P), cv,
                                         w[:, 2 * NT:3 * NT].unsqueeze(2).to_broadcast([P, NT, P]), ALU.subtract))
                    V.tensor_scalar(x, x, CLAMP, -CLAMP, ALU.min, ALU.max).then_inc(s_de, 1)
                for i in range(2):
                    for key in z_uses(i):
                        A.wait_read(dve, key)
                for d in range(2):
                    dve.wait_ge(s_dexp, 4 * k + 2 * d + 1)
                    V.tensor_tensor(qt[d][k], qT[:, k, :], tmp[2 * d + 1], ALU.mult).then_inc(s_qk, 1)
                    dve.wait_ge(s_dexp, 4 * k + 2 * d + 2)
                    V.tensor_tensor(kt_[d][k], kT[:, k, :], tmp[2 * d], ALU.mult).then_inc(s_qk, 1)
                dve.wait_ge(s_qk, 4 * k + 4)

            def fold():
                for i in (3, 4):
                    for key in z_uses(i):
                        A.wait_read(dve, key)
                up_ = uT[:, :, CTX + 1:CTX + FOLD]
                down_ = uT[:, :, CTX + LAT - 1:CTX + FOLD:-1]
                own.did(V.tensor_tensor(Ef[:, :, 1:FOLD], up_, down_, ALU.add))
                own.did(V.tensor_tensor(Of[:, :, 1:FOLD], up_, down_, ALU.subtract))
                own.did(V.tensor_copy(Ef[:, :, 0:FOLD + 1:FOLD], uT[:, :, CTX:CTX + FOLD + 1:FOLD]))
                V.memset(Of[:, :, 0:1], 0.0).then_inc(s_fold, 1)


            def silu_gate(x):
                cs = slice(CW * x, CW * x + CW)
                for r in range(3):
                    js = slice(3 * r, 3 * r + 3)
                    dve.wait_ge(s_ge, NT * x + 3 * r + 3)
                    e, g = gex[:, js, cs], gN[:, js, cs]
                    step(V.tensor_scalar(e, e, 1.0, None, ALU.add))
                    step(V.reciprocal(e, e))
                    step(V.tensor_tensor(g, g, e, ALU.mult))
                    V.tensor_tensor(g, g, ghb[:, cs].unsqueeze(1).to_broadcast([P, 3, CW]), ALU.mult).then_inc(s_gs, 1)

            dve.wait_ge(s_misc, 48)
            for i in range(len(zin)):
                if i + 2 < len(zin):
                    chunk_max(dve, i + 2)
                if i + 1 < len(zin):
                    chunk_low(dve, i + 1)
                if i == 3:
                    decays(0)
                if i == 5:
                    decays(1)
                if i == 6:
                    fold()
                if i == 8:
                    silu_gate(0)
                    silu_gate(1)

            def blocks(out, S, w, done=None):
                own.did(V.tensor_scalar(out[0:DK, 0:DV], S[0:DK, :], w[0:DK, :], None, ALU.mult))
                V.tensor_scalar(out[DK:P, DV:2 * DV], S[DK:P, :], w[DK:P, :], None, ALU.mult).then_inc(done, 1)

            def absorb(d, j, k):
                key = ("U", d, j, k)
                w = wexp[2 * d + k]
                bank = A.take(dve, key)
                dst = Sctx[d][:, k, :] if j == 0 else tU[k]
                own.did(V.tensor_scalar(dst[0:DK, :], bank[0:DK, 0:DV], w[0:DK, NT + j:NT + j + 1], None, ALU.mult))
                V.tensor_scalar(dst[DK:P, :], bank[DK:P, DV:2 * DV], w[DK:P, NT + j:NT + j + 1], None,
                                ALU.mult).then_inc(A.read(key), 1)
                if j > 0:
                    A.wait_read(dve, key)
                    own.settle()
                    step(V.scalar_tensor_tensor(out=Sst[:, d, k, :], in0=Sst[:, d, k, :], scalar=w[:, j:j + 1], in1=tU[k],
                                                op0=ALU.mult, op1=ALU.add))

            step(V.memset(Srf, 0.0))
            dve.wait_ge(s_state, 32)
            for k in range(HK):
                blocks(Srf[:, 0, k, :], Sst[:, 0, k, :], wexp[k][:, 2 * NT + 1:2 * NT + 2], s_srf)
            for j in f_order[:-1]:
                for k in range(HK):
                    absorb(0, j, k)
                    if j > 0:
                        blocks(Srf[:, j, k, :], Sst[:, 0, k, :], wexp[k][:, 2 * NT + j + 1:2 * NT + j + 2], s_srf)

            def groups(y):
                return y.rearrange("p (g c) -> p g c", g=GROUPS)

            for i in range(-1, 4):
                key = ("P", i)
                bank = A.take(dve, key)
                A.wait_read(dve, ("Q", i))
                if i >= 0:
                    B.take(dve, ("Y1", i - 1))
                if i >= 1:
                    B.take(dve, ("Y2", i - 1))
                p, q = groups(bank[:, 0:GROUPS * NCOS]), groups(Qs[:, 0:GROUPS * NSIN])
                outs = [(groups(Y1b), ALU.subtract, ALU.add)] + ([(groups(Y2b), ALU.add, ALU.subtract)] if i >= 0 else [])
                for n, (y, low, high) in enumerate(outs):
                    own.did(V.tensor_tensor(y[:, :, 1:64], p[:, :, 1:64], q, low))
                    own.did(V.tensor_tensor(y[:, :, P - 1:64:-1], p[:, :, 1:64], q, high))
                    ins = V.tensor_copy(y[:, :, 0:NCOS:64], p[:, :, 0:NCOS:64])
                    if n < len(outs) - 1:
                        own.did(ins)
                ins.then_inc(A.read(key), 1)
            key = ("P", 4)
            bank = A.take(dve, key)
            B.take(dve, ("Y1", 3))
            p, y = groups(bank[0:1, 0:GROUPS * NCOS]), groups(Y1b[0:1, :])
            own.did(V.tensor_copy(y[:, :, 0:NCOS], p))
            V.tensor_copy(y[:, :, P - 1:64:-1], p[:, :, 1:64]).then_inc(A.read(key), 1)

            def y_max(half):
                V.tensor_reduce(ymx[:, half:half + 1], R7[:, 4608 * half:4608 * half + 4608], AX_X, ALU.max,
                                apply_absolute_value=True).then_inc(s_ymx, 1)

            B.wait_read(dve, ("Y1", 4))
            y_max(1)

            step(V.memset(Srb, 0.0))

            def scores(s, j):
                for h in range(HEADS):
                    key = ("At", j, h)
                    bank = A.take(dve, key)
                    if s >= 1:
                        dve.wait_ge(s_at, HEADS * (s - 1) + h + 1)
                    V.tensor_tensor(Am[:, h, :], bank[:, 0:2 * P], masks, ALU.mult).then_inc(A.read(key), 1)
                if j == 1:
                    return
                nxt = b_order[s + 1]
                for k in range(HK):
                    absorb(1, j, k)
                    if k == 0 and s >= 2:
                        B.take(dve, ("o", b_order[s - 2]))
                    blocks(Srb[:, (s + 1) % 3, k, :], Sst[:, 1, k, :], wexp[2 + k][:, 2 * NT + nxt:2 * NT + nxt + 1], s_srb)

            def gate_o(s, j):
                key = ("o", j)
                bank = B.take(dve, key)
                dve.wait_ge(s_ors, s + 1)
                if s >= 2:
                    B.take(dve, ("oT", b_order[s - 2]))
                for h in range(HEADS):
                    hv = slice(DV * h, DV * h + DV)
                    ins = V.scalar_tensor_tensor(out=yo[:, s % 2, hv], in0=bank[:, hv], scalar=ors[:, 4 * j + h:4 * j + h + 1],
                                                 in1=gN[:, j, hv], op0=ALU.mult, op1=ALU.mult)
                    if h < HEADS - 1:
                        own.did(ins)
                ins.then_inc(B.read(key), 1)

            scores(0, b_order[0])
            for s, j in enumerate(b_order):
                if s + 1 < NT:
                    scores(s + 1, b_order[s + 1])
                gate_o(s, j)
            B.wait_read(dve, ("oT", b_order[-1]))
            y_max(0)

            def low_y(half, j):
                dve.wait_ge(s_yh, NT * (1 - half) + j + 1)
                t_ = (slice(None), slice(4 * half, 4 * half + 4), slice(P * j, P * j + P))
                V.scalar_tensor_tensor(out=YTl[t_], in0=yT[t_], scalar=yscl[:, half:half + 1], in1=YTh[t_],
                                       op0=ALU.mult, op1=ALU.subtract).then_inc(s_yl, 1)

            dve.wait_ge(s_bc, 64)
            for nn, c in enumerate(ada2):
                if c[1] in (GT_M, GT_F):
                    g = 0 if c[1] == GT_M else 1
                    key = ("mod", c)
                    cs = slice(CW * c[2], CW * c[2] + CW)
                    bank = B.take(dve, key)
                    own.did(V.tensor_tensor(gates[:, g, 0, cs], bank[:, 0:CW], bcast[:, 2 * g, cs], ALU.add))
                    V.tensor_tensor(gates[:, g, 1, cs], bank[:, CW:2 * CW], bcast[:, 2 * g, cs], ALU.add).then_inc(B.read(key), 1)
                    own.settle()
                    B.wait_read(dve, key)
                    for v in range(2):
                        own.did(V.tensor_tensor(gates[:, g, v, cs], gates[:, g, v, cs], bcast[:, 2 * g + 1, cs], ALU.mult))
                else:
                    mod_cols(c, 1)
                    if c[1] == SC_F and c[2] == 3:
                        finish_gains(1, R_GPF)
                for r in range(2 * NT * nn // len(ada2), 2 * NT * (nn + 1) // len(ada2)):
                    low_y(1 - r // NT, r % NT)
            w0 = len(zin)
            chunk_max(dve, w0)
            chunk_max(dve, w0 + 1)
            scale_gains(1)
            chunk_low(dve, w0)

            def post(j):
                dve.wait_ge(s_prs, j + 1)
                v = 1 if j == 0 else 0
                step(V.scalar_tensor_tensor(out=yN[:, j, :], in0=yN[:, j, :], scalar=prs[:, j:j + 1], in1=gates[:, 0, v, :],
                                            op0=ALU.mult, op1=ALU.mult))
                dve.wait_ge(s_x1[j], 16)
                V.tensor_tensor(x1[:, j, :], x1[:, j, :], yN[:, j, :], ALU.add).then_inc(s_xr, 1)

            def modulate_2(j):
                for h in range(2):
                    if j >= 1:
                        dve.wait_ge(s_2l, 2 * (j - 1) + h + 1)
                    modulate(("x2", j, h), 1, j, h, tb2[h])
                for h in range(2):
                    B.wait_read(dve, ("x2", j, h))
                    low_h(s_2h, s_2l, HT2h, HT2l, j, h, tb2[h])

            own.settle()
            for c in range(4):
                i = w0 + c
                chunk_max(dve, i + 2)
                chunk_low(dve, i + 1)
                n = wout[c][2]
                cof = wcof[:, i % 8:i % 8 + 1]
                for j in range(NT):
                    key = ("wo", c, j)
                    bank = A.take(dve, key)
                    y = yN[:, j, 512 * n:512 * n + 512]
                    if c % 2 == 0:
                        V.tensor_scalar(y, bank[:], cof, None, ALU.mult).then_inc(A.read(key), 1)
                    else:
                        A.wait_read(dve, ("wo", c - 1, j))
                        V.scalar_tensor_tensor(out=y, in0=bank[:], scalar=cof, in1=y, op0=ALU.mult,
                                               op1=ALU.add).then_inc(A.read(key), 1)
                    if c == 3 and j >= 2:
                        post(j - 2)
                    if c == 3 and j >= LAG2:
                        modulate_2(j - LAG2)
            post(NT - 2)
            post(NT - 1)
            for j in range(NT - LAG2, NT):
                modulate_2(j)

            def up(g, x, t=0):
                for u in range(6):
                    r = 6 * x + u
                    n = 12 * g + r
                    key = A0 + UA * g + r
                    tb_, m = u // 2, 2 * x + u % 2
                    A.wait_read(dve, key, 6 * t)
                    if n >= 2:
                        dve.wait_ge(s_fl, n - 1 + 24 * t)
                    V.tensor_tensor(fsq[:, n % 2, :], frel[:, n % 2, :], frel[:, n % 2, :], ALU.mult).then_inc(s_fq, 1)
                    dve.wait_ge(s_fq, n + 1 + 24 * t)
                    dve.wait_ge(s_fh, n + 1 + 24 * t)
                    toks = slice(TBW * tb_, TBW * tb_ + TBW)
                    V.tensor_tensor(FTl[g % 2][:, m, toks], fsq[:, n % 2, :], FTh[g % 2][:, m, toks],
                                    ALU.subtract).then_inc(s_fl, 1)

            def down(i, g, n, t=0, then=None):
                cof = wcof[:, i % 8:i % 8 + 1]
                for j in range(NT):
                    key = B0 + UB * g + NT * n + j
                    bank = B.take(dve, key, 12 * t)
                    B.wait_read(dve, key - UB, 12 * t)
                    y = acc[:, j, 512 * n:512 * n + 512]
                    V.scalar_tensor_tensor(out=y, in0=bank[:], scalar=cof, in1=y, op0=ALU.mult,
                                           op1=ALU.add).then_inc(B.read(key), 1)
                    if then is not None:
                        then(j)

            F = ff_split
            chunk_max(dve, F + 2)
            chunk_low(dve, F + 1)
            up(0, 0)
            chunk_max(dve, F + 3)
            chunk_low(dve, F + 2)
            up(0, 1)
            dve.wait_ge(s_accz, 1)

            def group(g, t):
                for s in range(4):
                    chunk_max(dve, F + 4 * g + 4 + s, t)
                    chunk_low(dve, F + 4 * g + 3 + s, t)
                    if s < 2:
                        up(g + 1, s, t)
                    else:
                        down(F + 4 * g + 4 + s - 2, g, s - 2, t)

            with dve.Fori(0, NG // 2 - 1) as t:
                group(0, t)
                group(1, t)
            group(NG - 2, 0)

            def finish(j):
                dve.wait_ge(s_frs, j + 1)
                v = 1 if j == 0 else 0
                step(V.scalar_tensor_tensor(out=acc[:, j, :], in0=acc[:, j, :], scalar=frs[:, j:j + 1], in1=gates[:, 1, v, :],
                                            op0=ALU.mult, op1=ALU.mult))
                V.tensor_tensor(x1[:, j, :], x1[:, j, :], acc[:, j, :], ALU.add).then_inc(s_y, 1)

            chunk_low(dve, F + 4 * NG - 1)
            down(F + 4 * NG - 2, NG - 1, 0)
            down(F + 4 * NG - 1, NG - 1, 1, 0, lambda j: finish(j - 2) if j >= 2 else None)
            finish(NT - 2)
            finish(NT - 1)


def _constants():
    import numpy as np
    i = np.arange(P)
    k = np.zeros((P, C_ALL), np.float64)
    k[:, C_ID:C_ID + P] = np.eye(P)
    k[:, C_MASK:C_MASK + P] = i[:, None] <= i[None, :]
    k[:, C_MASK + P:C_MASK + 2 * P] = i[:, None] >= i[None, :]
    for v in range(2):
        k[v::32, C_SEL2 + v] = 1.0
        k[v::32, C_SELB + P * v:C_SELB + P * v + P] = 1.0
    turn = 2.0 * np.pi * (np.outer(i, i) % P) / P
    k[:, C_CH:C_CH + NCOS] = np.cos(turn)[:, 0:NCOS]
    k[:, C_CH + NCOS:C_CH + P] = np.sin(turn)[:, 1:64]
    k[:, C_CTX:C_CTX + P] = np.cos(turn) / P
    k[:, C_CTX + P:C_CTX + 2 * P] = np.sin(turn) / P
    unit = 1.0 / np.sqrt(LAT * P)
    k[:, C_ALT] = unit * (1.0 - 2.0 * (i % 2))
    m = np.arange(FOLD)
    turn = 2.0 * np.pi * (np.outer(m, m) % LAT) / LAT
    f = np.float32
    nf = D // 4
    omega = (f(1.0) / (f(10000.0) ** (np.arange(nf, dtype=f) / f(nf)))).astype(f)
    row, col = np.arange(LAT // 64, dtype=f)[:, None] * omega, (i % 64).astype(f)[:, None] * omega
    return {
        "k_consts": k.astype(f),
        "k_dft_cos": (unit * np.cos(turn)).astype(f),
        "k_dft_sin": (unit * np.sin(turn)).astype(f),
        "k_alt": (unit * (1.0 - 2.0 * (m % 2)))[None, :].astype(f),
        "k_pos_row": np.concatenate([np.sin(row), np.cos(row)], axis=1).astype(f),
        "k_pos_col": np.concatenate([np.sin(col), np.cos(col)], axis=1).astype(f),
    }


_INS = ["x_prompt", "x_sample", "state_gla_fwd", "state_gla_bwd", "c", "c_ctx", "w_in", "w_out", "w_a2", "b_a2",
        "g_head", "w_ada", "b_ada", "g_pre_mix", "g_post_mix", "g_pre_mlp", "g_post_mlp", "w_fc1", "w_fc2"]
_OUTS = [(1, CTX, D), (1, LAT, D), (1, 1, HEADS, DK, DV), (1, 1, HEADS, DK, DV)]


def kernel(**inputs):
    import numpy as _np
    import concourse.bacc as _bacc
    from concourse.bass_utils import run_bass_kernel_spmd as _run

    nc = _bacc.Bacc("TRN2", target_bir_lowering=False, num_devices=1)
    arrays, args = {}, {}
    for name, x in [(n, _np.ascontiguousarray(inputs[n])) for n in _INS] + list(_constants().items()):
        arrays[f"in_{name}"] = x
        args[name] = nc.dram_tensor(f"in_{name}", x.shape, F32, kind="ExternalInput").ap()
    for i, shape in enumerate(_OUTS):
        args[f"out_{i}"] = nc.dram_tensor(f"out_{i}_dram", shape, F32, kind="ExternalOutput").ap()
    hybrid_step(nc, args)
    r = _run(nc, [arrays], core_ids=[0])
    return tuple(r.results[0][f"out_{i}_dram"] for i in range(len(_OUTS)))
```

```python
from contextlib import ExitStack

import concourse.bass as bass
from concourse import mybir

ALU = mybir.AluOpType
ACT = mybir.ActivationFunctionType
AX_X = mybir.AxisListType.X
AX_XY = mybir.AxisListType.XY
F32 = mybir.dt.float32
F16 = mybir.dt.float16
RMAX = bass.bass_isa.ReduceOp.max

P = 128
D = 1024
KT = D // P
CTX = 128
LAT = 1024
TOK = CTX + LAT
NT = TOK // P
TB = 3
TBW = TOK // TB
HEADS, DK, DV = 4, 64, 128
HK = HEADS * DK // P
VW = HEADS * DV
RANK = 16
GROUPS = 4
FF = 4 * D
GFF = 512
NG = FF // GFF
FT = GFF // P
CW = 256
EPS = 1e-6
TAU = 16.0
CLAMP = 80.0 * TAU
NCOS, NSIN = 65, 63
FOLD = LAT // 2
TOP = 2.0 ** 15
TINY = 1e-30
F_ALPHA = 2.0 ** -28

Q0, K0, V0, G0 = 0, 256, 512, 1024
LR0 = 1536
U0 = LR0 + 2 * RANK
SH_M, SC_M, GT_M, SH_F, SC_F, GT_F = range(6)

C_ID, C_MASK, C_SEL2, C_CH, C_CTX, C_ALT = 0, 128, 384, 386, 514, 770
C_ALL = 771
SMALL = 784
R_C, R_CTX, R_GPM, R_GPF, R_SHM, R_SCM, R_SHF, R_SCF, R_BA = 0, 8, 16, 24, 32, 40, 48, 56, 64
R_GTM, R_GTF, R_PM, R_PF = 68, 76, 84, 92
R_ALL = 100


class Ring:

    def __init__(self, banks, full, free, keys):
        self.banks, self.full, self.free, self.keys = banks, full, free, keys
        self.at = {k: i for i, k in enumerate(keys)}
        self.next = 0

    def spot(self, key, turns=0):
        i = self.at[key] if not isinstance(key, int) else key
        return i % len(self.banks), i // len(self.banks) + 1, turns

    def open(self, eng, key, turns=0):
        if not isinstance(key, int):
            assert self.at[key] == self.next, (key, self.keys[self.next])
            self.next += 1
        b, n, t = self.spot(key, turns)
        if n > 1:
            eng.wait_ge(self.free[b], n - 1 + t)
        return self.banks[b]

    def filled(self, key):
        return self.full[self.spot(key)[0]]

    def read(self, key):
        return self.free[self.spot(key)[0]]

    def take(self, eng, key, turns=0):
        b, n, t = self.spot(key, turns)
        eng.wait_ge(self.full[b], n + t)
        return self.banks[b]

    def wait_read(self, eng, key, turns=0):
        b, n, t = self.spot(key, turns)
        eng.wait_ge(self.free[b], n + t)


class Steps:

    def __init__(self, eng, sem):
        self.eng, self.sem, self.n = eng, sem, 0

    def did(self, ins):
        ins.then_inc(self.sem, 1)
        self.n += 1

    def settle(self):
        self.eng.wait_ge(self.sem, self.n)


def hybrid_step(nc, a):
    x_prompt, x_sample, w_in, w_out, w_ada, w_fc1, w_fc2 = (
        a[n] for n in ("x_prompt", "x_sample", "w_in", "w_out", "w_ada", "w_fc1", "w_fc2"))
    out_p, out_s, out_sf, out_sb = a["out_0"], a["out_1"], a["out_2"], a["out_3"]

    ada1 = [("ada", s, n) for s in (SH_M, SC_M) for n in range(D // CW)]
    zin = [("win", LR0, 2 * RANK), ("win", Q0, CW), ("win", K0, CW), ("win", U0, CW), ("win", U0 + CW, CW),
           ("win", V0, CW), ("win", V0 + CW, CW), ("win", G0, CW), ("win", G0 + CW, CW)]
    ada2 = [("ada", s, n) for s in (GT_M, SH_F, SC_F, GT_F) for n in range(D // CW)]
    wout = [("wout", part, n) for n in range(2) for part in (1, 0)]
    chunks = zin + ada2 + wout
    splits = zin + wout
    ff_chunk = len(chunks)
    ff_split = len(splits)
    chunk_of = {c: i for i, c in enumerate(chunks)}
    split_of = {c: i for i, c in enumerate(splits)}

    def w1_split(g, x):
        return ff_split + x if g == 0 else ff_split + 4 * g - 2 + x

    LR, Q, K, U_A, U_B, V_A, V_B, G_A, G_B = range(9)
    TFORM = (LR, Q, K, U_A, U_B)
    a_keys, b_keys = [], []
    a_keys.append("vec")
    start = []
    for what in "x0 a0 x1 a1 x2 x3 a2 x4 a3 x5 x6 a4 x7 x8 a5 a6 a7".split():
        n = int(what[1])
        start.append(("x" if what[0] == "x" else "rows", n))
        if what[0] == "a" and n >= 1:
            start.append(("out", n - 1))
    start.append(("out", len(ada1) - 1))
    for what, n in start:
        if what == "x":
            b_keys += [("xT", n, h) for h in range(2)]
        elif what == "rows":
            a_keys.append(ada1[n])
        else:
            b_keys.append(("mod", ada1[n]))

    def z_uses(i):
        if i == LR:
            return [("z", i, 0, t) for t in range(TB)]
        if i in TFORM:
            return [("z", i, m, t) for t in range(TB) for m in range(2)]
        return [("z", i, 0, j) for j in range(NT)]

    for i in range(len(zin)):
        a_keys += z_uses(i)
    logit_keys = [("la", d, k, t) for k in range(HK) for d in range(2) for t in range(TB)]
    b_keys += logit_keys
    f_order = [0] + list(range(1, NT))
    b_order = [0] + list(range(NT - 1, 0, -1))
    def ada_step(n):
        return ([("rows", n)] if n < len(ada2) else []) + ([("out", n - 1)] if n >= 1 else [])

    def ada_keys(n):
        for what, m in ada_step(n):
            if what == "rows":
                a_keys.append(ada2[m])
            else:
                b_keys.append(("mod", ada2[m]))

    N_FWD, N_FOU = NT - 1, 5
    for s, j in enumerate(f_order[:-1]):
        for k in range(HK):
            b_keys.append(("kn", 0, j, k))
            a_keys.append(("U", 0, j, k))
        ada_keys(s)
    for i in range(4):
        a_keys.append(("dA", i))
    a_keys += [("dA", 4), ("dA", 5)]
    for i in range(-1, 4):
        a_keys += [("P", i), ("Q", i)]
        ada_keys(N_FWD + 1 + i)
        if i >= 0:
            b_keys += [("Y1", i - 1)] + ([("Y2", i - 1)] if i >= 1 else [])
    a_keys.append(("P", 4))
    b_keys += [("Y1", 3), ("Y2", 3), ("Y1", 4)]

    def gla_scores(j):
        for h in range(HEADS):
            a_keys.append(("At", j, h))
        if j != 1:
            for k in range(HK):
                b_keys.append(("kn", 1, j, k))
                a_keys.append(("U", 1, j, k))

    gla_scores(b_order[0])
    for s, j in enumerate(b_order):
        if s + 1 < NT:
            gla_scores(b_order[s + 1])
        b_keys.append(("o", j))
        if s >= 1:
            b_keys.append(("oT", b_order[s - 1]))
        if N_FWD + N_FOU + s <= len(ada2):
            ada_keys(N_FWD + N_FOU + s)
    b_keys.append(("oT", b_order[-1]))
    for j in range(NT):
        a_keys += [("wo", c, j) for c in range(4)]
        if j < 2:
            b_keys += [("gate", 4 * j + q) for q in range(4)]
        if j >= 2:
            b_keys += [("x2", j - 2, h) for h in range(2)]
    for j in (NT - 2, NT - 1):
        b_keys += [("x2", j, h) for h in range(2)]
    A0, B0 = len(a_keys), len(b_keys)
    UA, UB = 2 * TB * 2, 2 * NT
    w2_rel = {4 * g + 4 + n for g in range(NG - 1) for n in range(2)} | {4 * NG - 2, 4 * NG - 1}

    with ExitStack() as ctx:
        def sb(name, shape, dt=F32):
            return ctx.enter_context(nc.sbuf_tensor(name, shape, dt))

        def sem(name):
            return ctx.enter_context(nc.semaphore(name))

        banks = [ctx.enter_context(nc.psum_tensor(f"bank{i}", [P, 512], F32)) for i in range(8)]
        A = Ring(banks[0:4], [sem(f"a_full{i}") for i in range(4)], [sem(f"a_free{i}") for i in range(4)], a_keys)
        B = Ring(banks[4:7], [sem(f"b_full{i}") for i in range(3)], [sem(f"b_free{i}") for i in range(3)], b_keys)
        junk = banks[7]

        R1 = sb("region1", [P, 9216])
        R2 = sb("region2", [P, 9216])
        R34 = sb("region34", [P, 9216])
        R5 = sb("region5", [P, 4608])
        R7 = sb("region7", [P, 9216])
        stage = [sb(f"stage{i}", [P, 2048]) for i in range(2)]
        whi = [sb(f"whi{i}", [P, 2048], F16) for i in range(2)]
        wlo = [sb(f"wlo{i}", [P, 2048], F16) for i in range(2)]

        consts = sb("consts", [P, C_ALL])
        small = sb("small", [P, SMALL])
        vrow = sb("vrow", [P, P])
        ones = vrow[:]
        part = [sb(f"part{i}", [P, CW]) for i in range(2)]
        slq = sb("slq", [P, KT, 32])
        ghb = sb("ghb", [P, VW])
        gex = part + [sb("gex", [P, CW])]

        ident = consts[:, C_ID:C_ID + P]
        masks = consts[:, C_MASK:C_MASK + 2 * P]
        sel2 = consts[:, C_SEL2:C_SEL2 + 2]
        dft_ch = consts[:, C_CH:C_CH + P]
        dft_ctx = consts[:, C_CTX:C_CTX + 2 * P]
        alt_col = consts[:, C_ALT:C_ALT + 1]

        used = [0]

        def cols(n):
            used[0] += n
            assert used[0] <= SMALL
            return small[:, used[0] - n:used[0]]

        vT = cols(R_ALL)
        sil, sil2 = cols(16), cols(16)
        shf = [cols(16) for _ in range(2)]
        amul = [cols(16) for _ in range(2)]
        hmx = [cols(3) for _ in range(2)]
        hinv, hscl = ([cols(1) for _ in range(2)] for _ in range(2))
        hgo = cols(1)
        neg = cols(5)
        ssq, sqs, rst = cols(2 * NT), cols(NT), cols(NT)
        wmax, wall, winv, wscl, wcof = (cols(8) for _ in range(5))
        fmx, frg, ftm, finv = (cols(2) for _ in range(4))
        beta = cols(4)
        ymx, yall, yinv, yscl = (cols(2) for _ in range(4))
        ymt = cols(NT)
        gtc = [cols(16) for _ in range(2)]
        wexp = [cols(3 * NT) for _ in range(4)]
        oss, ors = cols(4 * NT), cols(4 * NT)
        pss, psm, prs = cols(2 * NT), cols(NT), cols(NT)
        qss, qsm, qrs = cols(2 * NT), cols(NT), cols(NT)
        fss, fsm, frs = cols(2 * NT), cols(NT), cols(NT)

        HTh = R1[:, 0:4608].bitcast(F16).rearrange("p (k t) -> p k t", k=KT)
        HTl = R1[:, 4608:9216].bitcast(F16).rearrange("p (k t) -> p k t", k=KT)
        YTh, YTl = HTh, HTl
        dftC = R1[:, 0:2048].rearrange("p (m n) -> p m n", m=4)
        dftS = R1[:, 2048:4096].rearrange("p (m n) -> p m n", m=4)
        AB = R1[:, 4096:6144].rearrange("p (m n) -> p m n", m=4)
        Y1b, Y2b, Qs = R1[:, 6144:6656], R1[:, 6656:7168], R1[:, 7168:7680]
        A512 = R1[0:1, 7680:7940]
        alt_row = R1[0:1, 7940:8068]
        kn = [R1[:, 8068:8196], R1[:, 8196:8324]]
        tU = [R1[:, 8324:8452], R1[:, 8452:8580]]
        Sctx = [R1[:, 8580 + 256 * d:8836 + 256 * d].rearrange("p (k n) -> p k n", k=HK) for d in range(2)]
        ATb = R1[:, 0:1024].rearrange("p (b h t) -> p b h t", b=2, h=HEADS)
        Am = R1[:, 1024:2048].rearrange("p (h t) -> p h t", h=HEADS)
        Srb = R1[:, 4096:5632].rearrange("p (b k n) -> p b k n", b=3, k=HK)
        yo = R1[:, 3072:4096].rearrange("p (b n) -> p b n", b=2)

        qt = [[R2[:, 2304 * d + 1152 * k:2304 * d + 1152 * k + 1152] for k in range(HK)] for d in range(2)]
        kt_ = [[R2[:, 4608 + 2304 * d + 1152 * k:4608 + 2304 * d + 1152 * k + 1152] for k in range(HK)] for d in range(2)]
        x1 = R2[:].rearrange("p (j n) -> p j n", j=NT)

        qT = R34[:, 0:2304].rearrange("p (k t) -> p k t", k=HK)
        kT = R34[:, 2304:4608].rearrange("p (k t) -> p k t", k=HK)
        Srf = R34[:, 0:4096].rearrange("p (j k n) -> p j k n", j=NT - 1, k=HK)
        Sst = R34[:, 4096:4608].rearrange("p (d k n) -> p d k n", d=2, k=HK)
        vN = R34[:, 4608:9216].rearrange("p (j n) -> p j n", j=NT)
        ada_room = [R1[:, 2048 * i:2048 * i + 2048] for i in range(4)] + [R34[:, 2048 * i:2048 * i + 2048] for i in range(4)]
        xh = [R1[:, 8192:9216], R34[:, 8192:9216]]
        wo_late = [[R34[:, 2048 * b + 1024 * x:2048 * b + 1024 * x + 1024].bitcast(F16) for x in range(2)] for b in range(2)]
        yN = R34[:, 4608:4608 + 4096].rearrange("p (j n) -> p j n", j=4)
        FTh = [R34[:, 4608 * b:4608 * b + 2304].bitcast(F16).rearrange("p (f t) -> p f t", f=FT) for b in range(2)]
        FTl = [R34[:, 4608 * b + 2304:4608 * b + 4608].bitcast(F16).rearrange("p (f t) -> p f t", f=FT) for b in range(2)]

        gN = R5[:].rearrange("p (j n) -> p j n", j=NT)
        tmp = [R5[:, 1152 * i:1152 * i + 1152] for i in range(4)]
        posr = R5[:, 0:4096].rearrange("p (j n) -> p j n", j=NT - 1)
        posc = R5[:, 4096:4608]
        gates = R5[:, 0:4096].rearrange("p (g v n) -> p g v n", g=2, v=2)
        tb2 = [R5[:, 4096:4608], ghb[:]]
        frel = R5[:, 0:768].rearrange("p (b n) -> p b n", b=2)
        fsq = R5[:, 768:1536].rearrange("p (b n) -> p b n", b=2)

        uT = R7[:, 0:4608].rearrange("p (g t) -> p g t", g=GROUPS)
        Ef = R7[:, 4608:4608 + 4 * (FOLD + 1)].rearrange("p (g t) -> p g t", g=GROUPS)
        Of = R7[:, 6660:6660 + 4 * FOLD].rearrange("p (g t) -> p g t", g=GROUPS)
        yT = R7[:].rearrange("p (k t) -> p k t", k=KT)
        xT = yT
        HT2h = R7[:, 0:4608].bitcast(F16).rearrange("p (k t) -> p k t", k=KT)
        HT2l = R7[:, 4608:9216].bitcast(F16).rearrange("p (k t) -> p k t", k=KT)
        acc = R1[:].rearrange("p (j n) -> p j n", j=NT)

        wa2 = R34[0:2 * RANK, 4608:4608 + 512]
        lrS = R34[0:2 * RANK, 5120:5120 + TOK]

        s_2h = sem("h2_high")
        s_2l = sem("h2_low")
        s_2x = sem("x1_normed")
        s_accz = sem("ff_sums_zeroed")
        s_act = sem("act_steps")
        s_at = sem("scores_summed")
        s_cof = sem("w_out_factors_set")
        s_dg = sem("gate_diagonals")
        s_beta = sem("ff_scale_set")
        s_const = sem("consts_loaded")
        s_de = sem("decay_exponents")
        s_dexp = sem("decay_exps")
        s_dft = sem("dft_loaded")
        s_gsg = sem("gate_sigmoid")
        s_dln = sem("decay_log1p")
        s_dve = sem("dve_steps")
        s_fh = sem("f_high")
        s_fl = sem("f_low")
        s_fold = sem("u_folded")
        s_fq = sem("f_squared")
        s_frs = sem("f_rstd")
        s_fss = sem("f_squares")
        s_ge = sem("gate_exp")
        s_gn = sem("gains_scaled")
        s_gs = sem("gate_silu")
        s_hmx = sem("h_bound_parts")
        s_hsc = sem("h_scale_set")
        s_misc = sem("w_a2_g_head_loaded")
        s_ors = sem("o_rstd")
        s_oss = sem("o_squares")
        s_out = sem("outputs_stored")
        s_pool = sem("pool_steps")
        s_pos = sem("positions_loaded")
        s_ada = [sem(f"ada{i}_loaded") for i in range(len(ada1))]
        s_ma = sem("h_by_act")
        s_mv = sem("h_by_dve")
        s_posd = sem("pos_added")
        s_prs = sem("post_rstd")
        s_pss = sem("post_squares")
        s_qk = sem("decayed_q_k")
        s_qrs = sem("x1_rstd")
        s_qss = sem("x1_squares")
        s_rst = sem("x_rstd")
        s_sexp = sem("exp_c")
        s_slp = sem("silu_c_set")
        s_sout = sem("states_stored")
        s_srb = sem("bwd_state_blocks")
        s_srf = sem("fwd_state_blocks")
        s_ssq = sem("x_squares")
        s_stage = [sem(f"stage{i}_loaded") for i in range(2)]
        s_state = sem("states_loaded")
        s_th = sem("h_high")
        s_tl = sem("h_low")
        s_vec = sem("vectors_loaded")
        s_wa2 = sem("wa2_zeroed")
        s_whi = sem("chunk_high")
        s_wlo = sem("chunk_low")
        s_wmax = sem("chunk_max")
        s_wscl = sem("chunk_scale")
        s_x = [sem(f"x{i}_loaded") for i in range(NT)]
        s_x1 = [sem(f"x1_{i}_loaded") for i in range(NT)]
        s_xh = sem("x_normed")
        s_xr = sem("x1_set")
        s_xst = sem("x_kept")
        s_y = sem("y_final")
        s_yh = sem("y_high")
        s_yl = sem("y_low")
        s_ymx = sem("y_max")
        s_ysc = sem("y_scale")
        s_zero = sem("silu_pad_zeroed")
        xkeep = nc.dram_tensor("x_with_position", [TOK, D], F32, kind="Internal").ap()

        def x_ready(eng, j):
            if j == 0:
                eng.wait_ge(s_x[0], 16)
            else:
                eng.wait_ge(s_posd, j)

        def x_src(j):
            return x_prompt[0] if j == 0 else x_sample[0, P * (j - 1):P * j, :]

        def block_parts(b):
            t0, t1 = TBW * b, TBW * b + TBW
            return [(1, slice(0, CTX)), (0, slice(CTX, t1))] if b == 0 else [(0, slice(t0, t1))]

        def stage_waits(eng, c):
            if c < 2:
                return
            old = chunks[c - 2] if c - 2 < ff_chunk else None
            if old is not None and old[0] == "ada":
                A.take(eng, old)
            else:
                n = split_of[old] + 1 if old is not None else c - 2 - ff_chunk + ff_split + 1
                eng.wait_ge(s_wlo, n)

        def chunk_src(ch):
            if ch[0] == "ada":
                c0 = D * ch[1] + CW * ch[2]
                return w_ada[0].rearrange("(k p) n -> p k n", p=P)[:, :, c0:c0 + CW], CW
            if ch[0] == "win":
                return w_in[0].rearrange("(k p) n -> p k n", p=P)[:, :, ch[1]:ch[1] + ch[2]], ch[2]
            rows = w_out[0, 512 * ch[1]:512 * ch[1] + 512, 512 * ch[2]:512 * ch[2] + 512]
            return rows.rearrange("(k p) n -> p k n", p=P), 512

        def staged(c, w):
            return stage[c % 2][:, 0:(2048 // (CW if w <= CW else 512)) * w].rearrange("p (k n) -> p k n", n=w)

        def load_chunk(eng, c):
            src, w = chunk_src(chunks[c])
            stage_waits(eng, c)
            eng.dma_start(staged(c, w), src).then_inc(s_stage[c % 2], 16)

        w1_v = w_fc1[0].rearrange("(k p) n -> p k n", p=P)
        w2_v = w_fc2[0].rearrange("(g k p) n -> g p k n", k=FT, p=P)

        def load_ff(eng, rel, src, t=0):
            c = ff_chunk + rel
            if rel < 2:
                stage_waits(eng, c)
            else:
                eng.wait_ge(s_wlo, ff_split + rel - 2 + 1 + 8 * t)
            w = src.shape[-1]
            eng.dma_start(stage[c % 2][:].rearrange("p (k n) -> p k n", n=w), src).then_inc(s_stage[c % 2], 16)

        def chunk_no(i):
            return chunk_of[splits[i]] if i < ff_split else ff_chunk + i - ff_split

        def wait_staged(eng, i, t=0):
            c = chunk_no(i)
            eng.wait_ge(s_stage[c % 2], 16 * (c // 2 + 1) + 64 * t)
            return stage[c % 2][:, 0:8 * splits[i][2]] if i < len(zin) else stage[c % 2][:]

        def rooms(i):
            if i in (len(zin) + 2, len(zin) + 3):
                return wo_late[i - len(zin) - 2]
            return whi[i % 2][:], wlo[i % 2][:]

        def pair(i):
            n = 8 * splits[i][2] if i < len(zin) else 2048
            w = splits[i][2] if i < len(zin) else (512 if i < ff_split or (i - ff_split) in w2_rel else CW)
            return [x[:, 0:n].rearrange("p (k n) -> p k n", n=w) for x in rooms(i)]

        def last_use(i):
            if i < len(zin):
                return A, z_uses(i)[-1]
            if i < ff_split:
                return A, ("wo", i - len(zin), NT - 1)
            r = i - ff_split
            if r < 2:
                return A, A0 + 6 * r + 5
            if r >= 4 * NG - 2:
                return B, B0 + UB * (NG - 1) + NT * (r - 4 * NG + 2) + NT - 1
            g, x = (r - 2) // 4, (r - 2) % 4
            return (A, A0 + UA * (g + 1) + 6 * x + 5) if x < 2 else (B, B0 + UB * g + NT * (x - 2) + NT - 1)

        def wait_used(eng, i, t=0):
            ring, key = last_use(i)
            b, n, _ = ring.spot(key)
            eng.wait_ge(ring.full[b], n + (6 if ring is A else 12) * t)

        def chunk_max(dve, i, t=0):
            src = wait_staged(dve, i, t)
            nc.vector.tensor_reduce(wmax[:, i % 8:i % 8 + 1], src, AX_X, ALU.max, apply_absolute_value=True).then_inc(s_wmax, 1)

        def chunk_high(act, i, t=0):
            if i in (len(zin) + 2, len(zin) + 3):
                B.take(act, ("o", b_order[-1]))
            elif i in (ff_split, ff_split + 1):
                wait_used(act, i - 4)
            elif i >= 2:
                wait_used(act, i - 2, 0 if i - ff_split == 3 else t)
            act.wait_ge(s_wscl, i + 1 + 8 * t)
            src = wait_staged(act, i, t)
            n = src.shape[-1]
            nc.scalar.activation(rooms(i)[0][:, 0:n], src, ACT.Copy, scale=wscl[:, i % 8:i % 8 + 1]).then_inc(s_whi, 1)

        def chunk_low(dve, i, t=0):
            dve.wait_ge(s_whi, i + 1 + 8 * t)
            src = stage[chunk_no(i) % 2][:, 0:8 * splits[i][2] if i < len(zin) else 2048]
            n = src.shape[-1]
            hi, lo = rooms(i)
            nc.vector.scalar_tensor_tensor(out=lo[:, 0:n], in0=src, scalar=wscl[:, i % 8:i % 8 + 1], in1=hi[:, 0:n], op0=ALU.mult, op1=ALU.subtract).then_inc(s_wlo, 1)

        block = ctx.enter_context(nc.Block())

        @block.sync
        def _(sp):
            sp.dma_start(consts[:], a["k_consts"]).then_inc(s_const, 16)
            for row, src in ((R_C, a["c"][0]), (R_CTX, a["c_ctx"]), (R_GPM, a["g_pre_mix"][0]), (R_GPF, a["g_pre_mlp"][0]),
                             (R_SHM, a["b_ada"][0, 0:D]), (R_SCM, a["b_ada"][0, D:2 * D]),
                             (R_SHF, a["b_ada"][0, SH_F * D:SH_F * D + D]), (R_SCF, a["b_ada"][0, SC_F * D:SC_F * D + D]),
                             (R_GTM, a["b_ada"][0, GT_M * D:GT_M * D + D]), (R_GTF, a["b_ada"][0, GT_F * D:GT_F * D + D]),
                             (R_PM, a["g_post_mix"][0]), (R_PF, a["g_post_mlp"][0])):
                sp.dma_start(vrow[row:row + 8, :], src.rearrange("(k p) -> k p", p=P)).then_inc(s_vec, 16)
            sp.dma_start(vrow[R_BA:R_BA + 2 * HK, :], a["b_a2"][0].rearrange("d (k p) -> (d k) p", p=P)).then_inc(s_vec, 16)

            def load_x(j):
                sp.dma_start(x1[:, j, :], x_src(j)).then_inc(s_x[j], 16)

            def load_ada(n):
                src, w = chunk_src(ada1[n])
                sp.dma_start(ada_room[n].rearrange("p (k n) -> p k n", n=w), src).then_inc(s_ada[n], 16)

            for what, n in start:
                if what == "x":
                    load_x(n)
                elif what == "rows":
                    load_ada(n)
                if (what, n) == ("rows", 0):
                    sp.dma_start(posc, a["k_pos_col"]).then_inc(s_pos, 16)
                    rows = a["k_pos_row"].rearrange("(j r) n -> r j n", r=2)
                    for r in range(2):
                        sp.dma_start(posr[64 * r:64 * r + 64], rows[r].partition_broadcast(64)).then_inc(s_pos, 16)
                if (what, n) == ("x", NT - 1):
                    load_chunk(sp, 0)
            load_chunk(sp, 1)
            sp.dma_start(ghb[:], a["g_head"][0].rearrange("h v -> (h v)").partition_broadcast(P)).then_inc(s_misc, 16)
            sp.wait_ge(s_wa2, 1)
            for d in range(2):
                sp.dma_start(wa2[RANK * d:RANK * d + RANK, 256 * d:256 * d + 256], a["w_a2"][0, d]).then_inc(s_misc, 16)
            for j in range(NT):
                x_ready(sp, j)
                sp.dma_start(xkeep[P * j:P * j + P, :], x1[:, j, :]).then_inc(s_xst, 16)
            for c in range(2, len(zin)):
                load_chunk(sp, c)
            sp.wait_ge(s_qk, 8)
            for d, name in enumerate(("state_gla_fwd", "state_gla_bwd")):
                sp.dma_start(Sst[:, d], a[name][0, 0].rearrange("(k h) d v -> (h d) k v", k=HK)).then_inc(s_state, 16)
            A.take(sp, z_uses(len(zin) - 1)[-1])
            sp.dma_start(dftC, a["k_dft_cos"].rearrange("(m p) n -> p m n", p=P)).then_inc(s_dft, 16)
            sp.dma_start(dftS, a["k_dft_sin"].rearrange("(m p) n -> p m n", p=P)).then_inc(s_dft, 16)
            sp.dma_start(alt_row, a["k_alt"]).then_inc(s_dft, 16)
            for c in range(len(zin), len(zin) + N_FWD + N_FOU):
                load_chunk(sp, c)
            for d, out in enumerate((out_sf, out_sb)):
                for k in range(HK):
                    A.wait_read(sp, ("U", d, 0, k))
                sp.dma_start(out[0, 0].rearrange("(k h) d v -> (h d) k v", k=HK), Sctx[d]).then_inc(s_sout, 16)
            for c in range(len(zin) + N_FWD + N_FOU, ff_chunk):
                load_chunk(sp, c)
            B.take(sp, ("o", b_order[-1]))
            sp.wait_ge(s_xst, 16 * NT)
            for j in range(NT):
                sp.dma_start(x1[:, j, :], xkeep[P * j:P * j + P, :]).then_inc(s_x1[j], 16)
            load_ff(sp, 0, w1_v[:, :, 0:CW])
            load_ff(sp, 1, w1_v[:, :, CW:2 * CW])

            def group(g, t):
                for x in range(2):
                    load_ff(sp, 4 * g + 2 + x, w1_v[:, :, bass.ds(t * (2 * GFF) + GFF * (g + 1) + CW * x, CW)], t)
                for n in range(2):
                    down = w2_v[bass.ds(t * 2 + g, 1), :, :, 512 * n:512 * n + 512].rearrange("a p k n -> p (a k) n")
                    load_ff(sp, 4 * g + 4 + n, down, t)

            with sp.Fori(0, NG // 2 - 1) as t:
                group(0, t)
                group(1, t)
            group(NG - 2, 0)
            for n in range(2):
                load_ff(sp, 4 * NG - 2 + n, w2_v[NG - 1, :, :, 512 * n:512 * n + 512])
            for j in range(NT):
                sp.wait_ge(s_y, j + 1)
                sp.dma_start(out_p[0] if j == 0 else out_s[0, P * (j - 1):P * j, :], x1[:, j, :]).then_inc(s_out, 16)
            sp.wait_ge(s_sout, 32)
            sp.wait_ge(s_out, 16 * NT)

        @block.gpsimd
        def _(pool):
            own = Steps(pool, s_pool)
            nc.gpsimd.memset(slq[:], 0.0).then_inc(s_zero, 1)
            own.did(nc.gpsimd.memset(neg[:, 0:4], -0.5))
            own.did(nc.gpsimd.memset(neg[:, 4:5], -1.0))
            own.settle()

            def power(out, src, exponent, done=None):
                ins = nc.gpsimd.tensor_tensor(out, src, exponent, ALU.pow)
                if done is not None:
                    ins.then_inc(done, 1)
                else:
                    own.did(ins)
                    own.settle()

            def step(ins):
                own.did(ins)
                own.settle()

            def h_scale(n):
                pool.wait_ge(s_hmx, 2 * (n + 1))
                step(nc.gpsimd.partition_all_reduce(hmx[n][:, 1:3], hmx[n][:, 1:3], P, RMAX))
                step(nc.gpsimd.tensor_tensor(hmx[n][:, 0:1], hmx[n][:, 1:2], hmx[n][:, 2:3], ALU.add))
                step(nc.gpsimd.tensor_scalar(hinv[n], hmx[n][:, 0:1], D ** 0.5 / TOP, TINY, ALU.mult, ALU.max))
                if n == 0:
                    chunk_factor(0)
                power(hscl[n], hinv[n], neg[:, 4:5], s_hsc)

            def chunk_inverse(i, t=0):
                c = slice(i % 8, i % 8 + 1)
                pool.wait_ge(s_wmax, i + 1 + 8 * t)
                step(nc.gpsimd.partition_all_reduce(wall[:, c], wmax[:, c], P, RMAX))
                step(nc.gpsimd.tensor_scalar(winv[:, c], wall[:, c], 1.0 / TOP, TINY, ALU.mult, ALU.max))

            def chunk_factor(i, done=None):
                c = slice(i % 8, i % 8 + 1)
                if i < len(zin):
                    other, factor = hinv[0], DK ** -0.5 if i == Q else 1.0
                else:
                    half = wout[i - len(zin)][1]
                    other, factor = yinv[:, half:half + 1], 1.0
                ins = nc.gpsimd.tensor_scalar(wcof[:, c], winv[:, c], other, factor, ALU.mult, ALU.mult)
                if done is not None:
                    ins.then_inc(done, 1)
                else:
                    step(ins)

            def chunk_scale(i, factor=True):
                c = slice(i % 8, i % 8 + 1)
                chunk_inverse(i)
                if factor:
                    chunk_factor(i)
                power(wscl[:, c], winv[:, c], neg[:, 4:5], s_wscl)

            def ff_up_scale(g, x, t=0):
                i = w1_split(g, x)
                c = slice(i % 8, i % 8 + 1)
                chunk_inverse(i, t)
                power(wscl[:, c], winv[:, c], neg[:, 4:5], s_wscl)
                if x == 1:
                    b = g % 2
                    first = w1_split(g, 0) % 8
                    p = slice(b, b + 1)
                    step(nc.gpsimd.tensor_scalar(fmx[:, p], winv[:, first:first + 1], winv[:, c], None, ALU.max))
                    power(frg[:, p], fmx[:, p], neg[:, 4:5])
                    step(nc.gpsimd.tensor_scalar(ftm[:, p], fmx[:, p], hinv[1], 1.0 / F_ALPHA, ALU.mult, ALU.mult))
                    step(nc.gpsimd.tensor_tensor(finv[:, p], ftm[:, p], ftm[:, p], ALU.mult))
                    step(nc.gpsimd.tensor_scalar(beta[:, 2 * b:2 * b + 1], winv[:, first:first + 1], frg[:, p], F_ALPHA,
                                                 ALU.mult, ALU.mult))
                    nc.gpsimd.tensor_scalar(beta[:, 2 * b + 1:2 * b + 2], winv[:, c], frg[:, p], F_ALPHA,
                                            ALU.mult, ALU.mult).then_inc(s_beta, 1)

            def ff_down_scale(i, g, t=0):
                c = slice(i % 8, i % 8 + 1)
                chunk_inverse(i, t)
                step(nc.gpsimd.tensor_tensor(wcof[:, c], winv[:, c], finv[:, g % 2:g % 2 + 1], ALU.mult))
                power(wscl[:, c], winv[:, c], neg[:, 4:5], s_wscl)

            def rstd(out, mean, sums, n, done):
                if sums.shape[-1] == 2 * out.shape[-1]:
                    step(nc.gpsimd.tensor_tensor(mean, sums[:, 0:1], sums[:, 1:2], ALU.add))
                    sums = mean
                step(nc.gpsimd.tensor_scalar(mean, sums, 1.0 / n, EPS, ALU.mult, ALU.add))
                power(out, mean, neg[:, 0:out.shape[-1]], done)

            def x_rstd(j):
                pool.wait_ge(s_ssq, 2 * (j + 1))
                rstd(rst[:, j:j + 1], sqs[:, j:j + 1], ssq[:, 2 * j:2 * j + 2], D, s_rst)

            def y_scale(half):
                p = slice(half, half + 1)
                pool.wait_ge(s_ymx, 2 - half)
                step(nc.gpsimd.partition_all_reduce(yall[:, p], ymx[:, p], P, RMAX))
                step(nc.gpsimd.tensor_scalar(yinv[:, p], yall[:, p], 1.0 / TOP, TINY, ALU.mult, ALU.max))
                power(yscl[:, p], yinv[:, p], neg[:, 4:5], s_ysc)

            for j in range(NT):
                x_rstd(j)
            chunk_scale(0, False)
            A.take(pool, ada1[6])
            nc.gpsimd.memset(wa2, 0.0).then_inc(s_wa2, 1)
            h_scale(0)
            for i in range(1, len(zin)):
                chunk_scale(i)
            for s, j in enumerate(b_order):
                for h in range(HEADS):
                    A.wait_read(pool, ("At", j, h))
                    if s >= 2 and h == 0:
                        B.take(pool, ("o", b_order[s - 2]))
                    nc.gpsimd.tensor_tensor(ATb[:, s % 2, h, :], Am[:, h, 0:P], Am[:, h, P:2 * P], ALU.add).then_inc(s_at, 1)
                if s >= 1:
                    jj = b_order[s - 1]
                    pool.wait_ge(s_oss, HEADS * s)
                    rstd(ors[:, 4 * jj:4 * jj + 4], ors[:, 4 * jj:4 * jj + 4], oss[:, 4 * jj:4 * jj + 4], DV, s_ors)
                if s == 0:
                    y_scale(1)
                if s == 5:
                    h_scale(1)
                    chunk_scale(len(zin), False)
                    chunk_scale(len(zin) + 1, False)
                if s == 8:
                    chunk_scale(len(zin) + 2, False)
            jj = b_order[-1]
            pool.wait_ge(s_oss, HEADS * NT)
            rstd(ors[:, 4 * jj:4 * jj + 4], ors[:, 4 * jj:4 * jj + 4], oss[:, 4 * jj:4 * jj + 4], DV, s_ors)
            chunk_scale(len(zin) + 3, False)
            y_scale(0)
            for c in range(4):
                chunk_factor(len(zin) + c, s_cof if c == 3 else None)
            for s in range(NT + 1):
                if s == 4:
                    ff_up_scale(0, 0)
                if s < NT:
                    pool.wait_ge(s_pss, 2 * (s + 1))
                    rstd(prs[:, s:s + 1], psm[:, s:s + 1], pss[:, 2 * s:2 * s + 2], D, s_prs)
                if s >= 1:
                    j = s - 1
                    pool.wait_ge(s_qss, 2 * (j + 1))
                    rstd(qrs[:, j:j + 1], qsm[:, j:j + 1], qss[:, 2 * j:2 * j + 2], D, s_qrs)
            A.take(pool, ("wo", 3, NT - 1))
            nc.gpsimd.memset(acc, 0.0).then_inc(s_accz, 1)
            ff_up_scale(0, 1)
            ff_up_scale(1, 0)

            def group(g, t):
                ff_up_scale(g + 1, 1, t)
                for n in range(2):
                    ff_down_scale(ff_split + 4 * g + 4 + n, g, t)
                if g + 2 < NG:
                    ff_up_scale(g + 2, 0, t)

            for t in range(NG // 2 - 1):
                group(0, t)
                group(1, t)
            group(NG - 2, 0)
            for n in range(2):
                ff_down_scale(ff_split + 4 * NG - 2 + n, NG - 1)
            for j in range(NT):
                pool.wait_ge(s_fss, 2 * (j + 1))
                rstd(frs[:, j:j + 1], fsm[:, j:j + 1], fss[:, 2 * j:2 * j + 2], D, s_frs)

        @block.scalar
        def _(act):
            own = Steps(act, s_act)

            squared = {}
            last_squares = []

            def squares(src, out2, done, width=512):
                for h in range(src.shape[-1] // width):
                    if last_squares:
                        act.wait_ge(last_squares[-1], squared[last_squares[-1].name])
                    nc.scalar.activation(junk[:, 0:width], src[:, width * h:width * h + width], ACT.Square,
                                         accum_out=out2[:, h:h + 1]).then_inc(done, 1)
                    squared[done.name] = squared.get(done.name, 0) + 1
                    last_squares.append(done)

            A.wait_read(act, "vec")
            nc.scalar.activation(sil, vT[:, 0:16], ACT.Exp, scale=-1.0).then_inc(s_sexp, 1)

            def mod_part(n, c):
                bank = A.take(act, c)
                if n >= 2:
                    B.take(act, ("mod", mods[n - 2]))
                nc.scalar.activation(part[n % 2][:], bank[:, 0:CW], ACT.Copy).then_inc(A.read(c), 1)

            mods = ada1 + ada2

            def norm_x(j):
                act.wait_ge(s_rst, j + 1)
                if j >= 2:
                    B.take(act, ("xT", j - 2, 1))
                nc.scalar.activation(xh[j % 2], x1[:, j, :], ACT.Copy, scale=rst[:, j:j + 1]).then_inc(s_xh, 1)

            def square_x(j):
                x_ready(act, j)
                squares(x1[:, j, :], ssq[:, 2 * j:2 * j + 2], s_ssq)

            square_x(0)
            norm_x(0)
            square_x(1)
            for what, n in start:
                if what == "x":
                    if n + 2 < NT:
                        square_x(n + 2)
                    if n + 1 < NT:
                        norm_x(n + 1)
                elif what == "rows":
                    mod_part(n, ada1[n])
            chunk_high(act, 0)
            for h in range(2):
                B.wait_read(act, ("xT", NT - 1, h))
            B.wait_read(act, ("xT", NT - 2, 1))
            act.wait_ge(s_gn, 1)

            for b in range(TB):
                for h in range(2):
                    for k in (4 * h + 2, 4 * h + 3):
                        for v, toks in block_parts(b):
                            c = 2 * k + v
                            own.did(nc.scalar.activation(xT[:, k, toks], xT[:, k, toks], ACT.Identity,
                                                         scale=amul[0][:, c:c + 1], bias=shf[0][:, c:c + 1]))
                    own.settle()
                    act.wait_ge(s_mv, 2 * b + h + 1)
                    t_ = (slice(None), slice(4 * h, 4 * h + 4), slice(TBW * b, TBW * b + TBW))
                    nc.scalar.activation(HTh[t_], xT[t_], ACT.Copy).then_inc(s_th, 1)

            def take_z(key):
                return A.take(act, key)

            def evac_t(i, dst):
                for key in z_uses(i):
                    _, _, m, t = key
                    bank = take_z(key)
                    nc.scalar.activation(dst[:, m, TBW * t:TBW * t + TBW], bank[:, 0:TBW], ACT.Copy,
                                         scale=wcof[:, i % 8:i % 8 + 1]).then_inc(A.read(key), 1)

            def decay_logs(k):
                for d in range(2):
                    for t in range(TB):
                        B.wait_read(act, ("la", d, k, t))
                    own.did(nc.scalar.activation(tmp[2 * d + 1], tmp[2 * d], ACT.Abs))
                own.settle()
                for d in range(2):
                    own.did(nc.scalar.activation(tmp[2 * d + 1], tmp[2 * d + 1], ACT.Exp, scale=-1.0))
                own.settle()
                for d in range(2):
                    nc.scalar.activation(tmp[2 * d + 1], tmp[2 * d + 1], ACT.Ln, bias=1.0).then_inc(s_dln, 1)

            def decay_exps(k):
                for d in range(2):
                    act.wait_ge(s_de, 2 * k + d + 1)
                    own.did(nc.scalar.activation(wexp[2 * d + k], wexp[2 * d + k], ACT.Exp, scale=1.0 / TAU))
                    nc.scalar.activation(tmp[2 * d + 1], tmp[2 * d], ACT.Exp, scale=1.0 / TAU).then_inc(s_dexp, 1)
                    act.wait_ge(s_dexp, 4 * k + 2 * d + 1)
                    nc.scalar.activation(tmp[2 * d], tmp[2 * d], ACT.Exp, scale=-1.0 / TAU).then_inc(s_dexp, 1)

            for i in range(len(zin)):
                if i + 1 < ff_split and i + 1 < len(zin):
                    chunk_high(act, i + 1)
                if i == LR:
                    for key in z_uses(i):
                        bank = take_z(key)
                        t = key[3]
                        nc.scalar.activation(lrS[:, TBW * t:TBW * t + TBW], bank[0:2 * RANK, 0:TBW], ACT.Copy,
                                             scale=wcof[0:2 * RANK, i % 8:i % 8 + 1]).then_inc(A.read(key), 1)
                elif i == Q:
                    evac_t(i, qT)
                elif i == K:
                    decay_logs(0)
                    evac_t(i, kT)
                elif i == U_A:
                    decay_exps(0)
                    evac_t(i, uT[:, 0:2, :])
                elif i == U_B:
                    decay_logs(1)
                    evac_t(i, uT[:, 2:4, :])
                elif i in (V_A, V_B):
                    if i == V_A:
                        decay_exps(1)
                    for key in z_uses(i):
                        bank = take_z(key)
                        nc.scalar.activation(vN[:, key[3], CW * (i - V_A):CW * (i - V_A) + CW], bank[:, 0:CW], ACT.Copy,
                                             scale=wcof[:, i % 8:i % 8 + 1]).then_inc(A.read(key), 1)
                else:
                    act.wait_ge(s_qk, 8)
                    x = i - G_A
                    for key in z_uses(i):
                        bank = take_z(key)
                        j = key[3]
                        r = NT * x + j
                        g, e = gN[:, j, CW * x:CW * x + CW], gex[r % 3][:]
                        nc.scalar.activation(g, bank[:, 0:CW], ACT.Copy,
                                             scale=wcof[:, i % 8:i % 8 + 1]).then_inc(A.read(key), 1)
                        if r >= 3:
                            act.wait_ge(s_gs, r - 2)
                        A.wait_read(act, key)
                        own.did(nc.scalar.activation(e, g, ACT.Exp, scale=-1.0))
                        own.settle()
                        own.did(nc.scalar.activation(e, e, ACT.Ln, bias=1.0))
                        own.settle()
                        nc.scalar.activation(e, e, ACT.Exp, scale=-1.0).then_inc(s_gsg, 1)

            def ada_parts(n):
                if n == 0:
                    act.wait_ge(s_gs, 2 * NT)
                if n < len(ada2):
                    mod_part(len(ada1) + n, ada2[n])

            def copy_kn(n, key, ukeys):
                bank = B.take(act, key)
                if n >= 2:
                    A.take(act, ukeys[n - 2])
                nc.scalar.activation(kn[n % 2], bank[:, 0:P], ACT.Copy).then_inc(B.read(key), 1)

            kn_keys = [k for k in b_keys if k[0] == "kn"]
            u_keys = [k for k in a_keys if k[0] == "U"]
            n_fwd = HK * (NT - 1)
            for n in range(n_fwd):
                copy_kn(n, kn_keys[n], u_keys)
                if n % HK == HK - 1:
                    ada_parts(n // HK)

            for i in range(4):
                bank = A.take(act, ("dA", i))
                nc.scalar.activation(AB[:, i, :], bank[:], ACT.Copy).then_inc(A.read(("dA", i)), 1)
            bank = A.take(act, ("dA", 4))
            nc.scalar.activation(A512, bank[0:1, 0:4 * NCOS], ACT.Copy).then_inc(A.read(("dA", 4)), 1)
            bank = A.take(act, ("dA", 5))
            nc.scalar.activation(Y2b, bank[:], ACT.Copy).then_inc(A.read(("dA", 5)), 1)

            def put_y(i):
                bank = B.take(act, ("Y1", i))
                c0 = 0 if i < 0 else CTX + P * i
                nc.scalar.activation(yT[:, 4:8, c0:c0 + P], bank[:].rearrange("p (g t) -> p g t", g=GROUPS),
                                     ACT.Copy).then_inc(B.read(("Y1", i)), 1)
                if i < 0:
                    return
                bank = B.take(act, ("Y2", i))
                first = 1 if i == 0 else 0
                c1 = CTX + LAT - P * i - first
                nc.scalar.activation(yT[:, 4:8, c1:c1 - (P - first):-1],
                                     bank[:].rearrange("p (g t) -> p g t", g=GROUPS)[:, :, first:P],
                                     ACT.Copy).then_inc(B.read(("Y2", i)), 1)

            for i in range(-1, 4):
                bank = A.take(act, ("Q", i))
                if i >= 0:
                    A.wait_read(act, ("P", i - 1))
                nc.scalar.activation(Qs[:, 0:4 * NSIN], bank[:, 0:4 * NSIN], ACT.Copy).then_inc(A.read(("Q", i)), 1)
                ada_parts(N_FWD + 1 + i)
                if i >= 0:
                    put_y(i - 1)
            put_y(3)
            bank = B.take(act, ("Y1", 4))
            nc.scalar.activation(yT[:, 4:8, CTX + FOLD:CTX + FOLD + 1], bank[:, 0:4].rearrange("p (g t) -> p g t", g=GROUPS),
                                 ACT.Copy).then_inc(B.read(("Y1", 4)), 1)

            n = [n_fwd]

            def scores(j):
                if j != 1:
                    for k in range(HK):
                        copy_kn(n[0], kn_keys[n[0]], u_keys)
                        n[0] += 1

            def put_o(j):
                bank = B.take(act, ("oT", j))
                nc.scalar.activation(yT[:, 0:4, P * j:P * j + P], bank[:].rearrange("p (g t) -> p g t", g=HEADS),
                                     ACT.Copy).then_inc(B.read(("oT", j)), 1)

            scores(b_order[0])
            for s, j in enumerate(b_order):
                if s + 1 < NT:
                    scores(b_order[s + 1])
                bank = B.take(act, ("o", j))
                squares(bank[:], oss[:, 4 * j:4 * j + 4], s_oss, DV)
                if s >= 1:
                    put_o(b_order[s - 1])
                ada_parts(N_FWD + N_FOU + s)
                if s == 6:
                    chunk_high(act, len(zin))
                    chunk_high(act, len(zin) + 1)
            put_o(b_order[-1])

            def high_y(j):
                for half in (1, 0):
                    act.wait_ge(s_ysc, 2 - half)
                    nc.scalar.activation(YTh[:, 4 * half:4 * half + 4, P * j:P * j + P],
                                         yT[:, 4 * half:4 * half + 4, P * j:P * j + P],
                                         ACT.Copy, scale=yscl[:, half:half + 1]).then_inc(s_yh, 1)

            def put_even(j):
                if j == 0:
                    act.wait_ge(s_cof, 1)
                if j >= 4:
                    B.take(act, ("x2", j - 4, 1))
                for c in (0, 2):
                    key = ("wo", c, j)
                    bank = A.take(act, key)
                    i = len(zin) + c
                    nc.scalar.activation(yN[:, j % 4, 256 * c:256 * c + 512], bank[:], ACT.Copy,
                                         scale=wcof[:, i % 8:i % 8 + 1]).then_inc(A.read(key), 1)

            def put_gates(q):
                key = ("gate", q)
                bank = B.take(act, key)
                nc.scalar.activation(gates[:, q // 4, q // 2 % 2, 512 * (q % 2):512 * (q % 2) + 512], bank[:],
                                     ACT.Copy).then_inc(B.read(key), 1)

            def squares_y(j):
                for c in (1, 3):
                    A.wait_read(act, ("wo", c, j))
                squares(yN[:, j % 4, :], pss[:, 2 * j:2 * j + 2], s_pss)

            def squares_x1(j):
                act.wait_ge(s_xr, j + 1)
                squares(x1[:, j, :], qss[:, 2 * j:2 * j + 2], s_qss)

            def norm_x1(j):
                act.wait_ge(s_qrs, j + 1)
                nc.scalar.activation(yN[:, j % 4, :], x1[:, j, :], ACT.Copy, scale=qrs[:, j:j + 1]).then_inc(s_2x, 1)

            def high_2(j):
                for h in range(2):
                    B.wait_read(act, ("x2", j, h))
                    nc.scalar.activation(HT2h[:, 4 * h:4 * h + 4, P * j:P * j + P],
                                         tb2[h].rearrange("p (k t) -> p k t", k=4), ACT.Copy).then_inc(s_2h, 1)

            act.wait_ge(s_sout, 32)
            high_y(0)
            chunk_high(act, len(zin) + 2)
            chunk_high(act, len(zin) + 3)
            high_y(1)
            for j in range(NT + 2):
                if j < NT:
                    put_even(j)
                    if j == 0:
                        B.wait_read(act, ("o", b_order[-1]))
                    if j < 2:
                        for q in range(4):
                            put_gates(4 * j + q)
                    squares_y(j)
                    if j + 2 < NT:
                        high_y(j + 2)
                if 1 <= j <= NT:
                    squares_x1(j - 1)
                    norm_x1(j - 1)
                if j == NT:
                    chunk_high(act, ff_split)
                if j >= 2:
                    high_2(j - 2)
            chunk_high(act, ff_split + 1)

            def up(g, x, t=0):
                for u in range(6):
                    r = 6 * x + u
                    tb_, m = u // 2, 2 * x + u % 2
                    n_ = 12 * g + r
                    key = A0 + UA * g + r
                    bank = A.take(act, key, 6 * t)
                    if r == 0:
                        act.wait_ge(s_beta, g + 1 + 2 * t)
                        if g >= 1:
                            B.take(act, B0 + UB * (g - 2) + UB - 1, 12 * t)
                    if n_ >= 2:
                        act.wait_ge(s_fq, n_ - 1 + 24 * t)
                        act.wait_ge(s_fh, n_ - 1 + 24 * t)
                    nc.scalar.activation(frel[:, n_ % 2, :], bank[:, 0:TBW], ACT.Relu,
                                         scale=beta[:, 2 * (g % 2) + x:2 * (g % 2) + x + 1]).then_inc(A.read(key), 1)
                    b, cnt, _ = A.spot(key)
                    act.wait_ge(A.free[b], cnt + 6 * t)
                    nc.scalar.activation(FTh[g % 2][:, m, TBW * tb_:TBW * tb_ + TBW], frel[:, n_ % 2, :],
                                         ACT.Square).then_inc(s_fh, 1)

            up(0, 0)
            chunk_high(act, ff_split + 2)
            up(0, 1)

            def group(g, t):
                for s in range(4):
                    if g == 0 and s == 0:
                        B.take(act, B0 - 1, 12 * t)
                    chunk_high(act, ff_split + 4 * g + 3 + s, t)
                    if s < 2:
                        up(g + 1, s, t)

            with act.Fori(0, NG // 2 - 1) as t:
                group(0, t)
                group(1, t)
            group(NG - 2, 0)
            chunk_high(act, ff_split + 4 * NG - 1)
            for j in range(NT):
                B.wait_read(act, B0 + UB * (NG - 1) + NT + j)
                squares(acc[:, j, :], fss[:, 2 * j:2 * j + 2], s_fss)

        @block.tensor
        def _(pe):
            def mm(out, lhsT, rhs, start, stop):
                return nc.tensor.matmul(out, lhsT, rhs, start=start, stop=stop, skip_group_check=True)

            def three(out, ks, lhs, rhs):
                (lh, ll), (rh, rl) = lhs, rhs
                terms = [(k, x) for k in ks for x in ((lh, rh), (lh, rl), (ll, rh))]
                for n, (k, (x, y)) in enumerate(terms):
                    ins = mm(out, x(k), y(k), n == 0, n == len(terms) - 1)
                return ins

            pe.wait_ge(s_const, 16)
            pe.wait_ge(s_vec, 16 * 13)
            bank = A.open(pe, "vec")
            nc.tensor.transpose(bank[:, 0:R_ALL], vrow[0:R_ALL, :], ident[0:R_ALL, 0:R_ALL]).then_inc(A.filled("vec"), 1)
            pe.wait_ge(s_slp, 1)
            mods = ada1 + ada2

            def mod_rows(c):
                if c in ada1:
                    pe.wait_ge(s_ada[ada1.index(c)], 16)
                    w = ada_room[ada1.index(c)].rearrange("p (k n) -> p k n", n=CW)
                else:
                    g = chunk_of[c]
                    pe.wait_ge(s_stage[g % 2], 16 * (g // 2 + 1))
                    w = staged(g, CW)
                bank = A.open(pe, c)
                for k in range(KT):
                    r = 32 * (k % 4)
                    ins = nc.tensor.matmul(bank[r:r + 32, 0:CW], slq[:, k, :], w[:, k, :], start=k < 4, stop=k >= 4,
                                           tile_position=(0, r), skip_group_check=True)
                ins.then_inc(A.filled(c), 1)

            def mod_out(n, c):
                A.wait_read(pe, c)
                key = ("mod", c)
                bank = B.open(pe, key)
                for m in range(2):
                    ins = mm(bank[:, 2 * m:2 * m + 2], part[n % 2][:, P * m:P * m + P], sel2, True, True)
                ins.then_inc(B.filled(key), 1)

            def ada_rows(n):
                for what, m in ada_step(n):
                    if what == "rows":
                        mod_rows(ada2[m])
                    else:
                        mod_out(len(ada1) + m, ada2[m])

            def turn(key, src, ready):
                ready()
                bank = B.open(pe, key)
                for k in range(4):
                    ins = nc.tensor.transpose(bank[:, P * k:P * k + P], src[:, P * k:P * k + P], ident)
                ins.then_inc(B.filled(key), 1)

            for what, n in start:
                if what == "x":
                    for h in range(2):
                        turn(("xT", n, h), xh[n % 2][:, 512 * h:512 * h + 512], lambda: pe.wait_ge(s_xh, n + 1))
                elif what == "rows":
                    mod_rows(ada1[n])
                else:
                    mod_out(n, ada1[n])

            def up_tile(ring_key, turns, i, m, t, Hh, Hl, mw=P):
                wh, wl = pair(i)
                bank = A.open(pe, ring_key, turns)
                toks = slice(TBW * t, TBW * t + TBW)
                return three(bank[0:mw, 0:TBW], range(KT),
                             (lambda k: wh[:, k, P * m:P * m + mw], lambda k: wl[:, k, P * m:P * m + mw]),
                             (lambda k: Hh[:, k, toks], lambda k: Hl[:, k, toks]))

            def row_tile(ring, ring_key, turns, i, j, ks, Hh, Hl, k0, w):
                wh, wl = pair(i)
                bank = ring.open(pe, ring_key, turns)
                toks = slice(P * j, P * j + P)
                return three(bank[:, 0:w], ks,
                             (lambda k: Hh[:, k0 + k, toks], lambda k: Hl[:, k0 + k, toks]),
                             (lambda k: wh[:, k, :], lambda k: wl[:, k, :]))

            def logits(k):
                pe.wait_ge(s_misc, 48)
                for t in range(TB):
                    A.wait_read(pe, ("z", LR, 0, t))
                for d in range(2):
                    for t in range(TB):
                        key = ("la", d, k, t)
                        bank = B.open(pe, key)
                        mm(bank[:, 0:TBW], wa2[:, 256 * d + P * k:256 * d + P * k + P], lrS[:, TBW * t:TBW * t + TBW],
                           True, True).then_inc(B.filled(key), 1)

            for i in range(len(zin)):
                pe.wait_ge(s_wlo, i + 1)
                for n, key in enumerate(z_uses(i)):
                    if i in TFORM:
                        _, _, m, t = key
                        if i == 0:
                            pe.wait_ge(s_tl, 2 * (t + 1))
                        ins = up_tile(key, 0, i, m, t, HTh, HTl, P if i != LR else 2 * RANK)
                    else:
                        ins = row_tile(A, key, 0, i, key[3], range(KT), HTh, HTl, 0, CW)
                    ins.then_inc(A.filled(key), 1)
                if i == Q:
                    logits(0)
                if i == U_A:
                    logits(1)

            def turn_k(d, j, k):
                key = ("kn", d, j, k)
                bank = B.open(pe, key)
                nc.tensor.transpose(bank[:, 0:P], kt_[d][k][:, P * j:P * j + P], ident).then_inc(B.filled(key), 1)

            def update(d, j, k):
                B.wait_read(pe, ("kn", d, j, k))
                key = ("U", d, j, k)
                n = u_keys.index(key)
                bank = A.open(pe, key)
                mm(bank[:, 0:2 * DV], kn[n % 2], vN[:, j, 2 * DV * k:2 * DV * k + 2 * DV], True, True).then_inc(A.filled(key), 1)

            u_keys = [k for k in a_keys if k[0] == "U"]
            A.wait_read(pe, z_uses(6)[-1])
            pe.wait_ge(s_qk, 8)
            for s, j in enumerate(f_order[:-1]):
                for k in range(HK):
                    turn_k(0, j, k)
                for k in range(HK):
                    update(0, j, k)
                ada_rows(s)

            pe.wait_ge(s_fold, 1)
            cosw, sinw = dft_ch[:, 0:NCOS], dft_ch[:, NCOS:P]
            for i in range(6):
                key = ("dA", i)
                bank = A.open(pe, key)
                for g in range(GROUPS):
                    if i < 4:
                        e, o = Ef[:, g, P * i:P * i + P], Of[:, g, P * i:P * i + P]
                    elif i == 4:
                        e, o = Ef[:, g, FOLD:FOLD + 1], None
                    else:
                        e = o = uT[:, g, 0:CTX]
                    ins = mm(bank[0:e.shape[-1], NCOS * g:NCOS * g + NCOS], e, cosw, True, True)
                    if o is not None:
                        c0 = GROUPS * NCOS + NSIN * g
                        ins = mm(bank[:, c0:c0 + NSIN], o, sinw, True, True)
                ins.then_inc(A.filled(key), 1)
            NP_, NQ_ = GROUPS * NCOS, GROUPS * NSIN
            pe.wait_ge(s_dft, 48)
            for i in range(4):
                A.wait_read(pe, ("dA", i))
            A.wait_read(pe, ("dA", 4))
            A.wait_read(pe, ("dA", 5))

            def turn_y(i):
                for b, y in (("Y1", Y1b), ("Y2", Y2b)):
                    if b == "Y2" and i < 0:
                        continue
                    turn((b, i), y, lambda: A.wait_read(pe, ("P", i)))

            for i in range(-1, 4):
                P_, Q_ = ("P", i), ("Q", i)
                bank = A.open(pe, P_)
                if i < 0:
                    ins = mm(bank[:, 0:NP_], dft_ctx[:, 0:P], Y2b[:, 0:NP_], True, True)
                else:
                    for m in range(4):
                        mm(bank[:, 0:NP_], dftC[:, m, P * i:P * i + P], AB[:, m, 0:NP_], m == 0, False)
                    ins = mm(bank[:, 0:NP_], alt_row, A512, False, True)
                ins.then_inc(A.filled(P_), 1)
                bank = A.open(pe, Q_)
                if i < 0:
                    ins = mm(bank[:, 0:NQ_], dft_ctx[:, P:2 * P], Y2b[:, NP_:512], True, True)
                else:
                    for m in range(4):
                        ins = mm(bank[:, 0:NQ_], dftS[:, m, P * i:P * i + P], AB[:, m, NP_:512], m == 0, m == 3)
                ins.then_inc(A.filled(Q_), 1)
                ada_rows(N_FWD + 1 + i)
                if i >= 0:
                    turn_y(i - 1)
            P_ = ("P", 4)
            bank = A.open(pe, P_)
            for m in range(4):
                mm(bank[0:1, 0:NP_], consts[:, C_ALT:C_ALT + 1], AB[:, m, 0:NP_], m == 0, False)
            mm(bank[0:1, 0:NP_], alt_row[:, 0:1], A512, False, True).then_inc(A.filled(P_), 1)
            turn_y(3)
            A.wait_read(pe, P_)
            key = ("Y1", 4)
            bank = B.open(pe, key)
            for g in range(GROUPS):
                ins = mm(bank[:, g:g + 1], Y1b[0:1, P * g:P * g + P], ident[0:1, 0:1], True, True)
            ins.then_inc(B.filled(key), 1)

            def scores(j):
                if j != 1:
                    for k in range(HK):
                        turn_k(1, j, k)
                for h in range(HEADS):
                    key = ("At", j, h)
                    bank = A.open(pe, key)
                    rows = slice(DK * (h % 2), DK * (h % 2) + DK)
                    for d in range(2):
                        ins = mm(bank[:, P * d:P * d + P], kt_[d][h // 2][rows, P * j:P * j + P],
                                 qt[d][h // 2][rows, P * j:P * j + P], True, True)
                    ins.then_inc(A.filled(key), 1)
                if j != 1:
                    for k in range(HK):
                        update(1, j, k)

            def outputs(s, j):
                key = ("o", j)
                pe.wait_ge(s_at, HEADS * (s + 1))
                if j > 0:
                    pe.wait_ge(s_srf, HK * j)
                    pe.wait_ge(s_srb, HK * s)
                bank = B.open(pe, key)
                for k in range(HK):
                    both = slice(2 * DV * k, 2 * DV * k + 2 * DV)
                    if j > 0:
                        mm(bank[:, both], qt[0][k][:, P * j:P * j + P], Srf[:, j - 1, k, :], True, False)
                        mm(bank[:, both], qt[1][k][:, P * j:P * j + P], Srb[:, s % 3, k, :], False, False)
                    for h in (2 * k, 2 * k + 1):
                        ins = mm(bank[:, DV * h:DV * h + DV], ATb[:, s % 2, h, :], vN[:, j, DV * h:DV * h + DV],
                                 j == 0, True)
                ins.then_inc(B.filled(key), 1)

            def turn_o(s, j):
                turn(("oT", j), yo[:, s % 2, :], lambda: B.wait_read(pe, ("o", j)))

            scores(b_order[0])
            for s, j in enumerate(b_order):
                if s + 1 < NT:
                    scores(b_order[s + 1])
                outputs(s, j)
                if s >= 1:
                    turn_o(s - 1, b_order[s - 1])
                if N_FWD + N_FOU + s <= len(ada2):
                    ada_rows(N_FWD + N_FOU + s)
            turn_o(NT - 1, b_order[-1])

            def turn_x(j):
                for h in range(2):
                    turn(("x2", j, h), yN[:, j % 4, 512 * h:512 * h + 512], lambda: pe.wait_ge(s_2x, j + 1))

            def spread_gates(q):
                key = ("gate", q)
                pe.wait_ge(s_dg, q + 1)
                bank = B.open(pe, key)
                for k in range(4):
                    ins = mm(bank[:, P * k:P * k + P], ones, tb2[q % 2][:, P * k:P * k + P], True, True)
                ins.then_inc(B.filled(key), 1)

            for j in range(NT):
                pe.wait_ge(s_yl, 2 * (j + 1))
                for c in range(4):
                    i = len(zin) + c
                    half = wout[c][1]
                    if j == 0:
                        pe.wait_ge(s_wlo, i + 1)
                    key = ("wo", c, j)
                    row_tile(A, key, 0, i, j, range(4), YTh, YTl, 4 * half, 512).then_inc(A.filled(key), 1)
                if j < 2:
                    for q in range(4):
                        spread_gates(4 * j + q)
                else:
                    turn_x(j - 2)

            def up(g, x, t=0):
                i = w1_split(g, x)
                pe.wait_ge(s_wlo, i + 1 + 8 * t)
                for u in range(6):
                    key = A0 + UA * g + 6 * x + u
                    if g == 0 and x == 0 and u % 2 == 0:
                        if u > 0:
                            turn_x(NT - 3 + u // 2)
                        pe.wait_ge(s_2l, 6 * (u // 2 + 1))
                    up_tile(key, 6 * t, i, u % 2, u // 2, HT2h, HT2l).then_inc(A.filled(key), 1)

            def down(i, g, n, t=0):
                pe.wait_ge(s_wlo, i + 1 + 8 * t)
                if n == 0:
                    pe.wait_ge(s_fl, 12 * (g + 1) + 24 * t)
                for j in range(NT):
                    key = B0 + UB * g + NT * n + j
                    row_tile(B, key, 12 * t, i, j, range(FT), FTh[g % 2], FTl[g % 2], 0, 512).then_inc(B.filled(key), 1)

            for x in range(2):
                up(0, x)

            def group(g, t):
                for x in range(2):
                    up(g + 1, x, t)
                for n in range(2):
                    down(ff_split + 4 * g + 4 + n, g, n, t)

            with pe.Fori(0, NG // 2 - 1) as t:
                group(0, t)
                group(1, t)
            group(NG - 2, 0)
            for n in range(2):
                down(ff_split + 4 * NG - 2 + n, NG - 1, n)

        @block.vector
        def _(dve):
            own = Steps(dve, s_dve)
            V = nc.vector

            def step(ins):
                own.did(ins)
                own.settle()

            bank = A.take(dve, "vec")
            V.tensor_copy(vT, bank[:, 0:R_ALL]).then_inc(A.read("vec"), 1)
            own.did(V.memset(ones, 1.0))
            A.wait_read(dve, "vec")
            dve.wait_ge(s_sexp, 1)
            step(V.tensor_scalar(sil, sil, 1.0, None, ALU.add))
            step(V.reciprocal(sil2, sil))
            dve.wait_ge(s_zero, 1)
            V.tensor_tensor(slq[:, :, 0:2], vT[:, 0:16].rearrange("p (v k) -> p k v", v=2),
                            sil2.rearrange("p (v k) -> p k v", v=2), ALU.mult).then_inc(s_slp, 1)

            def add_pos(j):
                dve.wait_ge(s_x[j], 16)
                if j == 1:
                    dve.wait_ge(s_pos, 48)
                own.did(V.tensor_tensor(x1[:, j, 0:512], x1[:, j, 0:512], posr[:, j - 1, :], ALU.add))
                V.tensor_tensor(x1[:, j, 512:D], x1[:, j, 512:D], posc, ALU.add).then_inc(s_posd, 1)

            def mod_cols(c):
                bank = B.take(dve, ("mod", c))
                dst = {SH_M: shf[0], SC_M: amul[0], GT_M: gtc[0], SH_F: shf[1], SC_F: amul[1], GT_F: gtc[1]}[c[1]]
                dst = dst.rearrange("p (k v) -> p k v", v=2)
                row = {SH_M: R_SHM, SC_M: R_SCM, GT_M: R_GTM, SH_F: R_SHF, SC_F: R_SCF, GT_F: R_GTF}[c[1]] + 2 * c[2]
                V.tensor_tensor(dst[:, 2 * c[2]:2 * c[2] + 2, :], bank[:, 0:4].rearrange("p (k v) -> p k v", v=2),
                                vT[:, row:row + 2].unsqueeze(2).to_broadcast([P, 2, 2]), ALU.add).then_inc(B.read(("mod", c)), 1)
                B.wait_read(dve, ("mod", c))

            def finish_gains(norm, row):
                view = amul[norm].rearrange("p (k v) -> p k v", v=2)
                step(V.scalar_tensor_tensor(out=view, in0=view, scalar=1.0,
                                            in1=vT[:, row:row + 8].unsqueeze(2).to_broadcast([P, 8, 2]),
                                            op0=ALU.add, op1=ALU.mult))
                V.tensor_reduce(hmx[norm][:, 1:2], amul[norm], AX_X, ALU.max, apply_absolute_value=True).then_inc(s_hmx, 1)
                V.tensor_reduce(hmx[norm][:, 2:3], shf[norm], AX_X, ALU.max, apply_absolute_value=True).then_inc(s_hmx, 1)

            def scale_gains(norm):
                dve.wait_ge(s_hsc, norm + 1)
                own.did(V.tensor_scalar(amul[norm], amul[norm], hscl[norm], None, ALU.mult))
                step(V.tensor_scalar(shf[norm], shf[norm], hscl[norm], None, ALU.mult))

            def put_x(j):
                for h in range(2):
                    key = ("xT", j, h)
                    bank = B.take(dve, key)
                    V.tensor_copy(xT[:, 4 * h:4 * h + 4, P * j:P * j + P],
                                  bank[:].rearrange("p (k t) -> p k t", k=4)).then_inc(B.read(key), 1)

            add_pos(1)
            for what, n in start:
                if what == "x":
                    if n + 2 < NT:
                        add_pos(n + 2)
                    put_x(n)
                elif what == "out":
                    mod_cols(ada1[n])
                    if n == 4:
                        chunk_max(dve, 0)
            finish_gains(0, R_GPM)
            scale_gains(0)
            V.tensor_copy(hgo, hscl[0]).then_inc(s_gn, 1)

            def modulate(key, norm, j, h, buf):
                bank = B.take(dve, key)
                v = 1 if j == 0 else 0
                for k in range(4):
                    c = 2 * (4 * h + k) + v
                    ins = V.tensor_scalar(buf[:, P * k:P * k + P], bank[:, P * k:P * k + P], amul[norm][:, c:c + 1],
                                          shf[norm][:, c:c + 1], ALU.mult, ALU.add)
                    if k < 3:
                        own.did(ins)
                ins.then_inc(B.read(key), 1)

            def low_h(high_done, low_done, hi, lo, j, h, buf):
                dve.wait_ge(high_done, 2 * j + h + 1)
                tile_ = (slice(None), slice(4 * h, 4 * h + 4), slice(P * j, P * j + P))
                V.tensor_tensor(lo[tile_], buf.rearrange("p (k t) -> p k t", k=4), hi[tile_], ALU.subtract).then_inc(low_done, 1)

            def gain_x(b, h):
                for k in (4 * h, 4 * h + 1):
                    for v, toks in block_parts(b):
                        c = 2 * k + v
                        ins = V.tensor_scalar(xT[:, k, toks], xT[:, k, toks], amul[0][:, c:c + 1], shf[0][:, c:c + 1],
                                              ALU.mult, ALU.add)
                        if k % 4 == 0 or v == 1:
                            own.did(ins)
                ins.then_inc(s_mv, 1)

            def low_x(b, h):
                dve.wait_ge(s_th, 2 * b + h + 1)
                t_ = (slice(None), slice(4 * h, 4 * h + 4), slice(TBW * b, TBW * b + TBW))
                V.tensor_tensor(HTl[t_], xT[t_], HTh[t_], ALU.subtract).then_inc(s_tl, 1)

            halves = [(b, h) for b in range(TB) for h in range(2)]
            for h in range(2):
                B.wait_read(dve, ("xT", NT - 1, h))
            B.wait_read(dve, ("xT", NT - 2, 1))
            gain_x(0, 0)
            gain_x(0, 1)
            for r, (b, h) in enumerate(halves):
                low_x(b, h)
                if r == 0:
                    chunk_low(dve, 0)
                if r + 2 < len(halves):
                    gain_x(*halves[r + 2])
                if r == 1:
                    chunk_max(dve, 1)

            def decay_bias(k):
                for d in range(2):
                    for t in range(TB):
                        key = ("la", d, k, t)
                        bank = B.take(dve, key)
                        r = R_BA + HK * d + k
                        V.tensor_scalar(tmp[2 * d][:, TBW * t:TBW * t + TBW], bank[:, 0:TBW], vT[:, r:r + 1], None,
                                        ALU.add).then_inc(B.read(key), 1)

            def decay_sums(k):
                for d in range(2):
                    x, c = tmp[2 * d], tmp[2 * d + 1]
                    dve.wait_ge(s_dln, 2 * k + d + 1)
                    step(V.scalar_tensor_tensor(out=x, in0=x, scalar=0.0, in1=c, op0=ALU.min, op1=ALU.subtract))
                    for j in range(NT):
                        part_ = slice(P * j, P * j + P) if d == 0 else slice(P * j + P - 1, P * j - 1 if j else None, -1)
                        own.did(V.tensor_tensor_scan(c[:, part_], ones, x[:, part_], 0.0, ALU.mult, ALU.add))
                    own.settle()
                    last, mid = (P - 1, P // 2 - 1) if d == 0 else (0, P // 2)
                    w = wexp[2 * d + k]
                    cv = c.rearrange("p (j t) -> p j t", t=P)
                    own.did(V.tensor_copy(w[:, 0:NT], cv[:, :, last]))
                    own.did(V.tensor_copy(w[:, 2 * NT:3 * NT], cv[:, :, mid]))
                    own.settle()
                    own.did(V.tensor_tensor(w[:, NT:2 * NT], w[:, 0:NT], w[:, 2 * NT:3 * NT], ALU.subtract))
                    step(V.tensor_tensor(x.rearrange("p (j t) -> p j t", t=P), cv,
                                         w[:, 2 * NT:3 * NT].unsqueeze(2).to_broadcast([P, NT, P]), ALU.subtract))
                    V.tensor_scalar(x, x, CLAMP, -CLAMP, ALU.min, ALU.max).then_inc(s_de, 1)

            def decay_q_k(k):
                for i in (Q, K):
                    for key in z_uses(i):
                        A.wait_read(dve, key)
                if k == 0:
                    dve.wait_ge(s_xst, 16 * NT)
                for d in range(2):
                    dve.wait_ge(s_dexp, 4 * k + 2 * d + 1)
                    V.tensor_tensor(qt[d][k], qT[:, k, :], tmp[2 * d + 1], ALU.mult).then_inc(s_qk, 1)
                    dve.wait_ge(s_dexp, 4 * k + 2 * d + 2)
                    V.tensor_tensor(kt_[d][k], kT[:, k, :], tmp[2 * d], ALU.mult).then_inc(s_qk, 1)
                dve.wait_ge(s_qk, 4 * k + 4)

            def fold():
                for i in (U_A, U_B):
                    for key in z_uses(i):
                        A.wait_read(dve, key)
                up_ = uT[:, :, CTX + 1:CTX + FOLD]
                down_ = uT[:, :, CTX + LAT - 1:CTX + FOLD:-1]
                own.did(V.tensor_tensor(Ef[:, :, 1:FOLD], up_, down_, ALU.add))
                own.did(V.tensor_tensor(Of[:, :, 1:FOLD], up_, down_, ALU.subtract))
                own.did(V.tensor_copy(Ef[:, :, 0:FOLD + 1:FOLD], uT[:, :, CTX:CTX + FOLD + 1:FOLD]))
                V.memset(Of[:, :, 0:1], 0.0).then_inc(s_fold, 1)


            def silu_gate(x):
                cs = slice(CW * x, CW * x + CW)
                for j in range(NT):
                    r = NT * x + j
                    dve.wait_ge(s_gsg, r + 1)
                    g = gN[:, j, cs]
                    V.tensor_tensor(g, g, gex[r % 3][:], ALU.mult).then_inc(s_gs, 1)
                    dve.wait_ge(s_gs, r + 1)
                    own.did(V.tensor_tensor(g, g, ghb[:, cs], ALU.mult))

            for i in range(len(zin)):
                if i + 2 < len(zin):
                    chunk_max(dve, i + 2)
                if i + 1 < len(zin):
                    chunk_low(dve, i + 1)
                if i == Q:
                    decay_bias(0)
                elif i == K:
                    decay_sums(0)
                elif i == U_A:
                    decay_q_k(0)
                    decay_bias(1)
                elif i == U_B:
                    decay_sums(1)
                elif i == V_A:
                    decay_q_k(1)
                elif i == V_B:
                    fold()
                elif i in (G_A, G_B):
                    if i == G_A:
                        dve.wait_ge(s_misc, 48)
                    silu_gate(i - G_A)
            own.settle()

            def blocks(out, S, w, done=None):
                own.did(V.tensor_scalar(out[0:DK, 0:DV], S[0:DK, :], w[0:DK, :], None, ALU.mult))
                V.tensor_scalar(out[DK:P, DV:2 * DV], S[DK:P, :], w[DK:P, :], None, ALU.mult).then_inc(done, 1)

            def absorb(d, j, k):
                key = ("U", d, j, k)
                w = wexp[2 * d + k]
                bank = A.take(dve, key)
                dst = Sctx[d][:, k, :] if j == 0 else tU[k]
                own.did(V.tensor_scalar(dst[0:DK, :], bank[0:DK, 0:DV], w[0:DK, NT + j:NT + j + 1], None, ALU.mult))
                V.tensor_scalar(dst[DK:P, :], bank[DK:P, DV:2 * DV], w[DK:P, NT + j:NT + j + 1], None,
                                ALU.mult).then_inc(A.read(key), 1)
                if j > 0:
                    A.wait_read(dve, key)
                    own.settle()
                    step(V.scalar_tensor_tensor(out=Sst[:, d, k, :], in0=Sst[:, d, k, :], scalar=w[:, j:j + 1], in1=tU[k],
                                                op0=ALU.mult, op1=ALU.add))

            step(V.memset(Srf, 0.0))
            dve.wait_ge(s_state, 32)
            for k in range(HK):
                blocks(Srf[:, 0, k, :], Sst[:, 0, k, :], wexp[k][:, 2 * NT + 1:2 * NT + 2], s_srf)
            def ada_sums(n):
                for what, m in ada_step(n):
                    if what == "out":
                        mod_cols(ada2[m])

            for s, j in enumerate(f_order[:-1]):
                if s >= 1:
                    ada_sums(s - 1)
                for k in range(HK):
                    absorb(0, j, k)
                    if j > 0:
                        blocks(Srf[:, j, k, :], Sst[:, 0, k, :], wexp[k][:, 2 * NT + j + 1:2 * NT + j + 2], s_srf)

            def groups(y):
                return y.rearrange("p (g c) -> p g c", g=GROUPS)

            ada_sums(N_FWD - 1)
            for i in range(-1, 4):
                key = ("P", i)
                bank = A.take(dve, key)
                A.wait_read(dve, ("Q", i))
                if i >= 0:
                    B.take(dve, ("Y1", i - 1))
                if i >= 1:
                    B.take(dve, ("Y2", i - 1))
                p, q = groups(bank[:, 0:GROUPS * NCOS]), groups(Qs[:, 0:GROUPS * NSIN])
                outs = [(groups(Y1b), ALU.subtract, ALU.add)] + ([(groups(Y2b), ALU.add, ALU.subtract)] if i >= 0 else [])
                for n, (y, low, high) in enumerate(outs):
                    own.did(V.tensor_tensor(y[:, :, 1:64], p[:, :, 1:64], q, low))
                    own.did(V.tensor_tensor(y[:, :, P - 1:64:-1], p[:, :, 1:64], q, high))
                    ins = V.tensor_copy(y[:, :, 0:NCOS:64], p[:, :, 0:NCOS:64])
                    if n < len(outs) - 1:
                        own.did(ins)
                ins.then_inc(A.read(key), 1)
                ada_sums(N_FWD + 1 + i)
            key = ("P", 4)
            bank = A.take(dve, key)
            B.take(dve, ("Y1", 3))
            p, y = groups(bank[0:1, 0:GROUPS * NCOS]), groups(Y1b[0:1, :])
            own.did(V.tensor_copy(y[:, :, 0:NCOS], p))
            V.tensor_copy(y[:, :, P - 1:64:-1], p[:, :, 1:64]).then_inc(A.read(key), 1)

            def y_max(half):
                V.tensor_reduce(ymx[:, half:half + 1], R7[:, 4608 * half:4608 * half + 4608], AX_X, ALU.max,
                                apply_absolute_value=True).then_inc(s_ymx, 1)

            B.wait_read(dve, ("Y1", 4))
            y_max(1)

            step(V.memset(Srb, 0.0))

            def scores(s, j):
                for h in range(HEADS):
                    key = ("At", j, h)
                    bank = A.take(dve, key)
                    if s >= 1:
                        dve.wait_ge(s_at, HEADS * (s - 1) + h + 1)
                    V.tensor_tensor(Am[:, h, :], bank[:, 0:2 * P], masks, ALU.mult).then_inc(A.read(key), 1)
                if j == 1:
                    return
                nxt = b_order[s + 1]
                for k in range(HK):
                    absorb(1, j, k)
                    if k == 0 and s >= 2:
                        B.take(dve, ("o", b_order[s - 2]))
                    blocks(Srb[:, (s + 1) % 3, k, :], Sst[:, 1, k, :], wexp[2 + k][:, 2 * NT + nxt:2 * NT + nxt + 1], s_srb)

            def gate_o(s, j):
                key = ("o", j)
                bank = B.take(dve, key)
                dve.wait_ge(s_ors, s + 1)
                if s >= 2:
                    B.take(dve, ("oT", b_order[s - 2]))
                for h in range(HEADS):
                    hv = slice(DV * h, DV * h + DV)
                    ins = V.scalar_tensor_tensor(out=yo[:, s % 2, hv], in0=bank[:, hv], scalar=ors[:, 4 * j + h:4 * j + h + 1],
                                                 in1=gN[:, j, hv], op0=ALU.mult, op1=ALU.mult)
                    if h < HEADS - 1:
                        own.did(ins)
                ins.then_inc(B.read(key), 1)

            def y_max_tile(j):
                B.wait_read(dve, ("oT", j))
                own.did(V.tensor_reduce(ymt[:, j:j + 1], yT[:, 0:4, P * j:P * j + P], AX_XY, ALU.max, apply_absolute_value=True))

            def finish_gates(g, row):
                view = gtc[g].rearrange("p (k v) -> p k v", v=2)
                own.did(V.tensor_tensor(view, view, vT[:, row:row + 8].unsqueeze(2).to_broadcast([P, 8, 2]), ALU.mult))

            w0 = len(zin)
            scores(0, b_order[0])
            for s, j in enumerate(b_order):
                if s + 1 < NT:
                    scores(s + 1, b_order[s + 1])
                gate_o(s, j)
                if s >= 2:
                    y_max_tile(b_order[s - 2])
                if N_FWD + N_FOU + s <= len(ada2):
                    ada_sums(N_FWD + N_FOU + s)
                if s == 4:
                    finish_gates(0, R_PM)
                    finish_gates(1, R_PF)
                    finish_gains(1, R_GPF)
                    chunk_max(dve, w0)
                    chunk_max(dve, w0 + 1)
                if s == 6:
                    scale_gains(1)
                    chunk_low(dve, w0)
                if s == 7:
                    chunk_low(dve, w0 + 1)
                    chunk_max(dve, w0 + 2)
            chunk_max(dve, w0 + 3)
            y_max_tile(b_order[-2])
            y_max_tile(b_order[-1])
            own.settle()
            V.tensor_reduce(ymx[:, 0:1], ymt, AX_X, ALU.max).then_inc(s_ymx, 1)

            def low_y(j):
                for half in (1, 0):
                    dve.wait_ge(s_yh, 2 * j + 2 - half)
                    t_ = (slice(None), slice(4 * half, 4 * half + 4), slice(P * j, P * j + P))
                    V.scalar_tensor_tensor(out=YTl[t_], in0=yT[t_], scalar=yscl[:, half:half + 1], in1=YTh[t_],
                                           op0=ALU.mult, op1=ALU.subtract).then_inc(s_yl, 1)

            def diagonals(q):
                g, v, h = q // 4, q // 2 % 2, q % 2
                if q >= 2:
                    B.take(dve, ("gate", q - 2))
                for k in range(4):
                    c = 2 * (4 * h + k) + v
                    ins = V.tensor_scalar(tb2[q % 2][:, P * k:P * k + P], ident, gtc[g][:, c:c + 1], None, ALU.mult)
                    if k < 3:
                        own.did(ins)
                ins.then_inc(s_dg, 1)

            def put_odd(j):
                for c in (1, 3):
                    key = ("wo", c, j)
                    bank = A.take(dve, key)
                    A.wait_read(dve, ("wo", c - 1, j))
                    i = w0 + c
                    y = yN[:, j % 4, 256 * (c - 1):256 * (c - 1) + 512]
                    V.scalar_tensor_tensor(out=y, in0=bank[:], scalar=wcof[:, i % 8:i % 8 + 1], in1=y, op0=ALU.mult,
                                           op1=ALU.add).then_inc(A.read(key), 1)

            def post(j):
                if j < 2:
                    for q in range(4):
                        B.wait_read(dve, ("gate", q))
                dve.wait_ge(s_prs, j + 1)
                v = 1 if j == 0 else 0
                y = yN[:, j % 4, :]
                step(V.scalar_tensor_tensor(out=y, in0=y, scalar=prs[:, j:j + 1], in1=gates[:, 0, v, :],
                                            op0=ALU.mult, op1=ALU.mult))
                dve.wait_ge(s_x1[j], 16)
                V.tensor_tensor(x1[:, j, :], x1[:, j, :], y, ALU.add).then_inc(s_xr, 1)

            def modulate(key, norm, j, h, buf):
                bank = B.take(dve, key)
                v = 1 if j == 0 else 0
                for k in range(4):
                    c = 2 * (4 * h + k) + v
                    ins = V.tensor_scalar(buf[:, P * k:P * k + P], bank[:, P * k:P * k + P], amul[norm][:, c:c + 1],
                                          shf[norm][:, c:c + 1], ALU.mult, ALU.add)
                    if k < 3:
                        own.did(ins)
                ins.then_inc(B.read(key), 1)

            def modulate_2(j):
                for h in range(2):
                    if j >= 1:
                        dve.wait_ge(s_2l, 2 * (j - 1) + h + 1)
                    modulate(("x2", j, h), 1, j, h, tb2[h])
                for h in range(2):
                    B.wait_read(dve, ("x2", j, h))
                    dve.wait_ge(s_2h, 2 * j + h + 1)
                    tile_ = (slice(None), slice(4 * h, 4 * h + 4), slice(P * j, P * j + P))
                    V.tensor_tensor(HT2l[tile_], tb2[h].rearrange("p (k t) -> p k t", k=4), HT2h[tile_],
                                    ALU.subtract).then_inc(s_2l, 1)

            own.settle()
            low_y(0)
            chunk_low(dve, w0 + 2)
            chunk_low(dve, w0 + 3)
            low_y(1)
            F = ff_split
            for j in range(NT + 2):
                if j < 2:
                    for q in range(4):
                        diagonals(4 * j + q)
                if j < NT:
                    put_odd(j)
                    if j + 2 < NT:
                        low_y(j + 2)
                if 1 <= j <= NT:
                    post(j - 1)
                if j == 3:
                    chunk_max(dve, F)
                if j == NT:
                    chunk_low(dve, F)
                if j >= 2:
                    modulate_2(j - 2)
            chunk_max(dve, F + 1)

            def up(g, x, t=0):
                for u in range(6):
                    r = 6 * x + u
                    n = 12 * g + r
                    key = A0 + UA * g + r
                    tb_, m = u // 2, 2 * x + u % 2
                    A.wait_read(dve, key, 6 * t)
                    if n >= 2:
                        dve.wait_ge(s_fl, n - 1 + 24 * t)
                    V.tensor_tensor(fsq[:, n % 2, :], frel[:, n % 2, :], frel[:, n % 2, :], ALU.mult).then_inc(s_fq, 1)
                    dve.wait_ge(s_fq, n + 1 + 24 * t)
                    dve.wait_ge(s_fh, n + 1 + 24 * t)
                    toks = slice(TBW * tb_, TBW * tb_ + TBW)
                    V.tensor_tensor(FTl[g % 2][:, m, toks], fsq[:, n % 2, :], FTh[g % 2][:, m, toks],
                                    ALU.subtract).then_inc(s_fl, 1)

            def down(i, g, n, t=0, then=None):
                cof = wcof[:, i % 8:i % 8 + 1]
                for j in range(NT):
                    key = B0 + UB * g + NT * n + j
                    bank = B.take(dve, key, 12 * t)
                    B.wait_read(dve, key - UB, 12 * t)
                    y = acc[:, j, 512 * n:512 * n + 512]
                    V.scalar_tensor_tensor(out=y, in0=bank[:], scalar=cof, in1=y, op0=ALU.mult,
                                           op1=ALU.add).then_inc(B.read(key), 1)
                    if then is not None:
                        then(j)

            chunk_max(dve, F + 2)
            chunk_low(dve, F + 1)
            up(0, 0)
            chunk_max(dve, F + 3)
            chunk_low(dve, F + 2)
            up(0, 1)
            dve.wait_ge(s_accz, 1)

            def group(g, t):
                for s in range(4):
                    chunk_max(dve, F + 4 * g + 4 + s, t)
                    chunk_low(dve, F + 4 * g + 3 + s, t)
                    if s < 2:
                        up(g + 1, s, t)
                    else:
                        down(F + 4 * g + 4 + s - 2, g, s - 2, t)

            with dve.Fori(0, NG // 2 - 1) as t:
                group(0, t)
                group(1, t)
            group(NG - 2, 0)

            def finish(j):
                dve.wait_ge(s_frs, j + 1)
                v = 1 if j == 0 else 0
                step(V.scalar_tensor_tensor(out=acc[:, j, :], in0=acc[:, j, :], scalar=frs[:, j:j + 1], in1=gates[:, 1, v, :],
                                            op0=ALU.mult, op1=ALU.mult))
                V.tensor_tensor(x1[:, j, :], x1[:, j, :], acc[:, j, :], ALU.add).then_inc(s_y, 1)

            chunk_low(dve, F + 4 * NG - 1)
            down(F + 4 * NG - 2, NG - 1, 0)
            down(F + 4 * NG - 1, NG - 1, 1, 0, lambda j: finish(j - 2) if j >= 2 else None)
            finish(NT - 2)
            finish(NT - 1)


def _constants():
    import numpy as np
    i = np.arange(P)
    k = np.zeros((P, C_ALL), np.float64)
    k[:, C_ID:C_ID + P] = np.eye(P)
    k[:, C_MASK:C_MASK + P] = i[:, None] <= i[None, :]
    k[:, C_MASK + P:C_MASK + 2 * P] = i[:, None] >= i[None, :]
    for v in range(2):
        k[v::32, C_SEL2 + v] = 1.0
    turn = 2.0 * np.pi * (np.outer(i, i) % P) / P
    k[:, C_CH:C_CH + NCOS] = np.cos(turn)[:, 0:NCOS]
    k[:, C_CH + NCOS:C_CH + P] = np.sin(turn)[:, 1:64]
    k[:, C_CTX:C_CTX + P] = np.cos(turn) / P
    k[:, C_CTX + P:C_CTX + 2 * P] = np.sin(turn) / P
    unit = 1.0 / np.sqrt(LAT * P)
    k[:, C_ALT] = unit * (1.0 - 2.0 * (i % 2))
    m = np.arange(FOLD)
    turn = 2.0 * np.pi * (np.outer(m, m) % LAT) / LAT
    f = np.float32
    nf = D // 4
    omega = (f(1.0) / (f(10000.0) ** (np.arange(nf, dtype=f) / f(nf)))).astype(f)
    row, col = np.arange(LAT // 64, dtype=f)[:, None] * omega, (i % 64).astype(f)[:, None] * omega
    return {
        "k_consts": k.astype(f),
        "k_dft_cos": (unit * np.cos(turn)).astype(f),
        "k_dft_sin": (unit * np.sin(turn)).astype(f),
        "k_alt": (unit * (1.0 - 2.0 * (i % 2)))[None, :].astype(f),
        "k_pos_row": np.concatenate([np.sin(row), np.cos(row)], axis=1).astype(f),
        "k_pos_col": np.concatenate([np.sin(col), np.cos(col)], axis=1).astype(f),
    }


_INS = ["x_prompt", "x_sample", "state_gla_fwd", "state_gla_bwd", "c", "c_ctx", "w_in", "w_out", "w_a2", "b_a2",
        "g_head", "w_ada", "b_ada", "g_pre_mix", "g_post_mix", "g_pre_mlp", "g_post_mlp", "w_fc1", "w_fc2"]
_OUTS = [(1, CTX, D), (1, LAT, D), (1, 1, HEADS, DK, DV), (1, 1, HEADS, DK, DV)]


def kernel(**inputs):
    import numpy as _np
    import concourse.bacc as _bacc
    from concourse.bass_utils import run_bass_kernel_spmd as _run

    nc = _bacc.Bacc("TRN2", target_bir_lowering=False, num_devices=1)
    arrays, args = {}, {}
    for name, x in [(n, _np.ascontiguousarray(inputs[n])) for n in _INS] + list(_constants().items()):
        arrays[f"in_{name}"] = x
        args[name] = nc.dram_tensor(f"in_{name}", x.shape, F32, kind="ExternalInput").ap()
    for i, shape in enumerate(_OUTS):
        args[f"out_{i}"] = nc.dram_tensor(f"out_{i}_dram", shape, F32, kind="ExternalOutput").ap()
    hybrid_step(nc, args)
    r = _run(nc, [arrays], core_ids=[0])
    return tuple(r.results[0][f"out_{i}_dram"] for i in range(len(_OUTS)))
```

```python
from contextlib import ExitStack

import concourse.bass as bass
from concourse import mybir

ALU = mybir.AluOpType
ACT = mybir.ActivationFunctionType
AX_X = mybir.AxisListType.X
AX_XY = mybir.AxisListType.XY
F32 = mybir.dt.float32
F16 = mybir.dt.float16
RMAX = bass.bass_isa.ReduceOp.max

P = 128
D = 1024
KT = D // P
CTX = 128
LAT = 1024
TOK = CTX + LAT
NT = TOK // P
TB = 3
TBW = TOK // TB
HEADS, DK, DV = 4, 64, 128
HK = HEADS * DK // P
VW = HEADS * DV
RANK = 16
GROUPS = 4
FF = 4 * D
GFF = 512
NG = FF // GFF
FT = GFF // P
CW = 256
EPS = 1e-6
TAU = 16.0
CLAMP = 80.0 * TAU
NCOS, NSIN = 65, 63
FOLD = LAT // 2
TOP = 2.0 ** 15
TINY = 1e-30
F_ALPHA = 2.0 ** -28

Q0, K0, V0, G0 = 0, 256, 512, 1024
LR0 = 1536
U0 = LR0 + 2 * RANK
SH_M, SC_M, GT_M, SH_F, SC_F, GT_F = range(6)

C_ID, C_MASK, C_SEL2, C_CH, C_CTX, C_ALT = 0, 128, 384, 386, 514, 770
C_ALL = 771
SMALL = 784
R_C, R_CTX, R_GPM, R_GPF, R_BIAS, R_PM, R_PF, R_BA, R_ALL = 0, 8, 16, 24, 32, 80, 88, 96, 100
R_SHM, R_SCM, R_GTM, R_SHF, R_SCF, R_GTF = range(R_BIAS, R_BIAS + 48, 8)


class Ring:

    def __init__(self, banks, full, free, keys):
        self.banks, self.full, self.free, self.keys = banks, full, free, keys
        self.at = {k: i for i, k in enumerate(keys)}
        self.next = 0

    def spot(self, key, turns=0):
        i = self.at[key] if not isinstance(key, int) else key
        return i % len(self.banks), i // len(self.banks) + 1, turns

    def open(self, eng, key, turns=0):
        if not isinstance(key, int):
            assert self.at[key] == self.next, (key, self.keys[self.next])
            self.next += 1
        b, n, t = self.spot(key, turns)
        if n > 1:
            eng.wait_ge(self.free[b], n - 1 + t)
        return self.banks[b]

    def filled(self, key):
        return self.full[self.spot(key)[0]]

    def read(self, key):
        return self.free[self.spot(key)[0]]

    def take(self, eng, key, turns=0):
        b, n, t = self.spot(key, turns)
        eng.wait_ge(self.full[b], n + t)
        return self.banks[b]

    def wait_read(self, eng, key, turns=0):
        b, n, t = self.spot(key, turns)
        eng.wait_ge(self.free[b], n + t)


class Steps:

    def __init__(self, eng, sem):
        self.eng, self.sem, self.n = eng, sem, 0

    def did(self, ins):
        ins.then_inc(self.sem, 1)
        self.n += 1

    def settle(self):
        self.eng.wait_ge(self.sem, self.n)


def hybrid_step(nc, a):
    x_prompt, x_sample, w_in, w_out, w_ada, w_fc1, w_fc2 = (
        a[n] for n in ("x_prompt", "x_sample", "w_in", "w_out", "w_ada", "w_fc1", "w_fc2"))
    out_p, out_s, out_sf, out_sb = a["out_0"], a["out_1"], a["out_2"], a["out_3"]

    ada1 = [("ada", s, n) for s in (SH_M, SC_M) for n in range(D // CW)]
    zin = [("win", LR0, 2 * RANK), ("win", Q0, CW), ("win", K0, CW), ("win", U0, CW), ("win", U0 + CW, CW),
           ("win", V0, CW), ("win", V0 + CW, CW), ("win", G0, CW), ("win", G0 + CW, CW)]
    ada2 = [("ada", s, n) for s in (GT_M, SH_F, SC_F, GT_F) for n in range(D // CW)]
    wout = [("wout", part, n) for n in range(2) for part in (1, 0)]
    chunks = zin + ada2 + wout
    splits = zin + wout
    ff_chunk = len(chunks)
    ff_split = len(splits)
    chunk_of = {c: i for i, c in enumerate(chunks)}
    split_of = {c: i for i, c in enumerate(splits)}

    def w1_split(g, x):
        return ff_split + x if g == 0 else ff_split + 4 * g - 2 + x

    LR, Q, K, U_A, U_B, V_A, V_B, G_A, G_B = range(9)
    TFORM = (LR, Q, K, U_A, U_B)
    a_keys, b_keys = [], []
    a_keys.append("vec")
    start = []
    for what in "x0 a0 x1 a1 x2 x3 a2 x4 a3 x5 x6 a4 x7 x8 a5 a6 a7".split():
        n = int(what[1])
        start.append(("x" if what[0] == "x" else "rows", n))
        if what[0] == "a" and n >= 1:
            start.append(("out", n - 1))
    start.append(("out", len(ada1) - 1))
    for what, n in start:
        if what == "x":
            b_keys += [("xT", n, h) for h in range(2)]
        elif what == "rows":
            a_keys.append(ada1[n])
        else:
            b_keys.append(("mod", ada1[n]))

    def z_uses(i):
        if i == LR:
            return [("z", i, 0, t) for t in range(TB)]
        if i in TFORM:
            return [("z", i, m, t) for t in range(TB) for m in range(2)]
        return [("z", i, 0, j) for j in range(NT)]

    for i in range(G_A):
        a_keys += z_uses(i)
    b_keys += [("la", d, k, t) for k in range(HK) for d in range(2) for t in range(TB)]
    f_order = [0] + list(range(1, NT))
    b_order = [0] + list(range(NT - 1, 0, -1))

    def ada_step(n):
        return ([("rows", n)] if n < len(ada2) else []) + ([("out", n - 1)] if n >= 1 else [])

    def ada_keys(n):
        for what, m in ada_step(n):
            if what == "rows":
                a_keys.append(ada2[m])
            else:
                b_keys.append(("mod", ada2[m]))

    N_FWD, N_FOU = NT - 1, 5
    gate_events = []
    for r in range(2 * NT):
        gate_events.append(("z", r))
        if r % 2 == 1 and r // 2 < N_FWD:
            gate_events.append(("kn", r // 2))
        if r % 2 == 0 and 1 <= r // 2 <= N_FWD:
            gate_events.append(("U", r // 2 - 1))
    for what, n in gate_events:
        if what == "z":
            a_keys.append(("z", G_A + n // NT, 0, n % NT))
        elif what == "kn":
            b_keys.append(("kn", 0, f_order[n]))
        else:
            a_keys.append(("U", 0, f_order[n]))
            ada_keys(n)
    for i in range(4):
        a_keys.append(("dA", i))
    a_keys += [("dA", 4), ("dA", 5)]
    for i in range(-1, 4):
        a_keys += [("P", i), ("Q", i)]
        ada_keys(N_FWD + 1 + i)
        if i >= 0:
            b_keys += [("Y1", i - 1)] + ([("Y2", i - 1)] if i >= 1 else [])
    a_keys.append(("P", 4))
    b_keys += [("Y1", 3), ("Y2", 3), ("Y1", 4)]

    def gla_scores(j):
        if j != 1:
            b_keys.append(("kn", 1, j))
        a_keys.extend(("At", j, hp) for hp in range(HK))
        if j != 1:
            a_keys.append(("U", 1, j))

    gla_scores(b_order[0])
    for s, j in enumerate(b_order):
        if s + 1 < NT:
            gla_scores(b_order[s + 1])
        b_keys.append(("o", j))
        if s >= 1:
            b_keys.append(("oT", b_order[s - 1]))
        if N_FWD + N_FOU + s <= len(ada2):
            ada_keys(N_FWD + N_FOU + s)
    b_keys.append(("oT", b_order[-1]))
    for j in range(NT):
        a_keys += [("wo", c, j) for c in range(4)]
        if j >= 2:
            b_keys += [("x2", j - 2, h) for h in range(2)]
        if j < 2:
            b_keys += [("gate", 4 * j + q) for q in range(4)]
    for j in (NT - 2, NT - 1):
        b_keys += [("x2", j, h) for h in range(2)]
    A0, B0 = len(a_keys), len(b_keys)
    UA, UB = 2 * TB * 2, 2 * NT
    w2_rel = {4 * g + 4 + n for g in range(NG - 1) for n in range(2)} | {4 * NG - 2, 4 * NG - 1}

    with ExitStack() as ctx:
        def sb(name, shape, dt=F32):
            return ctx.enter_context(nc.sbuf_tensor(name, shape, dt))

        def sem(name):
            return ctx.enter_context(nc.semaphore(name))

        banks = [ctx.enter_context(nc.psum_tensor(f"bank{i}", [P, 512], F32)) for i in range(8)]
        A = Ring(banks[0:4], [sem(f"a_full{i}") for i in range(4)], [sem(f"a_free{i}") for i in range(4)], a_keys)
        B = Ring(banks[4:7], [sem(f"b_full{i}") for i in range(3)], [sem(f"b_free{i}") for i in range(3)], b_keys)
        junk = banks[7]

        R1 = sb("region1", [P, 9216])
        R2 = sb("region2", [P, 9216])
        R34 = sb("region34", [P, 9216])
        R5 = sb("region5", [P, 4608])
        R7 = sb("region7", [P, 9216])
        stage = [sb(f"stage{i}", [P, 2048]) for i in range(2)]
        whi = [sb(f"whi{i}", [P, 2048], F16) for i in range(2)]
        wlo = [sb(f"wlo{i}", [P, 2048], F16) for i in range(2)]

        consts = sb("consts", [P, C_ALL])
        small = sb("small", [P, SMALL])
        vrow = sb("vrow", [P, P])
        ones = vrow[:]
        part = [sb(f"part{i}", [P, CW]) for i in range(2)]
        slq = sb("slq", [P, KT, 32])
        ghb = sb("ghb", [P, VW])
        gex = sb("gex", [P, 2, CW])

        ident = consts[:, C_ID:C_ID + P]
        masks = consts[:, C_MASK:C_MASK + 2 * P]
        sel2 = consts[:, C_SEL2:C_SEL2 + 2]
        dft_ch = consts[:, C_CH:C_CH + P]
        dft_ctx = consts[:, C_CTX:C_CTX + 2 * P]

        used = [0]

        def cols(n):
            used[0] += n
            assert used[0] <= SMALL
            return small[:, used[0] - n:used[0]]

        vT = cols(R_ALL)
        sil, sil2 = cols(16), cols(16)
        shf = [cols(16) for _ in range(2)]
        amul = [cols(16) for _ in range(2)]
        hmx = [cols(3) for _ in range(2)]
        hinv, hscl = ([cols(1) for _ in range(2)] for _ in range(2))
        hgo = cols(1)
        neg = cols(5)
        ssq, sqs, rst = cols(2 * NT), cols(NT), cols(NT)
        wmax, wall, winv, wscl, wcof = (cols(8) for _ in range(5))
        fmx, frg, ftm, finv = (cols(2) for _ in range(4))
        beta = cols(4)
        ymx, yall, yinv, yscl = (cols(2) for _ in range(4))
        ymt, ymf = cols(NT), cols(GROUPS)
        gtc = [cols(16) for _ in range(2)]
        wexp = [cols(3 * NT) for _ in range(4)]
        oss, ors = cols(4 * NT), cols(4 * NT)
        pss, psm, prs = cols(2 * NT), cols(NT), cols(NT)
        qss, qsm, qrs = cols(2 * NT), cols(NT), cols(NT)
        fss, fsm, frs = cols(2 * NT), cols(NT), cols(NT)

        HTh = R1[:, 0:4608].bitcast(F16).rearrange("p (k t) -> p k t", k=KT)
        HTl = R1[:, 4608:9216].bitcast(F16).rearrange("p (k t) -> p k t", k=KT)
        YTh, YTl = HTh, HTl
        dftC = R1[:, 0:2048].rearrange("p (m n) -> p m n", m=4)
        dftS = R1[:, 2048:4096].rearrange("p (m n) -> p m n", m=4)
        AB = R1[:, 4096:6144].rearrange("p (m n) -> p m n", m=4)
        Y1b, Y2b, Qs = R1[:, 6144:6656], R1[:, 6656:7168], R1[:, 7168:7680]
        A512 = R1[0:1, 7680:7940]
        alt_row = R1[0:1, 7940:8068]
        ATb = R1[:, 0:1024].rearrange("p (b h t) -> p b h t", b=2, h=HEADS)
        Am = R1[:, 1024:2048].rearrange("p (h t) -> p h t", h=HEADS)
        Srb = R1[:, 4096:5632].rearrange("p (b k n) -> p b k n", b=3, k=HK)
        yo = R1[:, 3072:4096].rearrange("p (b n) -> p b n", b=2)

        qt = [[R2[:, 2304 * d + 1152 * k:2304 * d + 1152 * k + 1152] for k in range(HK)] for d in range(2)]
        kt_ = [[R2[:, 4608 + 2304 * d + 1152 * k:4608 + 2304 * d + 1152 * k + 1152] for k in range(HK)] for d in range(2)]
        x1 = R2[:].rearrange("p (j n) -> p j n", j=NT)

        qT = R34[:, 0:2304].rearrange("p (k t) -> p k t", k=HK)
        kT = R34[:, 2304:4608].rearrange("p (k t) -> p k t", k=HK)
        Srf = R34[:, 0:4096].rearrange("p (j k n) -> p j k n", j=NT - 1, k=HK)
        Sst = R34[:, 4096:4608].rearrange("p (d k n) -> p d k n", d=2, k=HK)
        vN = R34[:, 4608:9216].rearrange("p (j n) -> p j n", j=NT)
        ada_room = [R1[:, 2048 * i:2048 * i + 2048] for i in range(4)] + [R34[:, 2048 * i:2048 * i + 2048] for i in range(4)]
        xh = [R1[:, 8192:9216], R34[:, 8192:9216]]
        wo_late = [[R34[:, 2048 * b + 1024 * x:2048 * b + 1024 * x + 1024].bitcast(F16) for x in range(2)] for b in range(2)]
        yN = R34[:, 4608:4608 + 4096].rearrange("p (j n) -> p j n", j=4)
        FTh = [R34[:, 4608 * b:4608 * b + 2304].bitcast(F16).rearrange("p (f t) -> p f t", f=FT) for b in range(2)]
        FTl = [R34[:, 4608 * b + 2304:4608 * b + 4608].bitcast(F16).rearrange("p (f t) -> p f t", f=FT) for b in range(2)]

        gN = R5[:].rearrange("p (j n) -> p j n", j=NT)
        tmp = [R5[:, 1152 * i:1152 * i + 1152] for i in range(4)]
        posr = R5[:, 0:4096].rearrange("p (j n) -> p j n", j=NT - 1)
        posc = R5[:, 4096:4608]
        gates = R5[:, 0:4096].rearrange("p (g v n) -> p g v n", g=2, v=2)
        tb2 = [R5[:, 4096:4608], ghb[:]]
        diag = tb2 + [gex[:].rearrange("p b n -> p (b n)"), R34[:, 8704:9216]]
        frel = R5[:, 0:768].rearrange("p (b n) -> p b n", b=2)
        fsq = R5[:, 768:1536].rearrange("p (b n) -> p b n", b=2)

        uT = R7[:, 0:4608].rearrange("p (g t) -> p g t", g=GROUPS)
        Ef = R7[:, 4608:4608 + 4 * FOLD].rearrange("p (g t) -> p g t", g=GROUPS)
        Of = R7[:, 6656:6656 + 4 * FOLD].rearrange("p (g t) -> p g t", g=GROUPS)
        kn = [R7[:, 8704:8960], R1[:, 8068:8324]]
        Sctx = [r.rearrange("p (k n) -> p k n", k=HK) for r in (R7[:, 8960:9216], R1[:, 8324:8580])]
        yT = R7[:].rearrange("p (k t) -> p k t", k=KT)
        xT = yT
        HT2h = R7[:, 0:4608].bitcast(F16).rearrange("p (k t) -> p k t", k=KT)
        HT2l = R7[:, 4608:9216].bitcast(F16).rearrange("p (k t) -> p k t", k=KT)
        acc = R1[:].rearrange("p (j n) -> p j n", j=NT)

        wa2 = R34[0:2 * RANK, 4608:4608 + 512]
        lrS = R34[0:2 * RANK, 5120:5120 + TOK]

        s_2h = sem("h2_high")
        s_2l = sem("h2_low")
        s_2x = sem("x1_normed")
        s_accz = sem("ff_sums_zeroed")
        s_act = sem("act_steps")
        s_at = sem("scores_summed")
        s_cof = sem("w_out_factors_set")
        s_dg = sem("gate_diagonals")
        s_beta = sem("ff_scale_set")
        s_const = sem("consts_loaded")
        s_de = sem("decay_exponents")
        s_dexp = sem("decay_exps")
        s_dft = sem("dft_loaded")
        s_gsg = sem("gate_denominator")
        s_gh = sem("gate_times_gain")
        s_dln = sem("decay_log1p")
        s_dve = sem("dve_steps")
        s_fh = sem("f_high")
        s_fl = sem("f_low")
        s_fold = sem("u_folded")
        s_fq = sem("f_squared")
        s_frs = sem("f_rstd")
        s_fss = sem("f_squares")
        s_ge = sem("gate_exp")
        s_gn = sem("gains_scaled")
        s_gs = sem("gate_silu")
        s_hmx = sem("h_bound_parts")
        s_hsc = sem("h_scale_set")
        s_misc = sem("w_a2_g_head_loaded")
        s_ors = sem("o_rstd")
        s_oss = sem("o_squares")
        s_out = sem("outputs_stored")
        s_pool = sem("pool_steps")
        s_pos = [sem(f"positions{i}_loaded") for i in range(4)]
        s_ada = [sem(f"ada{i}_loaded") for i in range(len(ada1))]
        s_mv = sem("h_by_dve")
        s_posd = sem("pos_added")
        s_prs = sem("post_rstd")
        s_pss = sem("post_squares")
        s_qk = sem("decayed_q_k")
        s_qrs = sem("x1_rstd")
        s_qss = sem("x1_squares")
        s_rst = sem("x_rstd")
        s_sexp = sem("exp_c")
        s_slp = sem("silu_c_set")
        s_sout = sem("states_stored")
        s_srb = sem("bwd_state_blocks")
        s_srf = sem("fwd_state_blocks")
        s_srz = sem("bwd_blocks_zeroed")
        s_ssq = sem("x_squares")
        s_stage = [sem(f"stage{i}_loaded") for i in range(2)]
        s_state = sem("states_loaded")
        s_th = sem("h_high")
        s_tl = sem("h_low")
        s_vec = sem("vectors_loaded")
        s_wa2 = sem("wa2_zeroed")
        s_whi = sem("chunk_high")
        s_wlo = sem("chunk_low")
        s_wmax = sem("chunk_max")
        s_wscl = sem("chunk_scale")
        s_x = [sem(f"x{i}_loaded") for i in range(NT)]
        s_x1 = [sem(f"x1_{i}_loaded") for i in range(NT)]
        s_xh = sem("x_normed")
        s_xr = sem("x1_set")
        s_xst = sem("x_kept")
        s_y = sem("y_final")
        s_yh = sem("y_high")
        s_yl = sem("y_low")
        s_ymx = sem("y_max")
        s_ysc = sem("y_scale")
        s_zero = sem("silu_pad_zeroed")
        xkeep = nc.dram_tensor("x_with_position", [TOK, D], F32, kind="Internal").ap()

        def x_ready(eng, j):
            if j == 0:
                eng.wait_ge(s_x[0], 16)
            else:
                eng.wait_ge(s_posd, j)

        def x_src(j):
            return x_prompt[0] if j == 0 else x_sample[0, P * (j - 1):P * j, :]

        def block_parts(b):
            t0, t1 = TBW * b, TBW * b + TBW
            return [(1, slice(0, CTX)), (0, slice(CTX, t1))] if b == 0 else [(0, slice(t0, t1))]

        def stage_waits(eng, c):
            if c < 2:
                return
            old = chunks[c - 2] if c - 2 < ff_chunk else None
            if old is not None and old[0] == "ada":
                A.take(eng, old)
            else:
                n = split_of[old] + 1 if old is not None else c - 2 - ff_chunk + ff_split + 1
                eng.wait_ge(s_wlo, n)

        def chunk_src(ch):
            if ch[0] == "ada":
                c0 = D * ch[1] + CW * ch[2]
                return w_ada[0].rearrange("(k p) n -> p k n", p=P)[:, :, c0:c0 + CW], CW
            if ch[0] == "win":
                return w_in[0].rearrange("(k p) n -> p k n", p=P)[:, :, ch[1]:ch[1] + ch[2]], ch[2]
            rows = w_out[0, 512 * ch[1]:512 * ch[1] + 512, 512 * ch[2]:512 * ch[2] + 512]
            return rows.rearrange("(k p) n -> p k n", p=P), 512

        def staged(c, w):
            return stage[c % 2][:, 0:(2048 // (CW if w <= CW else 512)) * w].rearrange("p (k n) -> p k n", n=w)

        def load_chunk(eng, c):
            src, w = chunk_src(chunks[c])
            stage_waits(eng, c)
            eng.dma_start(staged(c, w), src).then_inc(s_stage[c % 2], 16)

        w1_v = w_fc1[0].rearrange("(k p) n -> p k n", p=P)
        w2_v = w_fc2[0].rearrange("(g k p) n -> g p k n", k=FT, p=P)

        def load_ff(eng, rel, src, t=0):
            c = ff_chunk + rel
            if rel < 2:
                stage_waits(eng, c)
            else:
                eng.wait_ge(s_wlo, ff_split + rel - 2 + 1 + 8 * t)
            w = src.shape[-1]
            eng.dma_start(stage[c % 2][:].rearrange("p (k n) -> p k n", n=w), src).then_inc(s_stage[c % 2], 16)

        def chunk_no(i):
            return chunk_of[splits[i]] if i < ff_split else ff_chunk + i - ff_split

        def wait_staged(eng, i, t=0):
            c = chunk_no(i)
            eng.wait_ge(s_stage[c % 2], 16 * (c // 2 + 1) + 64 * t)
            return stage[c % 2][:, 0:8 * splits[i][2]] if i < len(zin) else stage[c % 2][:]

        def pair(i):
            if i == ff_split:
                return [x[:, :, 0:CW] for x in (YTh, YTl)]
            n = 8 * splits[i][2] if i < len(zin) else 2048
            w = splits[i][2] if i < len(zin) else (512 if i < ff_split or (i - ff_split) in w2_rel else CW)
            late = i - len(zin) - 2
            rooms = wo_late[late] if late in (0, 1) else (whi[i % 2][:], wlo[i % 2][:])
            return [x[:, 0:n].rearrange("p (k n) -> p k n", n=w) for x in rooms]

        def last_use(i):
            if i < len(zin):
                return A, z_uses(i)[-1]
            if i < ff_split:
                return A, ("wo", i - len(zin), NT - 1)
            r = i - ff_split
            if r < 2:
                return A, A0 + 6 * r + 5
            if r >= 4 * NG - 2:
                return B, B0 + UB * (NG - 1) + NT * (r - 4 * NG + 2) + NT - 1
            g, x = (r - 2) // 4, (r - 2) % 4
            return (A, A0 + UA * (g + 1) + 6 * x + 5) if x < 2 else (B, B0 + UB * g + NT * (x - 2) + NT - 1)

        def wait_used(eng, i, t=0):
            ring, key = last_use(i)
            b, n, _ = ring.spot(key)
            eng.wait_ge(ring.full[b], n + (6 if ring is A else 12) * t)

        def chunk_max(dve, i, t=0):
            src = wait_staged(dve, i, t)
            nc.vector.tensor_reduce(wmax[:, i % 8:i % 8 + 1], src, AX_X, ALU.max, apply_absolute_value=True).then_inc(s_wmax, 1)

        def chunk_high(act, i, t=0):
            if i in (len(zin) + 2, len(zin) + 3):
                B.take(act, ("o", b_order[-1]))
            elif i == ff_split:
                A.take(act, ("wo", 3, 1))
            elif i in (ff_split + 1, ff_split + 2):
                wait_used(act, i - (4 if i == ff_split + 1 else 6))
            elif i >= 2:
                wait_used(act, i - 2, 0 if i - ff_split == 3 else t)
            act.wait_ge(s_wscl, i + 1 + 8 * t)
            src = wait_staged(act, i, t)
            hi = pair(i)[0]
            nc.scalar.activation(hi, src.rearrange("p (k n) -> p k n", n=hi.shape[-1]), ACT.Copy,
                                 scale=wscl[:, i % 8:i % 8 + 1]).then_inc(s_whi, 1)

        def chunk_low(dve, i, t=0):
            dve.wait_ge(s_whi, i + 1 + 8 * t)
            src = stage[chunk_no(i) % 2][:, 0:8 * splits[i][2] if i < len(zin) else 2048]
            hi, lo = pair(i)
            nc.vector.scalar_tensor_tensor(out=lo, in0=src.rearrange("p (k n) -> p k n", n=lo.shape[-1]),
                                           scalar=wscl[:, i % 8:i % 8 + 1], in1=hi, op0=ALU.mult,
                                           op1=ALU.subtract).then_inc(s_wlo, 1)

        block = ctx.enter_context(nc.Block())

        @block.sync
        def _(sp):
            sp.dma_start(consts[:], a["k_consts"]).then_inc(s_const, 16)
            for row, src in ((R_C, a["c"][0]), (R_CTX, a["c_ctx"]), (R_GPM, a["g_pre_mix"][0]), (R_GPF, a["g_pre_mlp"][0]),
                             (R_BIAS, a["b_ada"][0]), (R_PM, a["g_post_mix"][0]), (R_PF, a["g_post_mlp"][0])):
                sp.dma_start(vrow[row:row + src.shape[0] // P, :], src.rearrange("(k p) -> k p", p=P)).then_inc(s_vec, 16)
            sp.dma_start(vrow[R_BA:R_ALL, :], a["b_a2"][0].rearrange("d (k p) -> (d k) p", p=P)).then_inc(s_vec, 16)

            def load_x(j):
                sp.dma_start(x1[:, j, :], x_src(j)).then_inc(s_x[j], 16)

            pos_rows = a["k_pos_row"].rearrange("(j r) n -> r j n", r=2)

            def load_pos(j):
                if j == 1:
                    sp.dma_start(posc, a["k_pos_col"]).then_inc(s_pos[0], 16)
                for r in range(2):
                    sp.dma_start(posr[64 * r:64 * r + 64, j - 1:j + 1],
                                 pos_rows[r, j - 1:j + 1].partition_broadcast(64)).then_inc(s_pos[j // 2], 16)

            def load_ada(n):
                src, w = chunk_src(ada1[n])
                sp.dma_start(ada_room[n].rearrange("p (k n) -> p k n", n=w), src).then_inc(s_ada[n], 16)

            for what, n in start:
                if what == "x":
                    if n % 2 == 1:
                        load_pos(n)
                    load_x(n)
                elif what == "rows":
                    load_ada(n)
                if (what, n) == ("x", NT - 1):
                    load_chunk(sp, 0)
            load_chunk(sp, 1)
            sp.dma_start(ghb[:], a["g_head"][0].rearrange("h v -> (h v)").partition_broadcast(P)).then_inc(s_misc, 16)
            sp.wait_ge(s_wa2, 1)
            for d in range(2):
                sp.dma_start(wa2[RANK * d:RANK * d + RANK, 256 * d:256 * d + 256], a["w_a2"][0, d]).then_inc(s_misc, 16)
            for j in range(NT):
                x_ready(sp, j)
                sp.dma_start(xkeep[P * j:P * j + P, :], x1[:, j, :]).then_inc(s_xst, 16)
            for c in range(2, len(zin)):
                load_chunk(sp, c)
            sp.wait_ge(s_qk, 8)
            for d, name in enumerate(("state_gla_fwd", "state_gla_bwd")):
                sp.dma_start(Sst[:, d], a[name][0, 0].rearrange("(k h) d v -> (h d) k v", k=HK)).then_inc(s_state, 16)
            for c in range(len(zin), len(zin) + 2):
                load_chunk(sp, c)

            def store_state(d, out):
                A.wait_read(sp, ("U", d, 0))
                sp.dma_start(out[0, 0].rearrange("(k h) d v -> (h d) k v", k=HK), Sctx[d]).then_inc(s_sout, 16)

            store_state(0, out_sf)
            for c in range(len(zin) + 2, len(zin) + N_FWD):
                load_chunk(sp, c)
            A.take(sp, z_uses(len(zin) - 1)[-1])
            sp.dma_start(dftC, a["k_dft_cos"].rearrange("(m p) n -> p m n", p=P)).then_inc(s_dft, 16)
            sp.dma_start(dftS, a["k_dft_sin"].rearrange("(m p) n -> p m n", p=P)).then_inc(s_dft, 16)
            sp.dma_start(alt_row, a["k_alt"]).then_inc(s_dft, 16)
            for c in range(len(zin) + N_FWD, len(zin) + N_FWD + N_FOU):
                load_chunk(sp, c)
            store_state(1, out_sb)
            for c in range(len(zin) + N_FWD + N_FOU, ff_chunk):
                load_chunk(sp, c)
            B.take(sp, ("o", b_order[-1]))
            sp.wait_ge(s_xst, 16 * NT)
            for j in range(NT):
                sp.dma_start(x1[:, j, :], xkeep[P * j:P * j + P, :]).then_inc(s_x1[j], 16)
            load_ff(sp, 0, w1_v[:, :, 0:CW])
            load_ff(sp, 1, w1_v[:, :, CW:2 * CW])

            def group(g, t):
                for x in range(2):
                    load_ff(sp, 4 * g + 2 + x, w1_v[:, :, bass.ds(t * (2 * GFF) + GFF * (g + 1) + CW * x, CW)], t)
                for n in range(2):
                    down = w2_v[bass.ds(t * 2 + g, 1), :, :, 512 * n:512 * n + 512].rearrange("a p k n -> p (a k) n")
                    load_ff(sp, 4 * g + 4 + n, down, t)

            with sp.Fori(0, NG // 2 - 1) as t:
                group(0, t)
                group(1, t)
            group(NG - 2, 0)
            for n in range(2):
                load_ff(sp, 4 * NG - 2 + n, w2_v[NG - 1, :, :, 512 * n:512 * n + 512])
            for j in range(NT):
                sp.wait_ge(s_y, j + 1)
                sp.dma_start(out_p[0] if j == 0 else out_s[0, P * (j - 1):P * j, :], x1[:, j, :]).then_inc(s_out, 16)
            sp.wait_ge(s_sout, 32)
            sp.wait_ge(s_out, 16 * NT)

        @block.gpsimd
        def _(pool):
            own = Steps(pool, s_pool)
            nc.gpsimd.memset(slq[:], 0.0).then_inc(s_zero, 1)
            own.did(nc.gpsimd.memset(neg[:, 0:4], -0.5))
            own.did(nc.gpsimd.memset(neg[:, 4:5], -1.0))
            own.settle()

            def power(out, src, exponent, done=None):
                ins = nc.gpsimd.tensor_tensor(out, src, exponent, ALU.pow)
                if done is not None:
                    ins.then_inc(done, 1)
                else:
                    own.did(ins)
                    own.settle()

            def step(ins):
                own.did(ins)
                own.settle()

            def h_scale(n):
                pool.wait_ge(s_hmx, 2 * (n + 1))
                step(nc.gpsimd.partition_all_reduce(hmx[n][:, 1:3], hmx[n][:, 1:3], P, RMAX))
                step(nc.gpsimd.tensor_tensor(hmx[n][:, 0:1], hmx[n][:, 1:2], hmx[n][:, 2:3], ALU.add))
                step(nc.gpsimd.tensor_scalar(hinv[n], hmx[n][:, 0:1], D ** 0.5 / TOP, TINY, ALU.mult, ALU.max))
                if n == 0:
                    chunk_factor(0)
                power(hscl[n], hinv[n], neg[:, 4:5], s_hsc)

            def chunk_inverse(i, t=0):
                c = slice(i % 8, i % 8 + 1)
                pool.wait_ge(s_wmax, i + 1 + 8 * t)
                step(nc.gpsimd.partition_all_reduce(wall[:, c], wmax[:, c], P, RMAX))
                step(nc.gpsimd.tensor_scalar(winv[:, c], wall[:, c], 1.0 / TOP, TINY, ALU.mult, ALU.max))

            def chunk_factor(i, done=None):
                c = slice(i % 8, i % 8 + 1)
                if i < len(zin):
                    other, factor = hinv[0], DK ** -0.5 if i == Q else 1.0
                else:
                    half = wout[i - len(zin)][1]
                    other, factor = yinv[:, half:half + 1], 1.0
                ins = nc.gpsimd.tensor_scalar(wcof[:, c], winv[:, c], other, factor, ALU.mult, ALU.mult)
                if done is not None:
                    ins.then_inc(done, 1)
                else:
                    step(ins)

            def chunk_scale(i, factor=True):
                c = slice(i % 8, i % 8 + 1)
                chunk_inverse(i)
                if factor:
                    chunk_factor(i)
                power(wscl[:, c], winv[:, c], neg[:, 4:5], s_wscl)

            def ff_up_scale(g, x, t=0):
                i = w1_split(g, x)
                c = slice(i % 8, i % 8 + 1)
                chunk_inverse(i, t)
                power(wscl[:, c], winv[:, c], neg[:, 4:5], s_wscl)
                if x == 1:
                    b = g % 2
                    first = w1_split(g, 0) % 8
                    p = slice(b, b + 1)
                    step(nc.gpsimd.tensor_scalar(fmx[:, p], winv[:, first:first + 1], winv[:, c], None, ALU.max))
                    power(frg[:, p], fmx[:, p], neg[:, 4:5])
                    step(nc.gpsimd.tensor_scalar(ftm[:, p], fmx[:, p], hinv[1], 1.0 / F_ALPHA, ALU.mult, ALU.mult))
                    step(nc.gpsimd.tensor_tensor(finv[:, p], ftm[:, p], ftm[:, p], ALU.mult))
                    step(nc.gpsimd.tensor_scalar(beta[:, 2 * b:2 * b + 1], winv[:, first:first + 1], frg[:, p], F_ALPHA,
                                                 ALU.mult, ALU.mult))
                    nc.gpsimd.tensor_scalar(beta[:, 2 * b + 1:2 * b + 2], winv[:, c], frg[:, p], F_ALPHA,
                                            ALU.mult, ALU.mult).then_inc(s_beta, 1)

            def ff_down_scale(i, g, t=0):
                c = slice(i % 8, i % 8 + 1)
                chunk_inverse(i, t)
                step(nc.gpsimd.tensor_tensor(wcof[:, c], winv[:, c], finv[:, g % 2:g % 2 + 1], ALU.mult))
                power(wscl[:, c], winv[:, c], neg[:, 4:5], s_wscl)

            def rstd(out, mean, sums, n, done):
                if sums.shape[-1] == 2 * out.shape[-1]:
                    step(nc.gpsimd.tensor_tensor(mean, sums[:, 0:1], sums[:, 1:2], ALU.add))
                    sums = mean
                step(nc.gpsimd.tensor_scalar(mean, sums, 1.0 / n, EPS, ALU.mult, ALU.add))
                power(out, mean, neg[:, 0:out.shape[-1]], done)

            def x_rstd(j):
                pool.wait_ge(s_ssq, 2 * (j + 1))
                rstd(rst[:, j:j + 1], sqs[:, j:j + 1], ssq[:, 2 * j:2 * j + 2], D, s_rst)

            def y_scale(half):
                p = slice(half, half + 1)
                pool.wait_ge(s_ymx, 2 - half)
                step(nc.gpsimd.partition_all_reduce(yall[:, p], ymx[:, p], P, RMAX))
                step(nc.gpsimd.tensor_scalar(yinv[:, p], yall[:, p], 1.0 / TOP, TINY, ALU.mult, ALU.max))
                power(yscl[:, p], yinv[:, p], neg[:, 4:5], s_ysc)

            for j in range(NT):
                x_rstd(j)
            chunk_scale(0, False)
            A.take(pool, ada1[6])
            nc.gpsimd.memset(wa2, 0.0).then_inc(s_wa2, 1)
            h_scale(0)
            for i in range(1, len(zin)):
                chunk_scale(i)
            pool.wait_ge(s_misc, 48)
            for r in range(2 * NT + 1):
                if r < 2 * NT:
                    pool.wait_ge(s_ge, r + 1)
                    nc.gpsimd.tensor_scalar(gex[:, r % 2, :], gex[:, r % 2, :], 1.0, None, ALU.add).then_inc(s_gsg, 1)
                if r >= 1:
                    pool.wait_ge(s_gs, r)
                    j, cs = (r - 1) % NT, slice(CW * ((r - 1) // NT), CW * ((r - 1) // NT) + CW)
                    nc.gpsimd.tensor_tensor(gN[:, j, cs], gN[:, j, cs], ghb[:, cs], ALU.mult).then_inc(s_gh, 1)
            A.take(pool, ("P", 4))
            nc.gpsimd.memset(Srb, 0.0).then_inc(s_srz, 1)
            for s, j in enumerate(b_order):
                for hp in range(HK):
                    A.wait_read(pool, ("At", j, hp))
                    if s >= 2 and hp == 0:
                        B.take(pool, ("o", b_order[s - 2]))
                    hs = slice(hp, HEADS, 2)
                    nc.gpsimd.tensor_tensor(ATb[:, s % 2, hs, :], Am[:, hs, 0:P], Am[:, hs, P:2 * P], ALU.add).then_inc(s_at, 1)
                if s >= 1:
                    jj = b_order[s - 1]
                    pool.wait_ge(s_oss, HEADS * s)
                    rstd(ors[:, 4 * jj:4 * jj + 4], ors[:, 4 * jj:4 * jj + 4], oss[:, 4 * jj:4 * jj + 4], DV, s_ors)
                if s == 6:
                    y_scale(1)
                if s == 8:
                    chunk_scale(len(zin) + 2, False)
                if s == 4:
                    h_scale(1)
                    chunk_scale(len(zin), False)
                    chunk_scale(len(zin) + 1, False)
            jj = b_order[-1]
            pool.wait_ge(s_oss, HEADS * NT)
            rstd(ors[:, 4 * jj:4 * jj + 4], ors[:, 4 * jj:4 * jj + 4], oss[:, 4 * jj:4 * jj + 4], DV, s_ors)
            y_scale(0)
            for c in range(3):
                chunk_factor(len(zin) + c)
            chunk_scale(len(zin) + 3, False)
            chunk_factor(len(zin) + 3, s_cof)
            for s in range(NT + 1):
                if s >= 1:
                    j = s - 1
                    pool.wait_ge(s_qss, 2 * (j + 1))
                    rstd(qrs[:, j:j + 1], qsm[:, j:j + 1], qss[:, 2 * j:2 * j + 2], D, s_qrs)
                if s in (5, 6):
                    ff_up_scale(0, s - 5)
                if s < NT:
                    pool.wait_ge(s_pss, 2 * (s + 1))
                    rstd(prs[:, s:s + 1], psm[:, s:s + 1], pss[:, 2 * s:2 * s + 2], D, s_prs)
            A.take(pool, ("wo", 3, NT - 1))
            A.take(pool, A0 + 5)
            nc.gpsimd.memset(acc, 0.0).then_inc(s_accz, 1)
            ff_up_scale(1, 0)

            def group(g, t):
                ff_up_scale(g + 1, 1, t)
                for n in range(2):
                    ff_down_scale(ff_split + 4 * g + 4 + n, g, t)
                if g + 2 < NG:
                    ff_up_scale(g + 2, 0, t)

            for t in range(NG // 2 - 1):
                group(0, t)
                group(1, t)
            group(NG - 2, 0)
            for n in range(2):
                ff_down_scale(ff_split + 4 * NG - 2 + n, NG - 1)
            for j in range(NT):
                pool.wait_ge(s_fss, 2 * (j + 1))
                rstd(frs[:, j:j + 1], fsm[:, j:j + 1], fss[:, 2 * j:2 * j + 2], D, s_frs)

        @block.scalar
        def _(act):
            own = Steps(act, s_act)

            squared = {}
            last_squares = []

            def squares(src, out2, done, width=512):
                for h in range(src.shape[-1] // width):
                    if last_squares:
                        act.wait_ge(last_squares[-1], squared[last_squares[-1].name])
                    nc.scalar.activation(junk[:, 0:width], src[:, width * h:width * h + width], ACT.Square,
                                         accum_out=out2[:, h:h + 1]).then_inc(done, 1)
                    squared[done.name] = squared.get(done.name, 0) + 1
                    last_squares.append(done)

            A.wait_read(act, "vec")
            nc.scalar.activation(sil, vT[:, 0:16], ACT.Exp, scale=-1.0).then_inc(s_sexp, 1)

            def mod_part(n, c):
                bank = A.take(act, c)
                if n >= 2:
                    B.take(act, ("mod", mods[n - 2]))
                nc.scalar.activation(part[n % 2][:], bank[:, 0:CW], ACT.Copy).then_inc(A.read(c), 1)

            mods = ada1 + ada2

            def norm_x(j):
                act.wait_ge(s_rst, j + 1)
                if j >= 2:
                    B.take(act, ("xT", j - 2, 1))
                nc.scalar.activation(xh[j % 2], x1[:, j, :], ACT.Copy, scale=rst[:, j:j + 1]).then_inc(s_xh, 1)

            def square_x(j):
                x_ready(act, j)
                squares(x1[:, j, :], ssq[:, 2 * j:2 * j + 2], s_ssq)

            square_x(0)
            norm_x(0)
            square_x(1)
            for what, n in start:
                if what == "x":
                    if n + 2 < NT:
                        square_x(n + 2)
                    if n + 1 < NT:
                        norm_x(n + 1)
                elif what == "rows":
                    mod_part(n, ada1[n])
            chunk_high(act, 0)
            for h in range(2):
                B.wait_read(act, ("xT", NT - 1, h))
            B.wait_read(act, ("xT", NT - 2, 1))
            act.wait_ge(s_gn, 1)

            for b in range(TB):
                for h in range(2):
                    for k in (4 * h + 2, 4 * h + 3):
                        for v, toks in block_parts(b):
                            c = 2 * k + v
                            own.did(nc.scalar.activation(xT[:, k, toks], xT[:, k, toks], ACT.Identity,
                                                         scale=amul[0][:, c:c + 1], bias=shf[0][:, c:c + 1]))
                    own.settle()
                    act.wait_ge(s_mv, 2 * b + h + 1)
                    t_ = (slice(None), slice(4 * h, 4 * h + 4), slice(TBW * b, TBW * b + TBW))
                    nc.scalar.activation(HTh[t_], xT[t_], ACT.Copy).then_inc(s_th, 1)

            def take_z(key):
                return A.take(act, key)

            def evac_t(i, dst):
                for key in z_uses(i):
                    _, _, m, t = key
                    bank = take_z(key)
                    nc.scalar.activation(dst[:, m, TBW * t:TBW * t + TBW], bank[:, 0:TBW], ACT.Copy,
                                         scale=wcof[:, i % 8:i % 8 + 1]).then_inc(A.read(key), 1)

            def decay_logs(k):
                for d in range(2):
                    for t in range(TB):
                        B.wait_read(act, ("la", d, k, t))
                    own.did(nc.scalar.activation(tmp[2 * d + 1], tmp[2 * d], ACT.Abs))
                own.settle()
                for d in range(2):
                    own.did(nc.scalar.activation(tmp[2 * d + 1], tmp[2 * d + 1], ACT.Exp, scale=-1.0))
                own.settle()
                for d in range(2):
                    nc.scalar.activation(tmp[2 * d + 1], tmp[2 * d + 1], ACT.Ln, bias=1.0).then_inc(s_dln, 1)

            def decay_exps(k):
                for d in range(2):
                    act.wait_ge(s_de, 2 * k + d + 1)
                    own.did(nc.scalar.activation(wexp[2 * d + k], wexp[2 * d + k], ACT.Exp, scale=1.0 / TAU))
                    nc.scalar.activation(tmp[2 * d + 1], tmp[2 * d], ACT.Exp, scale=1.0 / TAU).then_inc(s_dexp, 1)
                    act.wait_ge(s_dexp, 4 * k + 2 * d + 1)
                    nc.scalar.activation(tmp[2 * d], tmp[2 * d], ACT.Exp, scale=-1.0 / TAU).then_inc(s_dexp, 1)

            for i in range(G_A):
                chunk_high(act, i + 1)
                if i == LR:
                    for key in z_uses(i):
                        bank = take_z(key)
                        t = key[3]
                        nc.scalar.activation(lrS[:, TBW * t:TBW * t + TBW], bank[0:2 * RANK, 0:TBW], ACT.Copy,
                                             scale=wcof[0:2 * RANK, i % 8:i % 8 + 1]).then_inc(A.read(key), 1)
                elif i == Q:
                    evac_t(i, qT)
                elif i == K:
                    decay_logs(0)
                    evac_t(i, kT)
                elif i == U_A:
                    decay_exps(0)
                    evac_t(i, uT[:, 0:2, :])
                elif i == U_B:
                    decay_logs(1)
                    evac_t(i, uT[:, 2:4, :])
                else:
                    if i == V_A:
                        decay_exps(1)
                    for key in z_uses(i):
                        bank = take_z(key)
                        nc.scalar.activation(vN[:, key[3], CW * (i - V_A):CW * (i - V_A) + CW], bank[:, 0:CW], ACT.Copy,
                                             scale=wcof[:, i % 8:i % 8 + 1]).then_inc(A.read(key), 1)

            def ada_parts(n):
                if n < len(ada2):
                    mod_part(len(ada1) + n, ada2[n])

            def copy_kn(d, j, last):
                key = ("kn", d, j)
                bank = B.take(act, key)
                if last is not None:
                    A.take(act, last)
                nc.scalar.activation(kn[d], bank[:, 0:2 * P], ACT.Copy).then_inc(B.read(key), 1)

            def gate(r):
                return gN[:, r % NT, CW * (r // NT):CW * (r // NT) + CW]

            act.wait_ge(s_qk, 8)
            for what, n in gate_events:
                if what == "kn":
                    copy_kn(0, f_order[n], ("U", 0, f_order[n - 1]) if n >= 1 else None)
                elif what == "U":
                    ada_parts(n)
                else:
                    if n == 0:
                        chunk_high(act, G_B)
                    i = G_A + n // NT
                    key = ("z", i, 0, n % NT)
                    bank = take_z(key)
                    nc.scalar.activation(gate(n), bank[:, 0:CW], ACT.Copy, scale=wcof[:, i % 8:i % 8 + 1]).then_inc(A.read(key), 1)
                    if n >= 2:
                        act.wait_ge(s_gs, n - 1)
                    A.wait_read(act, key)
                    nc.scalar.activation(gex[:, n % 2, :], gate(n), ACT.Exp, scale=-1.0).then_inc(s_ge, 1)

            for i in range(4):
                bank = A.take(act, ("dA", i))
                nc.scalar.activation(AB[:, i, :], bank[:], ACT.Copy).then_inc(A.read(("dA", i)), 1)
            bank = A.take(act, ("dA", 4))
            nc.scalar.activation(A512, bank[0:1, 0:4 * NCOS], ACT.Copy).then_inc(A.read(("dA", 4)), 1)
            bank = A.take(act, ("dA", 5))
            nc.scalar.activation(Y2b, bank[:], ACT.Copy).then_inc(A.read(("dA", 5)), 1)

            act.wait_ge(s_sout, 16)

            def put_y(i):
                bank = B.take(act, ("Y1", i))
                c0 = 0 if i < 0 else CTX + P * i
                nc.scalar.activation(yT[:, 4:8, c0:c0 + P], bank[:].rearrange("p (g t) -> p g t", g=GROUPS),
                                     ACT.Copy).then_inc(B.read(("Y1", i)), 1)
                if i < 0:
                    return
                bank = B.take(act, ("Y2", i))
                first = 1 if i == 0 else 0
                c1 = CTX + LAT - P * i - first
                nc.scalar.activation(yT[:, 4:8, c1:c1 - (P - first):-1],
                                     bank[:].rearrange("p (g t) -> p g t", g=GROUPS)[:, :, first:P],
                                     ACT.Copy).then_inc(B.read(("Y2", i)), 1)

            for i in range(-1, 4):
                bank = A.take(act, ("Q", i))
                if i >= 0:
                    A.wait_read(act, ("P", i - 1))
                nc.scalar.activation(Qs[:, 0:4 * NSIN], bank[:, 0:4 * NSIN], ACT.Copy).then_inc(A.read(("Q", i)), 1)
                ada_parts(N_FWD + 1 + i)
                if i >= 0:
                    put_y(i - 1)
            put_y(3)
            bank = B.take(act, ("Y1", 4))
            nc.scalar.activation(yT[:, 4:8, CTX + FOLD:CTX + FOLD + 1], bank[:, 0:4].rearrange("p (g t) -> p g t", g=GROUPS),
                                 ACT.Copy).then_inc(B.read(("Y1", 4)), 1)

            def scores(j, last):
                if j != 1:
                    copy_kn(1, j, last)

            def put_o(j):
                bank = B.take(act, ("oT", j))
                nc.scalar.activation(yT[:, 0:4, P * j:P * j + P], bank[:].rearrange("p (g t) -> p g t", g=HEADS),
                                     ACT.Copy).then_inc(B.read(("oT", j)), 1)

            scores(b_order[0], None)
            for s, j in enumerate(b_order):
                if s + 1 < NT:
                    scores(b_order[s + 1], ("U", 1, j))
                bank = B.take(act, ("o", j))
                squares(bank[:], oss[:, 4 * j:4 * j + 4], s_oss, DV)
                if s >= 1:
                    put_o(b_order[s - 1])
                ada_parts(N_FWD + N_FOU + s)
                if s in (5, 6):
                    chunk_high(act, len(zin) + s - 5)
            put_o(b_order[-1])

            def high_y(j):
                for half in (1, 0):
                    act.wait_ge(s_ysc, 2 - half)
                    nc.scalar.activation(YTh[:, 4 * half:4 * half + 4, P * j:P * j + P],
                                         yT[:, 4 * half:4 * half + 4, P * j:P * j + P],
                                         ACT.Copy, scale=yscl[:, half:half + 1]).then_inc(s_yh, 1)

            def put_even(c, j):
                if c == 0 and j == 0:
                    act.wait_ge(s_cof, 1)
                if c == 0 and j >= 4:
                    B.take(act, ("x2", j - 4, 1))
                key = ("wo", c, j)
                bank = A.take(act, key)
                i = len(zin) + c
                nc.scalar.activation(yN[:, j % 4, 256 * c:256 * c + 512], bank[:], ACT.Copy,
                                     scale=wcof[:, i % 8:i % 8 + 1]).then_inc(A.read(key), 1)

            def put_gates(q):
                key = ("gate", q)
                bank = B.take(act, key)
                nc.scalar.activation(gates[:, q // 4, q // 2 % 2, 512 * (q % 2):512 * (q % 2) + 512], bank[:],
                                     ACT.Copy).then_inc(B.read(key), 1)

            def squares_y(j):
                for c in (1, 3):
                    A.wait_read(act, ("wo", c, j))
                squares(yN[:, j % 4, :], pss[:, 2 * j:2 * j + 2], s_pss)

            def squares_x1(j):
                act.wait_ge(s_xr, j + 1)
                squares(x1[:, j, :], qss[:, 2 * j:2 * j + 2], s_qss)

            def norm_x1(j):
                act.wait_ge(s_qrs, j + 1)
                nc.scalar.activation(yN[:, j % 4, :], x1[:, j, :], ACT.Copy, scale=qrs[:, j:j + 1]).then_inc(s_2x, 1)

            def high_2(j):
                for h in range(2):
                    B.wait_read(act, ("x2", j, h))
                    nc.scalar.activation(HT2h[:, 4 * h:4 * h + 4, P * j:P * j + P],
                                         tb2[h].rearrange("p (k t) -> p k t", k=4), ACT.Copy).then_inc(s_2h, 1)

            act.wait_ge(s_sout, 32)
            high_y(0)
            chunk_high(act, len(zin) + 2)
            chunk_high(act, len(zin) + 3)
            high_y(1)
            for j in range(NT + 2):
                if j < NT:
                    put_even(0, j)
                if j + 2 < NT:
                    high_y(j + 2)
                if 1 <= j <= NT:
                    squares_x1(j - 1)
                if j >= 2:
                    high_2(j - 2)
                if 1 <= j <= NT:
                    norm_x1(j - 1)
                if j < NT:
                    put_even(2, j)
                if j == 6:
                    chunk_high(act, ff_split)
                if j == NT:
                    chunk_high(act, ff_split + 1)
                if j == 0:
                    B.wait_read(act, ("o", b_order[-1]))
                if j < 2:
                    for q in range(4):
                        put_gates(4 * j + q)
                if j < NT:
                    squares_y(j)

            def up(g, x, t=0):
                for u in range(6):
                    r = 6 * x + u
                    tb_, m = u // 2, 2 * x + u % 2
                    n_ = 12 * g + r
                    key = A0 + UA * g + r
                    bank = A.take(act, key, 6 * t)
                    if r == 0:
                        act.wait_ge(s_beta, g + 1 + 2 * t)
                        if g >= 1:
                            B.take(act, B0 + UB * (g - 2) + UB - 1, 12 * t)
                    if n_ >= 2:
                        act.wait_ge(s_fq, n_ - 1 + 24 * t)
                        act.wait_ge(s_fh, n_ - 1 + 24 * t)
                    nc.scalar.activation(frel[:, n_ % 2, :], bank[:, 0:TBW], ACT.Relu,
                                         scale=beta[:, 2 * (g % 2) + x:2 * (g % 2) + x + 1]).then_inc(A.read(key), 1)
                    b, cnt, _ = A.spot(key)
                    act.wait_ge(A.free[b], cnt + 6 * t)
                    nc.scalar.activation(FTh[g % 2][:, m, TBW * tb_:TBW * tb_ + TBW], frel[:, n_ % 2, :],
                                         ACT.Square).then_inc(s_fh, 1)

            up(0, 0)
            chunk_high(act, ff_split + 2)
            up(0, 1)

            def group(g, t):
                for s in range(4):
                    if g == 0 and s == 0:
                        B.take(act, B0 - 1, 12 * t)
                    chunk_high(act, ff_split + 4 * g + 3 + s, t)
                    if s < 2:
                        up(g + 1, s, t)

            with act.Fori(0, NG // 2 - 1) as t:
                group(0, t)
                group(1, t)
            group(NG - 2, 0)
            chunk_high(act, ff_split + 4 * NG - 1)
            for j in range(NT):
                B.wait_read(act, B0 + UB * (NG - 1) + NT + j)
                squares(acc[:, j, :], fss[:, 2 * j:2 * j + 2], s_fss)

        @block.tensor
        def _(pe):
            def mm(out, lhsT, rhs, start, stop):
                return nc.tensor.matmul(out, lhsT, rhs, start=start, stop=stop, skip_group_check=True)

            def three(out, ks, lhs, rhs, halfway=None):
                (lh, ll), (rh, rl) = lhs, rhs
                terms = [(k, x) for k in ks for x in ((lh, rh), (lh, rl), (ll, rh))]
                for n, (k, (x, y)) in enumerate(terms):
                    if halfway is not None and n == len(terms) // 2:
                        halfway()
                    ins = mm(out, x(k), y(k), n == 0, n == len(terms) - 1)
                return ins

            pe.wait_ge(s_const, 16)
            pe.wait_ge(s_vec, 16 * 8)
            bank = A.open(pe, "vec")
            nc.tensor.transpose(bank[:, 0:R_ALL], vrow[0:R_ALL, :], ident[0:R_ALL, 0:R_ALL]).then_inc(A.filled("vec"), 1)
            pe.wait_ge(s_slp, 1)
            mods = ada1 + ada2

            def mod_rows(c):
                if c in ada1:
                    pe.wait_ge(s_ada[ada1.index(c)], 16)
                    w = ada_room[ada1.index(c)].rearrange("p (k n) -> p k n", n=CW)
                else:
                    g = chunk_of[c]
                    pe.wait_ge(s_stage[g % 2], 16 * (g // 2 + 1))
                    w = staged(g, CW)
                bank = A.open(pe, c)
                for k in range(KT):
                    r = 32 * (k % 4)
                    ins = nc.tensor.matmul(bank[r:r + 32, 0:CW], slq[:, k, :], w[:, k, :], start=k < 4, stop=k >= 4,
                                           tile_position=(0, r), skip_group_check=True)
                ins.then_inc(A.filled(c), 1)

            def mod_out(n, c):
                A.wait_read(pe, c)
                key = ("mod", c)
                bank = B.open(pe, key)
                for m in range(2):
                    ins = mm(bank[:, 2 * m:2 * m + 2], part[n % 2][:, P * m:P * m + P], sel2, True, True)
                ins.then_inc(B.filled(key), 1)

            def ada_rows(n):
                for what, m in ada_step(n):
                    if what == "rows":
                        mod_rows(ada2[m])
                    else:
                        mod_out(len(ada1) + m, ada2[m])

            def turn(key, src, ready):
                ready()
                bank = B.open(pe, key)
                for k in range(4):
                    ins = nc.tensor.transpose(bank[:, P * k:P * k + P], src[:, P * k:P * k + P], ident)
                ins.then_inc(B.filled(key), 1)

            for what, n in start:
                if what == "x":
                    for h in range(2):
                        turn(("xT", n, h), xh[n % 2][:, 512 * h:512 * h + 512], lambda: pe.wait_ge(s_xh, n + 1))
                elif what == "rows":
                    mod_rows(ada1[n])
                else:
                    mod_out(n, ada1[n])

            def up_tile(ring_key, turns, i, m, t, Hh, Hl, mw=P, halfway=None):
                wh, wl = pair(i)
                bank = A.open(pe, ring_key, turns)
                toks = slice(TBW * t, TBW * t + TBW)
                return three(bank[0:mw, 0:TBW], range(KT),
                             (lambda k: wh[:, k, P * m:P * m + mw], lambda k: wl[:, k, P * m:P * m + mw]),
                             (lambda k: Hh[:, k, toks], lambda k: Hl[:, k, toks]), halfway)

            def row_tile(ring, ring_key, turns, i, j, ks, Hh, Hl, k0, w):
                wh, wl = pair(i)
                bank = ring.open(pe, ring_key, turns)
                toks = slice(P * j, P * j + P)
                return three(bank[:, 0:w], ks,
                             (lambda k: Hh[:, k0 + k, toks], lambda k: Hl[:, k0 + k, toks]),
                             (lambda k: wh[:, k, :], lambda k: wl[:, k, :]))

            def logits(k):
                pe.wait_ge(s_misc, 48)
                for t in range(TB):
                    A.wait_read(pe, ("z", LR, 0, t))
                for d in range(2):
                    for t in range(TB):
                        key = ("la", d, k, t)
                        bank = B.open(pe, key)
                        mm(bank[:, 0:TBW], wa2[:, 256 * d + P * k:256 * d + P * k + P], lrS[:, TBW * t:TBW * t + TBW],
                           True, True).then_inc(B.filled(key), 1)

            for i in range(G_A):
                pe.wait_ge(s_wlo, i + 1)
                for n, key in enumerate(z_uses(i)):
                    if i in TFORM:
                        _, _, m, t = key
                        if i == LR:
                            pe.wait_ge(s_tl, 2 * t + 1)
                            ins = up_tile(key, 0, i, m, t, HTh, HTl, 2 * RANK, lambda: pe.wait_ge(s_tl, 2 * t + 2))
                        else:
                            ins = up_tile(key, 0, i, m, t, HTh, HTl)
                    else:
                        ins = row_tile(A, key, 0, i, key[3], range(KT), HTh, HTl, 0, CW)
                    ins.then_inc(A.filled(key), 1)
                if i == Q:
                    logits(0)
                if i == U_A:
                    logits(1)

            def turn_k(d, j):
                key = ("kn", d, j)
                bank = B.open(pe, key)
                for k in range(HK):
                    ins = nc.tensor.transpose(bank[:, P * k:P * k + P], kt_[d][k][:, P * j:P * j + P], ident)
                ins.then_inc(B.filled(key), 1)

            def update(d, j):
                B.wait_read(pe, ("kn", d, j))
                key = ("U", d, j)
                bank = A.open(pe, key)
                for k in range(HK):
                    both = slice(2 * DV * k, 2 * DV * k + 2 * DV)
                    ins = mm(bank[:, both], kn[d][:, P * k:P * k + P], vN[:, j, both], True, True)
                ins.then_inc(A.filled(key), 1)

            for what, n in gate_events:
                if what == "z":
                    i = G_A + n // NT
                    if n % NT == 0:
                        pe.wait_ge(s_wlo, i + 1)
                    key = ("z", i, 0, n % NT)
                    row_tile(A, key, 0, i, n % NT, range(KT), HTh, HTl, 0, CW).then_inc(A.filled(key), 1)
                elif what == "kn":
                    if n == 0:
                        pe.wait_ge(s_qk, 8)
                    turn_k(0, f_order[n])
                else:
                    if n == 0:
                        for key in z_uses(V_B)[-4:]:
                            A.wait_read(pe, key)
                    update(0, f_order[n])
                    ada_rows(n)

            pe.wait_ge(s_fold, 1)
            cosw, sinw = dft_ch[:, 0:NCOS], dft_ch[:, NCOS:P]
            for i in range(6):
                key = ("dA", i)
                bank = A.open(pe, key)
                for g in range(GROUPS):
                    if i < 4:
                        e, o = Ef[:, g, P * i:P * i + P], Of[:, g, P * i:P * i + P]
                    elif i == 4:
                        e, o = uT[:, g, CTX + FOLD:CTX + FOLD + 1], None
                    else:
                        e = o = uT[:, g, 0:CTX]
                    ins = mm(bank[0:e.shape[-1], NCOS * g:NCOS * g + NCOS], e, cosw, True, True)
                    if o is not None:
                        c0 = GROUPS * NCOS + NSIN * g
                        ins = mm(bank[:, c0:c0 + NSIN], o, sinw, True, True)
                ins.then_inc(A.filled(key), 1)
            NP_, NQ_ = GROUPS * NCOS, GROUPS * NSIN
            pe.wait_ge(s_dft, 48)
            for i in range(4):
                A.wait_read(pe, ("dA", i))
            A.wait_read(pe, ("dA", 4))
            A.wait_read(pe, ("dA", 5))

            def turn_y(i):
                for b, y in (("Y1", Y1b), ("Y2", Y2b)):
                    if b == "Y2" and i < 0:
                        continue
                    turn((b, i), y, lambda: A.wait_read(pe, ("P", i)))

            for i in range(-1, 4):
                P_, Q_ = ("P", i), ("Q", i)
                bank = A.open(pe, P_)
                if i < 0:
                    ins = mm(bank[:, 0:NP_], dft_ctx[:, 0:P], Y2b[:, 0:NP_], True, True)
                else:
                    for m in range(4):
                        mm(bank[:, 0:NP_], dftC[:, m, P * i:P * i + P], AB[:, m, 0:NP_], m == 0, False)
                    ins = mm(bank[:, 0:NP_], alt_row, A512, False, True)
                ins.then_inc(A.filled(P_), 1)
                bank = A.open(pe, Q_)
                if i < 0:
                    ins = mm(bank[:, 0:NQ_], dft_ctx[:, P:2 * P], Y2b[:, NP_:512], True, True)
                else:
                    for m in range(4):
                        ins = mm(bank[:, 0:NQ_], dftS[:, m, P * i:P * i + P], AB[:, m, NP_:512], m == 0, m == 3)
                ins.then_inc(A.filled(Q_), 1)
                ada_rows(N_FWD + 1 + i)
                if i >= 0:
                    turn_y(i - 1)
            P_ = ("P", 4)
            bank = A.open(pe, P_)
            for m in range(4):
                mm(bank[0:1, 0:NP_], consts[:, C_ALT:C_ALT + 1], AB[:, m, 0:NP_], m == 0, False)
            mm(bank[0:1, 0:NP_], alt_row[:, 0:1], A512, False, True).then_inc(A.filled(P_), 1)
            turn_y(3)
            A.wait_read(pe, P_)
            key = ("Y1", 4)
            bank = B.open(pe, key)
            for g in range(GROUPS):
                ins = mm(bank[:, g:g + 1], Y1b[0:1, P * g:P * g + P], ident[0:1, 0:1], True, True)
            ins.then_inc(B.filled(key), 1)

            def scores(j):
                if j != 1:
                    turn_k(1, j)
                for hp in range(HK):
                    key = ("At", j, hp)
                    bank = A.open(pe, key)
                    rows = slice(DK * hp, DK * hp + DK)
                    for k in range(HK):
                        for d in range(2):
                            c0 = 2 * P * k + P * d
                            ins = mm(bank[:, c0:c0 + P], kt_[d][k][rows, P * j:P * j + P],
                                     qt[d][k][rows, P * j:P * j + P], True, True)
                    ins.then_inc(A.filled(key), 1)
                if j != 1:
                    update(1, j)

            def outputs(s, j):
                key = ("o", j)
                pe.wait_ge(s_at, HK * (s + 1))
                if j > 0:
                    pe.wait_ge(s_srf, HK * j)
                    pe.wait_ge(s_srb, HK * s)
                bank = B.open(pe, key)
                for k in range(HK):
                    both = slice(2 * DV * k, 2 * DV * k + 2 * DV)
                    if j > 0:
                        mm(bank[:, both], qt[0][k][:, P * j:P * j + P], Srf[:, j - 1, k, :], True, False)
                        mm(bank[:, both], qt[1][k][:, P * j:P * j + P], Srb[:, s % 3, k, :], False, False)
                    for h in (2 * k, 2 * k + 1):
                        ins = mm(bank[:, DV * h:DV * h + DV], ATb[:, s % 2, h, :], vN[:, j, DV * h:DV * h + DV],
                                 j == 0, True)
                ins.then_inc(B.filled(key), 1)

            def turn_o(s, j):
                turn(("oT", j), yo[:, s % 2, :], lambda: B.wait_read(pe, ("o", j)))

            scores(b_order[0])
            for s, j in enumerate(b_order):
                if s + 1 < NT:
                    scores(b_order[s + 1])
                outputs(s, j)
                if s >= 1:
                    turn_o(s - 1, b_order[s - 1])
                if N_FWD + N_FOU + s <= len(ada2):
                    ada_rows(N_FWD + N_FOU + s)
            turn_o(NT - 1, b_order[-1])

            def turn_x(j):
                for h in range(2):
                    turn(("x2", j, h), yN[:, j % 4, 512 * h:512 * h + 512], lambda: pe.wait_ge(s_2x, j + 1))

            def spread_gates(q):
                key = ("gate", q)
                pe.wait_ge(s_dg, q + 1)
                bank = B.open(pe, key)
                for k in range(4):
                    ins = mm(bank[:, P * k:P * k + P], ones, diag[q % 4][:, P * k:P * k + P], True, True)
                ins.then_inc(B.filled(key), 1)

            for j in range(NT):
                for c in range(4):
                    i = len(zin) + c
                    half = wout[c][1]
                    if c < 2:
                        pe.wait_ge(s_yl, 2 * j + 1 + c)
                    if j == 0:
                        pe.wait_ge(s_wlo, i + 1)
                    key = ("wo", c, j)
                    row_tile(A, key, 0, i, j, range(4), YTh, YTl, 4 * half, 512).then_inc(A.filled(key), 1)
                    if c == 1 and j >= 2:
                        turn_x(j - 2)
                if j < 2:
                    for q in range(4):
                        spread_gates(4 * j + q)

            def up(g, x, t=0):
                i = w1_split(g, x)
                pe.wait_ge(s_wlo, i + 1 + 8 * t)
                for u in range(6):
                    key = A0 + UA * g + 6 * x + u
                    if g == 0 and x == 0:
                        if u in (1, 3):
                            turn_x(NT - 2 + u // 2)
                        if u % 2 == 0:
                            pe.wait_ge(s_2l, 6 * (u // 2 + 1))
                    up_tile(key, 6 * t, i, u % 2, u // 2, HT2h, HT2l).then_inc(A.filled(key), 1)

            def down(i, g, n, t=0):
                pe.wait_ge(s_wlo, i + 1 + 8 * t)
                if n == 0:
                    pe.wait_ge(s_fl, 12 * (g + 1) + 24 * t)
                for j in range(NT):
                    key = B0 + UB * g + NT * n + j
                    row_tile(B, key, 12 * t, i, j, range(FT), FTh[g % 2], FTl[g % 2], 0, 512).then_inc(B.filled(key), 1)

            for x in range(2):
                up(0, x)

            def group(g, t):
                for x in range(2):
                    up(g + 1, x, t)
                for n in range(2):
                    down(ff_split + 4 * g + 4 + n, g, n, t)

            with pe.Fori(0, NG // 2 - 1) as t:
                group(0, t)
                group(1, t)
            group(NG - 2, 0)
            for n in range(2):
                down(ff_split + 4 * NG - 2 + n, NG - 1, n)

        @block.vector
        def _(dve):
            own = Steps(dve, s_dve)
            V = nc.vector

            def step(ins):
                own.did(ins)
                own.settle()

            bank = A.take(dve, "vec")
            V.tensor_copy(vT, bank[:, 0:R_ALL]).then_inc(A.read("vec"), 1)
            own.did(V.memset(ones, 1.0))
            A.wait_read(dve, "vec")
            dve.wait_ge(s_sexp, 1)
            step(V.tensor_scalar(sil, sil, 1.0, None, ALU.add))
            step(V.reciprocal(sil2, sil))
            dve.wait_ge(s_zero, 1)
            V.tensor_tensor(slq[:, :, 0:2], vT[:, 0:16].rearrange("p (v k) -> p k v", v=2),
                            sil2.rearrange("p (v k) -> p k v", v=2), ALU.mult).then_inc(s_slp, 1)

            def add_pos(j):
                dve.wait_ge(s_x[j], 16)
                dve.wait_ge(s_pos[(j - 1) // 2], 48 if j <= 2 else 32)
                own.did(V.tensor_tensor(x1[:, j, 0:512], x1[:, j, 0:512], posr[:, j - 1, :], ALU.add))
                V.tensor_tensor(x1[:, j, 512:D], x1[:, j, 512:D], posc, ALU.add).then_inc(s_posd, 1)

            def mod_cols(c):
                bank = B.take(dve, ("mod", c))
                dst = {SH_M: shf[0], SC_M: amul[0], GT_M: gtc[0], SH_F: shf[1], SC_F: amul[1], GT_F: gtc[1]}[c[1]]
                dst = dst.rearrange("p (k v) -> p k v", v=2)
                row = {SH_M: R_SHM, SC_M: R_SCM, GT_M: R_GTM, SH_F: R_SHF, SC_F: R_SCF, GT_F: R_GTF}[c[1]] + 2 * c[2]
                V.tensor_tensor(dst[:, 2 * c[2]:2 * c[2] + 2, :], bank[:, 0:4].rearrange("p (k v) -> p k v", v=2),
                                vT[:, row:row + 2].unsqueeze(2).to_broadcast([P, 2, 2]), ALU.add).then_inc(B.read(("mod", c)), 1)
                B.wait_read(dve, ("mod", c))

            def finish_gains(norm, row):
                view = amul[norm].rearrange("p (k v) -> p k v", v=2)
                step(V.scalar_tensor_tensor(out=view, in0=view, scalar=1.0,
                                            in1=vT[:, row:row + 8].unsqueeze(2).to_broadcast([P, 8, 2]),
                                            op0=ALU.add, op1=ALU.mult))
                V.tensor_reduce(hmx[norm][:, 1:2], amul[norm], AX_X, ALU.max, apply_absolute_value=True).then_inc(s_hmx, 1)
                V.tensor_reduce(hmx[norm][:, 2:3], shf[norm], AX_X, ALU.max, apply_absolute_value=True).then_inc(s_hmx, 1)

            def scale_gains(norm):
                dve.wait_ge(s_hsc, norm + 1)
                own.did(V.tensor_scalar(amul[norm], amul[norm], hscl[norm], None, ALU.mult))
                step(V.tensor_scalar(shf[norm], shf[norm], hscl[norm], None, ALU.mult))

            def put_x(j):
                for h in range(2):
                    key = ("xT", j, h)
                    bank = B.take(dve, key)
                    V.tensor_copy(xT[:, 4 * h:4 * h + 4, P * j:P * j + P],
                                  bank[:].rearrange("p (k t) -> p k t", k=4)).then_inc(B.read(key), 1)

            add_pos(1)
            for what, n in start:
                if what == "x":
                    if n + 2 < NT:
                        add_pos(n + 2)
                    put_x(n)
                elif what == "out":
                    mod_cols(ada1[n])
                    if n == 4:
                        chunk_max(dve, 0)
            finish_gains(0, R_GPM)
            chunk_low(dve, 0)
            scale_gains(0)
            V.tensor_copy(hgo, hscl[0]).then_inc(s_gn, 1)

            def modulate(key, norm, j, h, buf):
                bank = B.take(dve, key)
                v = 1 if j == 0 else 0
                for k in range(4):
                    c = 2 * (4 * h + k) + v
                    ins = V.tensor_scalar(buf[:, P * k:P * k + P], bank[:, P * k:P * k + P], amul[norm][:, c:c + 1],
                                          shf[norm][:, c:c + 1], ALU.mult, ALU.add)
                    if k < 3:
                        own.did(ins)
                ins.then_inc(B.read(key), 1)

            def low_h(high_done, low_done, hi, lo, j, h, buf):
                dve.wait_ge(high_done, 2 * j + h + 1)
                tile_ = (slice(None), slice(4 * h, 4 * h + 4), slice(P * j, P * j + P))
                V.tensor_tensor(lo[tile_], buf.rearrange("p (k t) -> p k t", k=4), hi[tile_], ALU.subtract).then_inc(low_done, 1)

            def gain_x(b, h):
                for k in (4 * h, 4 * h + 1):
                    for v, toks in block_parts(b):
                        c = 2 * k + v
                        ins = V.tensor_scalar(xT[:, k, toks], xT[:, k, toks], amul[0][:, c:c + 1], shf[0][:, c:c + 1],
                                              ALU.mult, ALU.add)
                        if k % 4 == 0 or v == 1:
                            own.did(ins)
                ins.then_inc(s_mv, 1)

            def low_x(b, h):
                dve.wait_ge(s_th, 2 * b + h + 1)
                t_ = (slice(None), slice(4 * h, 4 * h + 4), slice(TBW * b, TBW * b + TBW))
                V.tensor_tensor(HTl[t_], xT[t_], HTh[t_], ALU.subtract).then_inc(s_tl, 1)

            halves = [(b, h) for b in range(TB) for h in range(2)]
            for h in range(2):
                B.wait_read(dve, ("xT", NT - 1, h))
            B.wait_read(dve, ("xT", NT - 2, 1))
            gain_x(0, 0)
            gain_x(0, 1)
            for r, (b, h) in enumerate(halves):
                low_x(b, h)
                if r + 2 < len(halves):
                    gain_x(*halves[r + 2])
                if r == 1:
                    chunk_max(dve, 1)

            def decay_bias(k):
                for d in range(2):
                    for t in range(TB):
                        key = ("la", d, k, t)
                        bank = B.take(dve, key)
                        r = R_BA + HK * d + k
                        V.tensor_scalar(tmp[2 * d][:, TBW * t:TBW * t + TBW], bank[:, 0:TBW], vT[:, r:r + 1], None,
                                        ALU.add).then_inc(B.read(key), 1)

            def decay_sums(k):
                for d in range(2):
                    x, c = tmp[2 * d], tmp[2 * d + 1]
                    dve.wait_ge(s_dln, 2 * k + d + 1)
                    step(V.scalar_tensor_tensor(out=x, in0=x, scalar=0.0, in1=c, op0=ALU.min, op1=ALU.subtract))
                    for j in range(NT):
                        part_ = slice(P * j, P * j + P) if d == 0 else slice(P * j + P - 1, P * j - 1 if j else None, -1)
                        own.did(V.tensor_tensor_scan(c[:, part_], ones, x[:, part_], 0.0, ALU.mult, ALU.add))
                    own.settle()
                    last, mid = (P - 1, P // 2 - 1) if d == 0 else (0, P // 2)
                    w = wexp[2 * d + k]
                    cv = c.rearrange("p (j t) -> p j t", t=P)
                    own.did(V.tensor_copy(w[:, 0:NT], cv[:, :, last]))
                    own.did(V.tensor_copy(w[:, 2 * NT:3 * NT], cv[:, :, mid]))
                    own.settle()
                    own.did(V.tensor_tensor(w[:, NT:2 * NT], w[:, 0:NT], w[:, 2 * NT:3 * NT], ALU.subtract))
                    step(V.tensor_tensor(x.rearrange("p (j t) -> p j t", t=P), cv,
                                         w[:, 2 * NT:3 * NT].unsqueeze(2).to_broadcast([P, NT, P]), ALU.subtract))
                    V.tensor_scalar(x, x, CLAMP, -CLAMP, ALU.min, ALU.max).then_inc(s_de, 1)

            def decay_q_k(k):
                for i in (Q, K):
                    for key in z_uses(i):
                        A.wait_read(dve, key)
                if k == 0:
                    dve.wait_ge(s_xst, 16 * NT)
                for d in range(2):
                    dve.wait_ge(s_dexp, 4 * k + 2 * d + 1)
                    V.tensor_tensor(qt[d][k], qT[:, k, :], tmp[2 * d + 1], ALU.mult).then_inc(s_qk, 1)
                    dve.wait_ge(s_dexp, 4 * k + 2 * d + 2)
                    V.tensor_tensor(kt_[d][k], kT[:, k, :], tmp[2 * d], ALU.mult).then_inc(s_qk, 1)
                dve.wait_ge(s_qk, 4 * k + 4)

            def fold():
                for i in (U_A, U_B):
                    for key in z_uses(i):
                        A.wait_read(dve, key)
                up_ = uT[:, :, CTX + 1:CTX + FOLD]
                down_ = uT[:, :, CTX + LAT - 1:CTX + FOLD:-1]
                own.did(V.tensor_tensor(Ef[:, :, 1:FOLD], up_, down_, ALU.add))
                own.did(V.tensor_tensor(Of[:, :, 1:FOLD], up_, down_, ALU.subtract))
                own.did(V.tensor_copy(Ef[:, :, 0:1], uT[:, :, CTX:CTX + 1]))
                V.memset(Of[:, :, 0:1], 0.0).then_inc(s_fold, 1)


            def silu_gate(r):
                dve.wait_ge(s_gsg, r + 1)
                j, cs = r % NT, slice(CW * (r // NT), CW * (r // NT) + CW)
                e = gex[:, r % 2, :]
                step(V.reciprocal(e, e))
                V.tensor_tensor(gN[:, j, cs], gN[:, j, cs], e, ALU.mult).then_inc(s_gs, 1)

            def blocks(out, S, w, done):
                own.did(V.tensor_scalar(out[0:DK, 0:DV], S[0:DK, :], w[0:DK, :], None, ALU.mult))
                V.tensor_scalar(out[DK:P, DV:2 * DV], S[DK:P, :], w[DK:P, :], None, ALU.mult).then_inc(done, 1)

            def absorb(d, n, j):
                key = ("U", d, j)
                if j > 0:
                    own.settle()
                    dve.wait_ge((s_srf, s_srb)[d], HK * n)
                    for k in range(HK):
                        own.did(V.tensor_scalar(Sst[:, d, k, :], Sst[:, d, k, :], wexp[2 * d + k][:, j:j + 1], None, ALU.mult))
                    own.settle()
                bank = A.take(dve, key)
                for k in range(HK):
                    for h in range(2):
                        rows, cols_ = slice(DK * h, DK * h + DK), slice(2 * DV * k + DV * h, 2 * DV * k + DV * h + DV)
                        w = wexp[2 * d + k][rows, NT + j:NT + j + 1]
                        if j == 0:
                            ins = V.tensor_scalar(Sctx[d][rows, k, :], bank[rows, cols_], w, None, ALU.mult)
                        else:
                            S = Sst[rows, d, k, :]
                            ins = V.scalar_tensor_tensor(out=S, in0=bank[rows, cols_], scalar=w, in1=S,
                                                         op0=ALU.mult, op1=ALU.add)
                        if (k, h) != (HK - 1, 1):
                            own.did(ins)
                ins.then_inc(A.read(key), 1)
                if j > 0:
                    A.wait_read(dve, key)
                    own.settle()

            def ada_sums(n):
                for what, m in ada_step(n):
                    if what == "out":
                        mod_cols(ada2[m])

            for i in range(G_A):
                chunk_max(dve, i + 2)
                chunk_low(dve, i + 1)
                if i == Q:
                    decay_bias(0)
                elif i == K:
                    decay_sums(0)
                elif i == U_A:
                    decay_q_k(0)
                    decay_bias(1)
                elif i == U_B:
                    decay_sums(1)
                elif i == V_A:
                    decay_q_k(1)
                elif i == V_B:
                    fold()
            step(V.memset(Srf, 0.0))
            dve.wait_ge(s_misc, 48)
            for what, n in gate_events:
                if what == "z":
                    if n == 0:
                        chunk_low(dve, G_B)
                    else:
                        silu_gate(n - 1)
                elif what == "U":
                    if n == 0:
                        dve.wait_ge(s_state, 32)
                        for k in range(HK):
                            blocks(Srf[:, 0, k, :], Sst[:, 0, k, :], wexp[k][:, 2 * NT + 1:2 * NT + 2], s_srf)
                    j = f_order[n]
                    if n >= 1:
                        ada_sums(n - 1)
                    absorb(0, n, j)
                    if j > 0:
                        for k in range(HK):
                            blocks(Srf[:, j, k, :], Sst[:, 0, k, :], wexp[k][:, 2 * NT + j + 1:2 * NT + j + 2], s_srf)
            silu_gate(2 * NT - 1)

            def groups(y):
                return y.rearrange("p (g c) -> p g c", g=GROUPS)

            ada_sums(N_FWD - 1)
            for i in range(-1, 4):
                key = ("P", i)
                bank = A.take(dve, key)
                A.wait_read(dve, ("Q", i))
                if i >= 0:
                    B.take(dve, ("Y1", i - 1))
                if i >= 1:
                    B.take(dve, ("Y2", i - 1))
                p, q = groups(bank[:, 0:GROUPS * NCOS]), groups(Qs[:, 0:GROUPS * NSIN])
                outs = [(groups(Y1b), ALU.subtract, ALU.add)] + ([(groups(Y2b), ALU.add, ALU.subtract)] if i >= 0 else [])
                for n, (y, low, high) in enumerate(outs):
                    own.did(V.tensor_tensor(y[:, :, 1:64], p[:, :, 1:64], q, low))
                    own.did(V.tensor_tensor(y[:, :, P - 1:64:-1], p[:, :, 1:64], q, high))
                    ins = V.tensor_copy(y[:, :, 0:NCOS:64], p[:, :, 0:NCOS:64])
                    if n < len(outs) - 1:
                        own.did(ins)
                ins.then_inc(A.read(key), 1)
                ada_sums(N_FWD + 1 + i)
            key = ("P", 4)
            bank = A.take(dve, key)
            B.take(dve, ("Y1", 3))
            p, y = groups(bank[0:1, 0:GROUPS * NCOS]), groups(Y1b[0:1, :])
            own.did(V.tensor_copy(y[:, :, 0:NCOS], p))
            V.tensor_copy(y[:, :, P - 1:64:-1], p[:, :, 1:64]).then_inc(A.read(key), 1)

            B.wait_read(dve, ("Y1", 4))

            def scores(s, j):
                for hp in range(HK):
                    key = ("At", j, hp)
                    bank = A.take(dve, key)
                    if s >= 1:
                        dve.wait_ge(s_at, HK * (s - 1) + hp + 1)
                    V.tensor_tensor(Am[:, hp:HEADS:2, :], bank[:].rearrange("p (h t) -> p h t", h=2),
                                    masks.unsqueeze(1).to_broadcast([P, 2, 2 * P]), ALU.mult).then_inc(A.read(key), 1)
                if j == 1:
                    return
                nxt = b_order[s + 1]
                absorb(1, s, j)
                if s == 0:
                    dve.wait_ge(s_srz, 1)
                if s >= 2:
                    B.take(dve, ("o", b_order[s - 2]))
                for k in range(HK):
                    blocks(Srb[:, (s + 1) % 3, k, :], Sst[:, 1, k, :], wexp[2 + k][:, 2 * NT + nxt:2 * NT + nxt + 1], s_srb)

            def gate_o(s, j):
                key = ("o", j)
                bank = B.take(dve, key)
                dve.wait_ge(s_ors, s + 1)
                if s == 0:
                    dve.wait_ge(s_gh, 2 * NT)
                if s >= 2:
                    B.take(dve, ("oT", b_order[s - 2]))
                for h in range(HEADS):
                    hv = slice(DV * h, DV * h + DV)
                    ins = V.scalar_tensor_tensor(out=yo[:, s % 2, hv], in0=bank[:, hv], scalar=ors[:, 4 * j + h:4 * j + h + 1],
                                                 in1=gN[:, j, hv], op0=ALU.mult, op1=ALU.mult)
                    if h < HEADS - 1:
                        own.did(ins)
                ins.then_inc(B.read(key), 1)

            def y_max_tile(j):
                B.wait_read(dve, ("oT", j))
                own.did(V.tensor_reduce(ymt[:, j:j + 1], yT[:, 0:4, P * j:P * j + P], AX_XY, ALU.max, apply_absolute_value=True))

            def finish_gates(g, row):
                view = gtc[g].rearrange("p (k v) -> p k v", v=2)
                own.did(V.tensor_tensor(view, view, vT[:, row:row + 8].unsqueeze(2).to_broadcast([P, 8, 2]), ALU.mult))

            w0 = len(zin)
            scores(0, b_order[0])
            for s, j in enumerate(b_order):
                if s + 1 < NT:
                    scores(s + 1, b_order[s + 1])
                gate_o(s, j)
                if s >= 2:
                    y_max_tile(b_order[s - 2])
                if s < 4:
                    own.did(V.tensor_reduce(ymf[:, s:s + 1], yT[:, 4 + s, :], AX_X, ALU.max, apply_absolute_value=True))
                if s == 4:
                    own.settle()
                    V.tensor_reduce(ymx[:, 1:2], ymf, AX_X, ALU.max).then_inc(s_ymx, 1)
                if N_FWD + N_FOU + s <= len(ada2):
                    ada_sums(N_FWD + N_FOU + s)
                if s == 3:
                    finish_gates(0, R_PM)
                    finish_gates(1, R_PF)
                    finish_gains(1, R_GPF)
                    chunk_max(dve, w0)
                    chunk_max(dve, w0 + 1)
                if s == 5:
                    scale_gains(1)
                    chunk_low(dve, w0)
                if s == 6:
                    chunk_max(dve, w0 + 2)
                if s == 7:
                    chunk_low(dve, w0 + 1)
            y_max_tile(b_order[-2])
            y_max_tile(b_order[-1])
            own.settle()
            V.tensor_reduce(ymx[:, 0:1], ymt, AX_X, ALU.max).then_inc(s_ymx, 1)

            def low_y(j, halves=(1, 0)):
                for half in halves:
                    dve.wait_ge(s_yh, 2 * j + 2 - half)
                    t_ = (slice(None), slice(4 * half, 4 * half + 4), slice(P * j, P * j + P))
                    V.scalar_tensor_tensor(out=YTl[t_], in0=yT[t_], scalar=yscl[:, half:half + 1], in1=YTh[t_],
                                           op0=ALU.mult, op1=ALU.subtract).then_inc(s_yl, 1)

            def diagonals(q):
                g, v, h = q // 4, q // 2 % 2, q % 2
                if q >= 4:
                    B.take(dve, ("gate", q - 4))
                for k in range(4):
                    c = 2 * (4 * h + k) + v
                    ins = V.tensor_scalar(diag[q % 4][:, P * k:P * k + P], ident, gtc[g][:, c:c + 1], None, ALU.mult)
                    if k < 3:
                        own.did(ins)
                ins.then_inc(s_dg, 1)

            def put_odd(c, j):
                key = ("wo", c, j)
                bank = A.take(dve, key)
                A.wait_read(dve, ("wo", c - 1, j))
                i = w0 + c
                y = yN[:, j % 4, 256 * (c - 1):256 * (c - 1) + 512]
                V.scalar_tensor_tensor(out=y, in0=bank[:], scalar=wcof[:, i % 8:i % 8 + 1], in1=y, op0=ALU.mult,
                                       op1=ALU.add).then_inc(A.read(key), 1)

            def post(j):
                if j < 2:
                    for q in range(4):
                        B.wait_read(dve, ("gate", q))
                dve.wait_ge(s_prs, j + 1)
                v = 1 if j == 0 else 0
                y = yN[:, j % 4, :]
                step(V.scalar_tensor_tensor(out=y, in0=y, scalar=prs[:, j:j + 1], in1=gates[:, 0, v, :],
                                            op0=ALU.mult, op1=ALU.mult))
                dve.wait_ge(s_x1[j], 16)
                V.tensor_tensor(x1[:, j, :], x1[:, j, :], y, ALU.add).then_inc(s_xr, 1)

            def modulate(key, norm, j, h, buf):
                bank = B.take(dve, key)
                v = 1 if j == 0 else 0
                for k in range(4):
                    c = 2 * (4 * h + k) + v
                    ins = V.tensor_scalar(buf[:, P * k:P * k + P], bank[:, P * k:P * k + P], amul[norm][:, c:c + 1],
                                          shf[norm][:, c:c + 1], ALU.mult, ALU.add)
                    if k < 3:
                        own.did(ins)
                ins.then_inc(B.read(key), 1)

            def modulate_2(j):
                for h in range(2):
                    if j >= 1:
                        dve.wait_ge(s_2l, 2 * (j - 1) + h + 1)
                    modulate(("x2", j, h), 1, j, h, tb2[h])
                for h in range(2):
                    B.wait_read(dve, ("x2", j, h))
                    dve.wait_ge(s_2h, 2 * j + h + 1)
                    tile_ = (slice(None), slice(4 * h, 4 * h + 4), slice(P * j, P * j + P))
                    V.tensor_tensor(HT2l[tile_], tb2[h].rearrange("p (k t) -> p k t", k=4), HT2h[tile_],
                                    ALU.subtract).then_inc(s_2l, 1)

            own.settle()
            low_y(0, (1,))
            chunk_max(dve, w0 + 3)
            low_y(0, (0,))
            chunk_low(dve, w0 + 2)
            for q in range(4):
                diagonals(q)
            chunk_low(dve, w0 + 3)
            low_y(1)
            F = ff_split
            for j in range(NT + 2):
                if j < NT:
                    put_odd(1, j)
                if j + 2 < NT:
                    low_y(j + 2)
                if 1 <= j <= NT:
                    post(j - 1)
                if j >= 2:
                    modulate_2(j - 2)
                if j < NT:
                    put_odd(3, j)
                if j in (4, 5):
                    chunk_max(dve, F + j - 4)
                if j == 6:
                    chunk_low(dve, F)
                if j == NT:
                    chunk_low(dve, F + 1)
                if j == 0:
                    for q in range(4, 8):
                        diagonals(q)

            def up(g, x, t=0):
                for u in range(6):
                    r = 6 * x + u
                    n = 12 * g + r
                    key = A0 + UA * g + r
                    tb_, m = u // 2, 2 * x + u % 2
                    A.wait_read(dve, key, 6 * t)
                    if n >= 2:
                        dve.wait_ge(s_fl, n - 1 + 24 * t)
                    V.tensor_tensor(fsq[:, n % 2, :], frel[:, n % 2, :], frel[:, n % 2, :], ALU.mult).then_inc(s_fq, 1)
                    dve.wait_ge(s_fq, n + 1 + 24 * t)
                    dve.wait_ge(s_fh, n + 1 + 24 * t)
                    toks = slice(TBW * tb_, TBW * tb_ + TBW)
                    V.tensor_tensor(FTl[g % 2][:, m, toks], fsq[:, n % 2, :], FTh[g % 2][:, m, toks],
                                    ALU.subtract).then_inc(s_fl, 1)

            def down(i, g, n, t=0, then=None):
                cof = wcof[:, i % 8:i % 8 + 1]
                for j in range(NT):
                    key = B0 + UB * g + NT * n + j
                    bank = B.take(dve, key, 12 * t)
                    B.wait_read(dve, key - UB, 12 * t)
                    y = acc[:, j, 512 * n:512 * n + 512]
                    V.scalar_tensor_tensor(out=y, in0=bank[:], scalar=cof, in1=y, op0=ALU.mult,
                                           op1=ALU.add).then_inc(B.read(key), 1)
                    if then is not None:
                        then(j)

            chunk_max(dve, F + 2)
            up(0, 0)
            chunk_max(dve, F + 3)
            chunk_low(dve, F + 2)
            up(0, 1)
            dve.wait_ge(s_accz, 1)

            def group(g, t):
                for s in range(4):
                    chunk_max(dve, F + 4 * g + 4 + s, t)
                    chunk_low(dve, F + 4 * g + 3 + s, t)
                    if s < 2:
                        up(g + 1, s, t)
                    else:
                        down(F + 4 * g + 4 + s - 2, g, s - 2, t)

            with dve.Fori(0, NG // 2 - 1) as t:
                group(0, t)
                group(1, t)
            group(NG - 2, 0)

            def finish(j):
                dve.wait_ge(s_frs, j + 1)
                v = 1 if j == 0 else 0
                step(V.scalar_tensor_tensor(out=acc[:, j, :], in0=acc[:, j, :], scalar=frs[:, j:j + 1], in1=gates[:, 1, v, :],
                                            op0=ALU.mult, op1=ALU.mult))
                V.tensor_tensor(x1[:, j, :], x1[:, j, :], acc[:, j, :], ALU.add).then_inc(s_y, 1)

            chunk_low(dve, F + 4 * NG - 1)
            down(F + 4 * NG - 2, NG - 1, 0)
            down(F + 4 * NG - 1, NG - 1, 1, 0, lambda j: finish(j - 1) if j >= 1 else None)
            finish(NT - 1)


def _constants():
    import numpy as np
    i = np.arange(P)
    k = np.zeros((P, C_ALL), np.float64)
    k[:, C_ID:C_ID + P] = np.eye(P)
    k[:, C_MASK:C_MASK + P] = i[:, None] <= i[None, :]
    k[:, C_MASK + P:C_MASK + 2 * P] = i[:, None] >= i[None, :]
    for v in range(2):
        k[v::32, C_SEL2 + v] = 1.0
    turn = 2.0 * np.pi * (np.outer(i, i) % P) / P
    k[:, C_CH:C_CH + NCOS] = np.cos(turn)[:, 0:NCOS]
    k[:, C_CH + NCOS:C_CH + P] = np.sin(turn)[:, 1:64]
    k[:, C_CTX:C_CTX + P] = np.cos(turn) / P
    k[:, C_CTX + P:C_CTX + 2 * P] = np.sin(turn) / P
    unit = 1.0 / np.sqrt(LAT * P)
    k[:, C_ALT] = unit * (1.0 - 2.0 * (i % 2))
    m = np.arange(FOLD)
    turn = 2.0 * np.pi * (np.outer(m, m) % LAT) / LAT
    f = np.float32
    nf = D // 4
    omega = (f(1.0) / (f(10000.0) ** (np.arange(nf, dtype=f) / f(nf)))).astype(f)
    row, col = np.arange(LAT // 64, dtype=f)[:, None] * omega, (i % 64).astype(f)[:, None] * omega
    return {
        "k_consts": k.astype(f),
        "k_dft_cos": (unit * np.cos(turn)).astype(f),
        "k_dft_sin": (unit * np.sin(turn)).astype(f),
        "k_alt": (unit * (1.0 - 2.0 * (i % 2)))[None, :].astype(f),
        "k_pos_row": np.concatenate([np.sin(row), np.cos(row)], axis=1).astype(f),
        "k_pos_col": np.concatenate([np.sin(col), np.cos(col)], axis=1).astype(f),
    }


_INS = ["x_prompt", "x_sample", "state_gla_fwd", "state_gla_bwd", "c", "c_ctx", "w_in", "w_out", "w_a2", "b_a2",
        "g_head", "w_ada", "b_ada", "g_pre_mix", "g_post_mix", "g_pre_mlp", "g_post_mlp", "w_fc1", "w_fc2"]
_OUTS = [(1, CTX, D), (1, LAT, D), (1, 1, HEADS, DK, DV), (1, 1, HEADS, DK, DV)]


def kernel(**inputs):
    import numpy as _np
    import concourse.bacc as _bacc
    from concourse.bass_utils import run_bass_kernel_spmd as _run

    nc = _bacc.Bacc("TRN2", target_bir_lowering=False, num_devices=1)
    arrays, args = {}, {}
    for name, x in [(n, _np.ascontiguousarray(inputs[n])) for n in _INS] + list(_constants().items()):
        arrays[f"in_{name}"] = x
        args[name] = nc.dram_tensor(f"in_{name}", x.shape, F32, kind="ExternalInput").ap()
    for i, shape in enumerate(_OUTS):
        args[f"out_{i}"] = nc.dram_tensor(f"out_{i}_dram", shape, F32, kind="ExternalOutput").ap()
    hybrid_step(nc, args)
    r = _run(nc, [arrays], core_ids=[0])
    return tuple(r.results[0][f"out_{i}_dram"] for i in range(len(_OUTS)))
```
